# Optimizing a Trainium2 kernel written in Bass

```python
import jax, jax.numpy as jnp
from jax import lax
import numpy as np
import math
import jax
import jax.numpy as jnp

D_MODEL = 1024
BATCH = 1
SEQ = 512
DEPTH = 2

CHUNK = 64
N_MEM = 256
ROPE_THETA = 10000.0
LN_EPS = 1e-5

POOL_GROUPS = 4
POOL_GROUP_DIM = 128
POOL_WINDOWS = (2, 4, 8, 16)
POOL_WIDTH = POOL_GROUPS * POOL_GROUP_DIM
ATT_HEADS = 8
ATT_HEAD_DIM = 64
ATT_WIDTH = ATT_HEADS * ATT_HEAD_DIM
IDX_HEADS = 8
IDX_HEAD_DIM = 64
TOPK_MAX = 256
Q_BLOCK = 128
MEM_HEADS = 4
MEM_HEAD_DIM = 128
MEM_WIDTH = MEM_HEADS * MEM_HEAD_DIM
N_BRANCH = 3
BRANCH_WIDTH = 512
IN_WIDTHS = (POOL_WIDTH, ATT_WIDTH, ATT_WIDTH, ATT_WIDTH, IDX_HEADS * IDX_HEAD_DIM,
             IDX_HEAD_DIM, IDX_HEADS, MEM_WIDTH, N_BRANCH * D_MODEL)
D_IN = sum(IN_WIDTHS)
N_EXPERTS = 16
N_GROUPS = 4
EXPERTS_PER_GROUP = N_EXPERTS // N_GROUPS
TOP_K_EXPERTS = 2
GROUP_SCORE_TOPK = 2
D_EXPERT = 512
MOE_BLOCK = 128
DN_ALPHA = (2 * DEPTH) ** 0.25
DN_BETA = (8 * DEPTH) ** -0.25


def layer_norm(x, g, b):
    xf = x.astype(jnp.float32)
    mu = jnp.mean(xf, axis=-1, keepdims=True)
    var = jnp.mean(jnp.square(xf - mu), axis=-1, keepdims=True)
    y = (xf - mu) * lax.rsqrt(var + LN_EPS) * g.astype(jnp.float32) + b.astype(jnp.float32)
    return y.astype(x.dtype)

def rotary(x, positions):
    half = x.shape[-1] // 2
    inv_freq = ROPE_THETA ** (-jnp.arange(half, dtype=jnp.float32) / half)
    ang = positions.astype(jnp.float32)[..., None] * inv_freq
    cos = jnp.cos(ang)[:, :, None, :]
    sin = jnp.sin(ang)[:, :, None, :]
    xf = x.astype(jnp.float32)
    x1, x2 = xf[..., :half], xf[..., half:]
    out = jnp.concatenate([x1 * cos - x2 * sin, x2 * cos + x1 * sin], axis=-1)
    return out.astype(x.dtype)

def pool_branch(u, pool_w, pool_scale):
    B, S, _ = u.shape
    u = u.reshape(B, S, POOL_GROUPS, POOL_GROUP_DIM)
    t = jnp.arange(S)
    outs = []
    for g, w in enumerate(POOL_WINDOWS):
        ug = u[:, :, g].astype(jnp.float32)
        cs = jnp.cumsum(ug, axis=1)
        lagged = jnp.pad(cs, ((0, 0), (w, 0), (0, 0)))[:, :S]
        cnt = jnp.minimum(t + 1, w).astype(jnp.float32)[None, :, None]
        outs.append((cs - lagged) / cnt - ug)
    d = jnp.stack(outs, axis=2).astype(u.dtype)
    mixed = jnp.einsum('bsgc,gce->bsge', d, pool_w).reshape(B, S, POOL_WIDTH)
    return mixed * pool_scale

def dsa_branch(q, k, v, iq, ik, iw, positions):
    B, S, _ = q.shape
    q = rotary(q.reshape(B, S, ATT_HEADS, ATT_HEAD_DIM), positions)
    k = rotary(k.reshape(B, S, ATT_HEADS, ATT_HEAD_DIM), positions)
    v = v.reshape(B, S, ATT_HEADS, ATT_HEAD_DIM)
    iq = rotary(iq.reshape(B, S, IDX_HEADS, IDX_HEAD_DIM), positions)
    ik = rotary(ik[:, :, None, :], positions)[:, :, 0]
    iw = iw * (IDX_HEADS ** -0.5)
    n_sel = min(TOPK_MAX, S // 4)
    nb = S // Q_BLOCK
    key_chunk = jnp.arange(S) // CHUNK

    def to_blocks(a):
        return a.reshape(B, nb, Q_BLOCK, *a.shape[2:]).swapaxes(0, 1)

    def attend_block(args):
        blk, qb, iqb, iwb = args
        t = blk * Q_BLOCK + jnp.arange(Q_BLOCK)
        q_chunk = t // CHUNK
        admissible = key_chunk[None, :] <= q_chunk[:, None]
        rel = jax.nn.relu(jnp.einsum('bqhd,bsd->bqhs', iqb, ik) * (IDX_HEAD_DIM ** -0.5))
        score = jnp.einsum('bqhs,bqh->bqs', rel, iwb).astype(jnp.float32)
        score = jnp.where(admissible[None], score, -jnp.inf)
        _, sel = lax.top_k(score, n_sel)
        valid = (sel // CHUNK) <= q_chunk[None, :, None]
        kg = jax.vmap(lambda kk, ii: kk[ii])(k, sel)
        vg = jax.vmap(lambda vv, ii: vv[ii])(v, sel)
        s = jnp.einsum('bqhd,bqkhd->bqhk', qb, kg).astype(jnp.float32) * (ATT_HEAD_DIM ** -0.5)
        s = jnp.where(valid[:, :, None, :], s, -jnp.inf)
        p = jax.nn.softmax(s, axis=-1).astype(vg.dtype)
        return jnp.einsum('bqhk,bqkhd->bqhd', p, vg)

    out = lax.map(attend_block, (jnp.arange(nb), to_blocks(q), to_blocks(iq), to_blocks(iw)))
    return out.swapaxes(0, 1).reshape(B, S, ATT_WIDTH)

def memory_branch(mq, mem, w_mem_kv):
    B, S, _ = mq.shape
    M = mem.shape[1]
    kv = jnp.einsum('bmd,de->bme', mem, w_mem_kv)
    mk, mv = jnp.split(kv, 2, axis=-1)
    mk = mk.reshape(B, M, MEM_HEADS, MEM_HEAD_DIM)
    mv = mv.reshape(B, M, MEM_HEADS, MEM_HEAD_DIM)
    q = mq.reshape(B, S, MEM_HEADS, MEM_HEAD_DIM)
    s = jnp.einsum('bshd,bmhd->bhsm', q, mk).astype(jnp.float32) * (MEM_HEAD_DIM ** -0.5)
    p = jax.nn.softmax(s, axis=-1).astype(mv.dtype)
    return jnp.einsum('bhsm,bmhd->bshd', p, mv).reshape(B, S, MEM_WIDTH)

def token_mixing(x, mem, positions, w_in, b_in, pool_w, pool_scale, w_mem_kv, w_br, w_out):
    B, S, D = x.shape
    proj = jnp.einsum('bsd,de->bse', x, w_in) + b_in
    split_points = np.cumsum(IN_WIDTHS)[:-1].tolist()
    u_pool, q, k, v, iq, ik, iw, mq, gate_logits = jnp.split(proj, split_points, axis=-1)
    gates = jax.nn.sigmoid(gate_logits.astype(jnp.float32)).astype(x.dtype).reshape(B, S, N_BRANCH, D)
    branches = (pool_branch(u_pool, pool_w, pool_scale),
                dsa_branch(q, k, v, iq, ik, iw, positions),
                memory_branch(mq, mem, w_mem_kv))
    merged = jnp.zeros_like(x)
    for n in range(N_BRANCH):
        merged = merged + gates[:, :, n] * jnp.einsum('bsc,cd->bsd', branches[n], w_br[n])
    return jnp.einsum('bsd,de->bse', merged, w_out)

def route(x2, w_router, router_bias):
    scores = jax.nn.sigmoid(jnp.einsum('nd,de->ne', x2, w_router).astype(jnp.float32))
    biased = scores + router_bias.astype(jnp.float32)
    grouped = biased.reshape(-1, N_GROUPS, EXPERTS_PER_GROUP)
    group_score = lax.top_k(grouped, GROUP_SCORE_TOPK)[0].sum(-1)
    best = jnp.argmax(group_score, axis=-1).astype(jnp.int32)
    within = jnp.take_along_axis(grouped, best[:, None, None], axis=1)[:, 0]
    _, local = lax.top_k(within, TOP_K_EXPERTS)
    expert_idx = (best[:, None] * EXPERTS_PER_GROUP + local).astype(jnp.int32)
    w = jnp.take_along_axis(scores, expert_idx, axis=1)
    w = w / jnp.sum(w, axis=-1, keepdims=True)
    return expert_idx, w

def moe(x2, w_router, router_bias, w1, w3, w2):
    N, D = x2.shape
    expert_idx, gate_w = route(x2, w_router, router_bias)
    n_assign = N * TOP_K_EXPERTS
    n_blk = -(-n_assign // MOE_BLOCK) + N_EXPERTS
    flat_e = expert_idx.reshape(-1)
    flat_tok = jnp.repeat(jnp.arange(N, dtype=jnp.int32), TOP_K_EXPERTS)
    flat_g = gate_w.reshape(-1).astype(x2.dtype)
    order = jnp.argsort(flat_e)
    e_sorted = flat_e[order]
    counts = jax.ops.segment_sum(jnp.ones_like(flat_e), flat_e, num_segments=N_EXPERTS)
    padded = ((counts + MOE_BLOCK - 1) // MOE_BLOCK) * MOE_BLOCK
    pad_end = jnp.cumsum(padded)
    pad_start = pad_end - padded
    start = jnp.cumsum(counts) - counts
    rank = jnp.arange(n_assign, dtype=jnp.int32) - start[e_sorted]
    dest = pad_start[e_sorted] + rank
    slot_tok = jnp.full((n_blk * MOE_BLOCK,), N, jnp.int32).at[dest].set(flat_tok[order])
    slot_gate = jnp.zeros((n_blk * MOE_BLOCK,), x2.dtype).at[dest].set(flat_g[order])
    blk_e = jnp.minimum(jnp.searchsorted(pad_end, jnp.arange(n_blk) * MOE_BLOCK, side='right'),
                        N_EXPERTS - 1).astype(jnp.int32)
    x_pad = jnp.concatenate([x2, jnp.zeros((1, D), x2.dtype)], axis=0)

    def run_block(args):
        e, toks = args
        xb = x_pad[toks]
        h = jax.nn.silu(xb @ w1[e]) * (xb @ w3[e])
        return h @ w2[e]

    yb = lax.map(run_block, (blk_e, slot_tok.reshape(n_blk, MOE_BLOCK)))
    y = yb.reshape(-1, D) * slot_gate[:, None]
    return jnp.zeros((N + 1, D), x2.dtype).at[slot_tok].add(y)[:N]

def first_inputs(seed: int = 0) -> dict:
    key = jax.random.key(seed)
    ks = jax.random.split(key, 20)
    f32 = jnp.float32
    nrm = lambda k, shape, scale: jax.random.normal(k, shape, f32) * scale
    return {
        'x': nrm(ks[0], (BATCH, SEQ, D_MODEL), 1.0),
        'mem': nrm(ks[1], (BATCH, N_MEM, D_MODEL), 1.0),
        'positions': jnp.broadcast_to(jnp.arange(SEQ, dtype=jnp.int32)[None], (BATCH, SEQ)),
        'w_in': nrm(ks[2], (DEPTH, D_MODEL, D_IN), D_MODEL ** -0.5),
        'b_in': nrm(ks[3], (DEPTH, D_IN), 0.02),
        'pool_w': nrm(ks[4], (DEPTH, POOL_GROUPS, POOL_GROUP_DIM, POOL_GROUP_DIM), POOL_GROUP_DIM ** -0.5),
        'pool_scale': 1.0 + nrm(ks[5], (DEPTH, POOL_WIDTH), 0.02),
        'w_mem_kv': nrm(ks[6], (DEPTH, D_MODEL, 2 * MEM_WIDTH), D_MODEL ** -0.5),
        'w_br': nrm(ks[7], (DEPTH, N_BRANCH, BRANCH_WIDTH, D_MODEL), DN_BETA * BRANCH_WIDTH ** -0.5),
        'w_out': nrm(ks[8], (DEPTH, D_MODEL, D_MODEL), DN_BETA * D_MODEL ** -0.5),
        'ln1_g': 1.0 + nrm(ks[9], (DEPTH, D_MODEL), 0.02),
        'ln1_b': nrm(ks[10], (DEPTH, D_MODEL), 0.02),
        'w_router': nrm(ks[11], (D_MODEL, N_EXPERTS), D_MODEL ** -0.5),
        'router_bias': nrm(ks[12], (N_EXPERTS,), 0.01),
        'w1': nrm(ks[13], (DEPTH, N_EXPERTS, D_MODEL, D_EXPERT), D_MODEL ** -0.5),
        'w3': nrm(ks[14], (DEPTH, N_EXPERTS, D_MODEL, D_EXPERT), D_MODEL ** -0.5),
        'w2': nrm(ks[15], (DEPTH, N_EXPERTS, D_EXPERT, D_MODEL), DN_BETA * D_EXPERT ** -0.5),
        'ln2_g': 1.0 + nrm(ks[16], (DEPTH, D_MODEL), 0.02),
        'ln2_b': nrm(ks[17], (DEPTH, D_MODEL), 0.02),
    }

def first_block(x, mem, positions, w_in, b_in, pool_w, pool_scale, w_mem_kv, w_br, w_out,
              ln1_g, ln1_b, w_router, router_bias, w1, w3, w2, ln2_g, ln2_b):
    B, S, D = x.shape
    for l in range(DEPTH):
        mix = token_mixing(x, mem, positions, w_in[l], b_in[l], pool_w[l], pool_scale[l],
                           w_mem_kv[l], w_br[l], w_out[l])
        x = layer_norm(DN_ALPHA * x + mix, ln1_g[l], ln1_b[l])
        ffn = moe(x.reshape(B * S, D), w_router, router_bias, w1[l], w3[l], w2[l]).reshape(B, S, D)
        x = layer_norm(DN_ALPHA * x + ffn, ln2_g[l], ln2_b[l])
    return x


DEPTH_2 = 1

D_MIX = D_MODEL
GDN_HEADS = 4
GDN_HEAD_DIM = 128
GDN_WIDTH = GDN_HEADS * GDN_HEAD_DIM
CONV_WIDTH = 5
SWA_HEADS = 8
SWA_HEAD_DIM = 64
SWA_WIDTH = SWA_HEADS * SWA_HEAD_DIM
DILATION_PATTERNS = ((128, 1), (512, 4), (2048, 16))
BAND_BLOCK = 64
REL_BUCKETS = 32
REL_MAX_DISTANCE = 1024
D_FF = 2816
EPS = 1e-6
NEG_BIG = -1e30
SPLITS = (3 * GDN_WIDTH, GDN_WIDTH, 2 * GDN_HEADS, 2 * GDN_HEADS, 3 * SWA_WIDTH)
N_IN = sum(SPLITS)


def rms_norm(x, w):
    xf = x.astype(jnp.float32)
    y = xf * lax.rsqrt(jnp.mean(xf * xf, axis=-1, keepdims=True) + EPS)
    return (y * w.astype(jnp.float32)).astype(x.dtype)

def l2_normalize(x):
    return x * lax.rsqrt(jnp.sum(x * x, axis=-1, keepdims=True) + EPS)

def swiglu(x, w_gate, w_up, w_down):
    return (jax.nn.silu(x @ w_gate) * (x @ w_up)) @ w_down

def t5_bucket(rel):
    nb = REL_BUCKETS // 2
    bucket = (rel > 0).astype(np.int32) * nb
    n = np.abs(rel)
    max_exact = nb // 2
    large = max_exact + (np.log(np.maximum(n, 1) / max_exact)
                         / math.log(REL_MAX_DISTANCE / max_exact) * (nb - max_exact)).astype(np.int32)
    large = np.minimum(large, nb - 1)
    return (bucket + np.where(n < max_exact, n, large)).astype(np.int32)

def short_conv(x, w):
    c, kw = w.shape
    rhs = jnp.transpose(w).astype(x.dtype)[:, None, :]
    return lax.conv_general_dilated(x, rhs, window_strides=(1,),
                                    padding=((kw // 2, kw // 2),),
                                    dimension_numbers=('NWC', 'WIO', 'NWC'),
                                    feature_group_count=c)

def gated_delta_chunked(q, k, v, g, beta):
    b, h, t, dk = q.shape
    dv = v.shape[-1]
    nc = t // CHUNK
    q = q * (dk ** -0.5)

    def chunks(a):
        return a.reshape(b, h, nc, CHUNK, *a.shape[3:])

    q, k, v, g, beta = chunks(q), chunks(k), chunks(v), chunks(g), chunks(beta)
    g = jnp.cumsum(g, axis=-1)
    incl = jnp.tril(jnp.ones((CHUNK, CHUNK), dtype=bool))
    strict = jnp.tril(jnp.ones((CHUNK, CHUNK), dtype=bool), -1)
    diff = g[..., :, None] - g[..., None, :]
    decay = jnp.where(incl, jnp.exp(jnp.where(incl, diff, 0.0)), 0.0)
    kb = k * beta[..., None]
    lmat = jnp.where(strict, jnp.einsum('bhncd,bhnjd->bhncj', kb, k) * decay, 0.0)
    eye = jnp.eye(CHUNK, dtype=jnp.float32)
    tmat = lax.linalg.triangular_solve(eye + lmat, jnp.broadcast_to(eye, lmat.shape),
                                       left_side=True, lower=True, unit_diagonal=True)
    u = tmat @ (v * beta[..., None])
    w = tmat @ (kb * jnp.exp(g)[..., None])
    intra = jnp.einsum('bhncd,bhnjd->bhncj', q, k) * decay
    qg = q * jnp.exp(g)[..., None]
    g_last = g[..., -1]
    kdec = k * jnp.exp(g_last[..., None] - g)[..., None]

    def step(state, inp):
        u_c, w_c, qg_c, intra_c, kdec_c, gl_c = inp
        v_new = u_c - w_c @ state
        o_c = qg_c @ state + intra_c @ v_new
        state = state * jnp.exp(gl_c)[..., None, None] + jnp.swapaxes(kdec_c, -1, -2) @ v_new
        return state, o_c

    xs = tuple(jnp.moveaxis(a, 2, 0) for a in (u, w, qg, intra, kdec, g_last))
    state0 = jnp.zeros((b, h, dk, dv), jnp.float32)
    _, o = lax.scan(step, state0, xs)
    return jnp.moveaxis(o, 0, 2).reshape(b, h, t, dv)

def _reverse(a):
    return jnp.flip(a, axis=2)

def gdn_mixer(qkv, z, a, beta_logit, conv_w, a_log, dt_bias, norm_w):
    b, s, _ = qkv.shape
    f32 = jnp.float32
    qkv = jax.nn.silu(short_conv(qkv, conv_w)).astype(f32)
    qkv = qkv.reshape(b, s, 3, GDN_HEADS, GDN_HEAD_DIM).transpose(2, 0, 3, 1, 4)
    q, k, v = l2_normalize(qkv[0]), l2_normalize(qkv[1]), qkv[2]
    a = a.astype(f32).reshape(b, s, 2, GDN_HEADS)
    g = -jnp.exp(a_log.astype(f32)) * jax.nn.softplus(a + dt_bias.astype(f32))
    beta = jax.nn.sigmoid(beta_logit.astype(f32).reshape(b, s, 2, GDN_HEADS))
    g = g.transpose(2, 0, 3, 1)
    beta = beta.transpose(2, 0, 3, 1)
    o_fwd = gated_delta_chunked(q, k, v, g[0], beta[0])
    o_bwd = _reverse(gated_delta_chunked(_reverse(q), _reverse(k), _reverse(v),
                                         _reverse(g[1]), _reverse(beta[1])))
    o = (o_fwd + o_bwd).transpose(0, 2, 1, 3)
    zg = jax.nn.silu(z.astype(f32).reshape(b, s, GDN_HEADS, GDN_HEAD_DIM))
    o = rms_norm(o, norm_w) * zg
    return o.reshape(b, s, GDN_WIDTH).astype(z.dtype)

def dilated_band_attention(q, k, v, rel_bias, window, dilation):
    b, s, h, dh = q.shape
    radius = window // (2 * dilation)
    blk = BAND_BLOCK
    length = s // dilation
    nb = -(-length // blk)
    lp = nb * blk

    def to_blocks(a):
        a = a.reshape(b, length, dilation, h, dh).transpose(0, 2, 3, 1, 4)
        a = jnp.pad(a, ((0, 0), (0, 0), (0, 0), (0, lp - length), (0, 0)))
        return a.reshape(b, dilation, h, nb, blk, dh)

    def band(a):
        ap = jnp.pad(a, ((0, 0), (0, 0), (0, 0), (1, 1), (0, 0), (0, 0)))
        return jnp.concatenate([ap[:, :, :, :-2], ap[:, :, :, 1:-1], ap[:, :, :, 2:]], axis=-2)

    qb = to_blocks(q)
    kw = band(to_blocks(k))
    vw = band(to_blocks(v))
    qi = np.arange(blk)[:, None]
    ki = np.arange(3 * blk)[None, :]
    rel = ki - blk - qi
    key_t = (np.arange(nb)[:, None, None] - 1) * blk + ki[None]
    valid = (np.abs(rel)[None] <= radius) & (key_t >= 0) & (key_t < length)
    bias = jnp.transpose(rel_bias[t5_bucket(rel * dilation)], (2, 0, 1))[:, None]
    logits = jnp.einsum('bdhnqe,bdhnke->bdhnqk', qb, kw, preferred_element_type=jnp.float32)
    logits = jnp.where(valid, logits + bias.astype(jnp.float32), NEG_BIG)
    m = jnp.max(logits, axis=-1, keepdims=True)
    p = jnp.exp(logits - m)
    den = jnp.sum(p, axis=-1, keepdims=True)
    o = jnp.einsum('bdhnqk,bdhnke->bdhnqe', p, vw.astype(jnp.float32)) / den
    lse = (m + jnp.log(den))[..., 0]
    o = o.reshape(b, dilation, h, lp, dh)[:, :, :, :length].transpose(0, 3, 1, 2, 4).reshape(b, s, h, dh)
    lse = lse.reshape(b, dilation, h, lp)[..., :length].transpose(0, 3, 1, 2).reshape(b, s, h)
    return o, lse

def dilated_mixer(qkv, q_norm_w, k_norm_w, rel_bias):
    b, s, _ = qkv.shape
    qkv = qkv.reshape(b, s, 3, SWA_HEADS, SWA_HEAD_DIM)
    q = rms_norm(qkv[:, :, 0], q_norm_w) * (SWA_HEAD_DIM ** -0.5)
    k = rms_norm(qkv[:, :, 1], k_norm_w)
    v = qkv[:, :, 2]
    outs, lses = [], []
    for window, dilation in DILATION_PATTERNS:
        o_p, lse_p = dilated_band_attention(q, k, v, rel_bias, window, dilation)
        outs.append(o_p)
        lses.append(lse_p)
    wts = jax.nn.softmax(jnp.stack(lses, axis=0), axis=0)
    o = jnp.sum(wts[..., None] * jnp.stack(outs, axis=0), axis=0)
    return o.reshape(b, s, SWA_WIDTH).astype(qkv.dtype)

def second_inputs(seed: int = 0) -> dict:
    key = jax.random.key(seed)
    ks = jax.random.split(key, 24)
    f32 = jnp.float32

    def dense(k, shape, fan_in):
        return jax.random.normal(k, shape, f32) * (fan_in ** -0.5)

    def gain(k, shape):
        return 1.0 + 0.02 * jax.random.normal(k, shape, f32)

    x = jax.random.normal(ks[0], (BATCH, SEQ, D_MODEL), f32)
    ffn1_norm = gain(ks[1], (DEPTH_2, D_MODEL))
    ffn1_w_gate = dense(ks[2], (DEPTH_2, D_MODEL, D_FF), D_MODEL)
    ffn1_w_up = dense(ks[3], (DEPTH_2, D_MODEL, D_FF), D_MODEL)
    ffn1_w_down = dense(ks[4], (DEPTH_2, D_FF, D_MODEL), D_FF)
    mix_norm = gain(ks[5], (DEPTH_2, D_MODEL))
    w_in = dense(ks[6], (DEPTH_2, D_MODEL, N_IN), D_MODEL)
    conv_w = dense(ks[7], (DEPTH_2, 3 * GDN_WIDTH, CONV_WIDTH), CONV_WIDTH)
    a_log = jnp.log(jax.random.uniform(ks[8], (DEPTH_2, 2, GDN_HEADS), f32, 1.0, 16.0))
    dt = jnp.exp(jax.random.uniform(ks[9], (DEPTH_2, 2, GDN_HEADS), f32, math.log(1e-3), math.log(1e-1)))
    dt_bias = dt + jnp.log(-jnp.expm1(-dt))
    gdn_norm_w = gain(ks[10], (DEPTH_2, GDN_HEAD_DIM))
    q_norm_w = gain(ks[11], (DEPTH_2, SWA_HEAD_DIM))
    k_norm_w = gain(ks[12], (DEPTH_2, SWA_HEAD_DIM))
    rel_bias = 0.2 * jax.random.normal(ks[13], (REL_BUCKETS, SWA_HEADS), f32)
    w_out = dense(ks[14], (DEPTH_2, D_MIX, D_MODEL), D_MIX)
    ffn2_norm = gain(ks[15], (DEPTH_2, D_MODEL))
    ffn2_w_gate = dense(ks[16], (DEPTH_2, D_MODEL, D_FF), D_MODEL)
    ffn2_w_up = dense(ks[17], (DEPTH_2, D_MODEL, D_FF), D_MODEL)
    ffn2_w_down = dense(ks[18], (DEPTH_2, D_FF, D_MODEL), D_FF)
    final_norm = gain(ks[19], (DEPTH_2, D_MODEL))
    return {"x": x, "ffn1_norm": ffn1_norm, "ffn1_w_gate": ffn1_w_gate, "ffn1_w_up": ffn1_w_up,
            "ffn1_w_down": ffn1_w_down, "mix_norm": mix_norm, "w_in": w_in, "conv_w": conv_w,
            "a_log": a_log, "dt_bias": dt_bias, "gdn_norm_w": gdn_norm_w, "q_norm_w": q_norm_w,
            "k_norm_w": k_norm_w, "rel_bias": rel_bias, "w_out": w_out, "ffn2_norm": ffn2_norm,
            "ffn2_w_gate": ffn2_w_gate, "ffn2_w_up": ffn2_w_up, "ffn2_w_down": ffn2_w_down,
            "final_norm": final_norm}

def second_block(x, ffn1_norm, ffn1_w_gate, ffn1_w_up, ffn1_w_down, mix_norm, w_in, conv_w,
              a_log, dt_bias, gdn_norm_w, q_norm_w, k_norm_w, rel_bias, w_out, ffn2_norm,
              ffn2_w_gate, ffn2_w_up, ffn2_w_down, final_norm):
    split_at = np.cumsum(SPLITS)[:-1].tolist()
    for l in range(DEPTH_2):
        x = x + 0.5 * swiglu(rms_norm(x, ffn1_norm[l]), ffn1_w_gate[l], ffn1_w_up[l], ffn1_w_down[l])
        h = rms_norm(x, mix_norm[l])
        proj = h @ w_in[l]
        qkv_a, z_a, a_a, b_a, qkv_b = jnp.split(proj, split_at, axis=-1)
        o_a = gdn_mixer(qkv_a, z_a, a_a, b_a, conv_w[l], a_log[l], dt_bias[l], gdn_norm_w[l])
        o_b = dilated_mixer(qkv_b, q_norm_w[l], k_norm_w[l], rel_bias)
        x = x + jnp.concatenate([o_a, o_b], axis=-1) @ w_out[l]
        x = x + 0.5 * swiglu(rms_norm(x, ffn2_norm[l]), ffn2_w_gate[l], ffn2_w_up[l], ffn2_w_down[l])
        x = rms_norm(x, final_norm[l])
    return x


def setup_inputs(seed=0):
    out = dict(first_inputs(seed))
    for name, value in second_inputs(seed + 1).items():
        if name != "x":
            out[name + "_2"] = value
    return out


def reference(
    x, mem, positions, w_in, b_in, pool_w, pool_scale, w_mem_kv, w_br, w_out, ln1_g, ln1_b,
    w_router, router_bias, w1, w3, w2, ln2_g, ln2_b, ffn1_norm_2, ffn1_w_gate_2, ffn1_w_up_2,
    ffn1_w_down_2, mix_norm_2, w_in_2, conv_w_2, a_log_2, dt_bias_2, gdn_norm_w_2, q_norm_w_2,
    k_norm_w_2, rel_bias_2, w_out_2, ffn2_norm_2, ffn2_w_gate_2, ffn2_w_up_2, ffn2_w_down_2,
    final_norm_2,
):
    x = first_block(
        x, mem, positions, w_in, b_in, pool_w, pool_scale, w_mem_kv, w_br, w_out, ln1_g, ln1_b,
        w_router, router_bias, w1, w3, w2, ln2_g, ln2_b,
    )
    return second_block(
        x, ffn1_norm_2, ffn1_w_gate_2, ffn1_w_up_2, ffn1_w_down_2, mix_norm_2, w_in_2, conv_w_2,
        a_log_2, dt_bias_2, gdn_norm_w_2, q_norm_w_2, k_norm_w_2, rel_bias_2, w_out_2,
        ffn2_norm_2, ffn2_w_gate_2, ffn2_w_up_2, ffn2_w_down_2, final_norm_2,
    )


_drawn_inputs = setup_inputs


def setup_inputs(seed=0):
    import zlib

    import numpy as np

    out = dict(_drawn_inputs(seed))
    spreads = {}
    factors = {'b_in': 2.771,
     'pool_scale': 7.681,
     'ffn1_norm_2': 6.005,
     'mix_norm_2': 4.627,
     'gdn_norm_w_2': 7.745,
     'q_norm_w_2': 8.0,
     'k_norm_w_2': 8.0,
     'rel_bias_2': 3.894,
     'ffn2_norm_2': 7.851}
    for name, (base, spread) in spreads.items():
        noise = np.random.default_rng([zlib.crc32(name.encode()), seed]).standard_normal(out[name].shape)
        drawn = base * np.exp(spread * noise) if base else spread * noise
        out[name] = jnp.asarray(drawn.astype(out[name].dtype))
    for name, factor in factors.items():
        out[name] = (out[name] * factor).astype(out[name].dtype)
    return out
```

```python
import concourse.bass as bass
import concourse.mybir as mybir
from contextlib import ExitStack

F32 = mybir.dt.float32
I32 = mybir.dt.int32
U32 = mybir.dt.uint32
ACT = mybir.ActivationFunctionType
ALU = mybir.AluOpType
AX = mybir.AxisListType

P = 128
S = 512
D = 1024
KC = D // P
NT = S // P
DEPTH = 2
N_MEM = 256
HEADS, HEAD_DIM = 8, 64
MEM_HEADS, MEM_DIM = 4, 128
N_SEL = 128
N_EXP, GROUPS, PER_GROUP = 16, 4, 4
D_EXP = 512
MOE_BLOCK = 128
N_BLK = (2 * S + N_EXP * (MOE_BLOCK - 1)) // MOE_BLOCK
XS_BLK = N_BLK + 2
XS_OF = [XS_BLK - XS_BLK // 2, XS_BLK // 2]
YS_OF = [N_BLK - N_BLK // 2, N_BLK // 2]
assert N_BLK % 2 == 1
DN_ALPHA = (2 * DEPTH) ** 0.25
LN_EPS, EPS = 1e-5, 1e-6
D_FF = 2816
FC = D_FF // P
CH = 64
NCH = S // CH
GH = 4
UN = 2 * GH
LEVELS = 6
CONV = 5
BIG_NEG = -1e30
LOWEST = -3e38

SLOTS, PAIR = 3, 2 * KC * P
LAYER_STREAM = 39
MOE_PAIRS = 6
UP_PAIRS = 4
LAYER_PAIRS = LAYER_STREAM + MOE_PAIRS * N_BLK
LAYER_USES = LAYER_PAIRS // SLOTS
TAIL_PAIRS = 87
assert LAYER_STREAM % SLOTS == LAYER_PAIRS % SLOTS == TAIL_PAIRS % SLOTS == MOE_PAIRS % SLOTS == 0

G_POOL, G_Q, G_MQ, G_K, G_IQ, G_IK, G_V, G_IW, N_G = 0, 4, 8, 12, 16, 20, 21, 25, 26
MEM_GROUPS = 8
LIN_LAYER = MEM_GROUPS + N_G
ROT_GROUPS = [*range(G_IQ, G_IQ + 4), G_IK, *range(G_Q, G_Q + 4), *range(G_K, G_K + 4)]
N_ROT, ROT_IDX = len(ROT_GROUPS), 5
ORDER = [*range(G_IQ, G_IQ + 4), G_IK, G_IW, *range(G_Q, G_Q + 4), *range(G_K, G_K + 4), *range(G_POOL, G_POOL + 4),
         *range(G_V, G_V + 4), *range(G_MQ, G_MQ + 4)]
AT_MV, AT_IW, AT_SCORE, AT_ROT, AT_VT = 5, 7, {8: 1, 13: 2, 18: 3}, {12: 5, 17: 9}, 24
N_TOP = NT - 1
assert P <= N_SEL
H_Q, H_K, H_SQ, H_SK, H_V, H_Z, H_SV, H_AB, N_H = 0, 4, 8, 12, 16, 20, 24, 28, 30
CONV_GROUPS = [*range(H_Q, H_Q + 8), *range(H_V, H_V + 4)]
N_NORM = 16

ATT = HEADS + MEM_HEADS
LOGIT_BANKS = (0, 1, 6)
OUT_BANKS = (0, 1, 6, 7, 2, 3, 4, 5)

TWO_PI = 6.283185307179586
PI_A, PI_B = 6.28125, 0.0019350051879882812
PI_C = TWO_PI - PI_A - PI_B
ROUND = 12582912.0



def two_blocks(nc, a, out):
    ctx = ExitStack()
    with ctx:
        def sb(name, cols, dt=F32, rows=P):
            return ctx.enter_context(nc.sbuf_tensor(name, [rows, cols], dt))

        def sem(name):
            return ctx.enter_context(nc.semaphore(name))

        cst = sb("cst", 6 * P)
        identity, ones, block_ones, rot, reverse, tri = (cst[:, c * P:(c + 1) * P] for c in range(6))
        cos_t, sin_t = sb("cos_t", S), sb("sin_t", S)
        ring = [sb(f"ring{s}", PAIR) for s in range(SLOTS)]
        xT = sb("xT", KC * S)
        xtok = sb("xtok", NT * D)
        big = sb("big", 30 * S)
        am = sb("am", KC * S)
        lnw = sb("lnw", NT * S)
        sr = sb("sr", 13312)
        bias_p, bias_g = sb("bias_p", DEPTH * N_G), sb("bias_g", DEPTH * 24)
        pool_scale, pool_rec = sb("pool_scale", DEPTH * 4), sb("pool_rec", 4 * 16)
        w_router, r_bias = sb("w_router", KC * N_EXP), sb("r_bias", N_EXP)
        inv_freq, blk_iota = sb("inv_freq", 1), sb("blk_iota", N_BLK)
        before = sb("before", PER_GROUP * PER_GROUP)
        iw_tok = sb("iw_tok", NT * 8)
        top8 = sb("top8", 8)
        stat = sb("stat", 64)
        ln_st, ln_mv = sb("ln_st", NT * 12), sb("ln_mv", NT * 5)
        ln_T = sb("ln_T", 2 * DEPTH * 2 * KC)
        dest = sb("dest", 2 * NT, I32)
        blk_e = sb("blk_e", N_BLK, I32)
        gate2 = sb("gate2", 2 * NT)
        normw = sb("normw", 4 * KC)
        conv_w = sb("conv_w", 12 * CONV)
        gn_w, qk_w = sb("gn_w", 1), sb("qk_w", 2)
        rel_b = sb("rel_b", HEADS, rows=32)
        ab, ga = sb("ab", NCH * 16), sb("ga", NCH * UN)
        gg, gbeta = sb("gg", NCH * GH), sb("gbeta", NCH * GH)
        alog, dtb = sb("alog", UN), sb("dtb", UN)
        gtri, id_pair, half_ones = sb("gtri", CH), sb("id_pair", CH), sb("half_ones", 2 * P)
        gs, bs, gend, dfac = (sb(n, GH) for n in ("gs", "bs", "gend", "dfac"))
        gl, egl = sb("gl", UN), [sb(f"egl{i}", UN) for i in range(2)]
        pb = [ctx.enter_context(nc.psum_tensor(f"pb{i}", [P, S], F32)) for i in range(8)]

        xs_dram = nc.dram_tensor("xs_dram", (XS_BLK * MOE_BLOCK, D), F32).ap()
        ys_dram = nc.dram_tensor("ys_dram", (N_BLK * MOE_BLOCK, D), F32).ap()
        rel_dram = nc.dram_tensor("rel_dram", (HEADS, 1024), F32)

        def grp(t, g, n=1, w=S):
            if isinstance(g, int):
                return t[:, g * w:(g + n) * w]
            return t[:, bass.ds(g * w, n * w)]

        def cut(ap, n):
            return ap.rearrange("p (g n) -> p g n", n=n)

        at = [0]

        def take(cols, rows=P):
            at[0] += cols
            assert at[0] <= 13312, at[0]
            return sr[0:rows, at[0] - cols:at[0]]

        adm = am[:, 0:NT * S]
        memT = am[:, NT * S:NT * S + KC * N_MEM]
        mk, mv, mvf = take(4 * N_MEM), take(2 * S), take(4 * N_MEM)
        relu2 = [take(S) for _ in range(2)]
        score, work, maskb = take(S), take(S), take(S)
        lg = [take(S) for _ in range(3)]
        pT = [take(S) for _ in range(2)]
        iq_b, q_b, mq_b = take(S), take(S), take(S)
        tmp = [take(S) for _ in range(2)]
        pw_b = take(S)
        vtok = grp(big, N_G, 4)
        merged = grp(big, G_K, 8)
        ln_par = grp(big, G_IK, 4)
        xs = [grp(big, 0, 2), grp(big, 2, 2)]
        xsT = [grp(big, 4, 2), grp(big, 6, 2)]
        sil, hid, hT = grp(big, 8), grp(big, 9), grp(big, 10)
        ysb = [grp(big, 11, 2), grp(big, 13, 2)]
        yg = [[grp(big, 15, 2), grp(big, 17, 2)], [grp(big, 24, 2), grp(big, 26, 2)]]
        rt = take(1024)
        rat = [0]

        def rtile(cols):
            rat[0] += cols
            return rt[:, rat[0] - cols:rat[0]]

        r_score, r_biased, r_rank, r_pick, r_t = (rtile(NT * N_EXP) for _ in range(5))
        r_one, r_u = [rtile(NT * N_EXP) for _ in range(2)], [rtile(NT * N_EXP) for _ in range(2)]
        r_gsum, r_grank, r_nblk, r_end = (rtile(N_EXP) for _ in range(4))
        r_cmp = tmp
        r_sum, r_dest, r_blk = rtile(NT), rtile(2 * NT), rtile(N_BLK)
        assert rat[0] <= 1024 and max(NT * GROUPS * PER_GROUP ** 2, N_BLK * N_EXP) <= S
        xn = xtok[:, :]
        at[0] = HEADS * 896 + NT * S + 2 * S
        sgl = [take(S) for _ in range(3)]
        sq2 = [take(S) for _ in range(2)]
        rs = take(S)
        at[0] = 0
        hank = take(HEADS * 896)
        v2 = take(NT * S)
        rel_oh = v2[0:32, 0:1024]
        rel_row = sr[0:HEADS, at[0]:at[0] + 1024]
        lg2 = [take(S) for _ in range(3)]
        pT2 = [take(S) for _ in range(2)]
        q2_b, lnw_b = take(S), take(S)
        ctmp = [pT2[0], pT2[1]]
        nsq = lg2[0:2]
        nrm = am[:, :]
        at[0] = 0
        ks, qs, vs, eg, kbF = (take(UN * CH) for _ in range(5))
        qg = [take(UN * CH) for _ in range(2)]
        dg, db, dT, lT, lbT, Tm, Mm, Am = (take(GH * CH) for _ in range(8))
        inT = [take(GH * CH) for _ in range(2)]
        vB, resid, vn = (take(GH * P) for _ in range(3))
        kdec = [take(GH * P) for _ in range(2)]
        st = [take(UN * P) for _ in range(2)]
        LW = GH * CH
        msk = am[:, 0:(LEVELS + 1) * LW]
        cat = xtok[:, :]
        of, ob = cat[:, 0:4 * S], lnw[:, :]

        loaded, rope_loaded, mem_loaded = sem("constants_loaded"), sem("positions_loaded"), sem("memory_loaded")
        xtok_loaded, lnw_loaded = sem("xtok_loaded"), sem("lnw_loaded")
        masks_loaded, hank_loaded, rel_stored = sem("masks_loaded"), sem("hank_loaded"), sem("rel_stored")
        xs_zeroed, zero_ready = sem("xs_zeroed"), sem("zero_ready")
        w_loaded = [sem(f"weights_loaded{s}") for s in range(SLOTS)]
        slot_free = sem("slot_free")
        rope_arg, rope_sin = sem("rope_arg"), sem("rope_sin")
        lin_ready, lin_free = sem("lin_ready"), sem("lin_free")
        rot_ready, rot_used = sem("rot_ready"), sem("rot_used")
        vt_ready, vt_copied = sem("v_transposed"), sem("v_copied")
        pool_w_loaded, oh_loaded = sem("pool_w_loaded"), sem("buckets_loaded")
        pool_in, pool_mixed, pool_done = sem("pool_in"), sem("pool_mixed"), sem("pool_done")
        adm_loaded, masks_ready, iq_staged = sem("adm_loaded"), sem("masks_ready"), sem("iq_staged")
        staged, idx_ready, idx_copied, idx_used = sem("staged"), sem("idx_ready"), sem("idx_copied"), sem("idx_used")
        lg_ready, lg_masked, exp_done, p_ready = sem("logits_ready"), sem("logits_masked"), sem("exp_done"), sem("p_ready")
        tr_ready, pT_ready, pv_ready, att_done = sem("p_transposed"), sem("pT_ready"), sem("pv_ready"), sem("att_done")
        merged_ready = sem("merged_ready")
        gate_ready, gate_free, br_ready, br_free = sem("gate_ready"), sem("gate_free"), sem("br_ready"), sem("br_free")
        mix_ready = sem("mix_ready")
        ln_loaded, var_ready, std_ready, shift_ready = sem("ln_loaded"), sem("var_ready"), sem("std_ready"), sem("shift_ready")
        normed, tok_done = sem("rows_normed"), sem("rows_scaled")
        xtr_ready, xT_ready = sem("xtr_ready"), sem("xT_ready")
        sc_ready, sig_ready, pick_ready, rank_ready, dest_ready, route_ready = (
            sem(n) for n in ("router_logits", "router_scores", "picks_ready", "ranks_ready", "dest_ready", "route_ready"))
        xs_scattered = sem("xs_scattered")
        xs_loaded = [sem(f"xs_loaded{s}") for s in range(2)]
        xs_tr, xsT_ready = sem("xs_transposed"), sem("xsT_ready")
        up_ready, sil_ready, hid_ready = sem("up_ready"), sem("sil_ready"), sem("hid_ready")
        ht_ready, hT_ready, y_ready, y_copied = sem("h_transposed"), sem("hT_ready"), sem("y_ready"), sem("y_copied")
        y_stored = [sem(f"y_stored{s}") for s in range(2)]
        y_back = [sem(f"y_back{s}") for s in range(2)]
        yg_used = sem("y_gathered_used")
        sq_ready, sq_used, rvar, rstd, xn_ready = (
            sem(n) for n in ("sq_ready", "sq_used", "rms_var", "rms_std", "xn_ready"))
        ff_ready, ff_silu, ff_free = sem("ff_ready"), sem("ff_silu"), sem("ff_free")
        dn_ready, dn_free = sem("down_ready"), sem("down_free")
        conv_ready, conv_silu = sem("conv_ready"), sem("conv_silu")
        nsq_ready, nsum_ready, nsum_used, nstd, n_done = (
            sem(n) for n in ("norm_sq", "norm_sums", "norm_sums_used", "norm_std", "norm_done"))
        rel_ready, rel_copied = sem("rel_ready"), sem("rel_copied")
        v2_tr, v2_ready = sem("v2_transposed"), sem("v2_ready")
        ab_tr, ab_ready, sp_ready, g_ready, gc_ready, gc_done = (
            sem(n) for n in ("ab_transposed", "ab_ready", "softplus_ready", "g_ready", "g_cumsum", "g_done"))
        g_staged, g_diag, g_rows, g_eg, g_diff, g_dexp = (sem("delta_" + n) for n in (
            "staged", "diagonals", "rows", "row_exps", "differences", "decays"))
        g_kv_used, g_mats = sem("delta_kv_used"), sem("delta_mats")
        g_a, g_am, g_up, g_tm = (sem("delta_" + n) for n in ("level_product", "level_copied", "level_update", "level_done"))
        g_r, g_rsub, g_vnm, g_vn, g_out, g_o, g_state = (sem("delta_" + n) for n in (
            "state_part", "residual", "new_values", "new_values_copied", "output", "output_copied", "state"))
        o_sum, o_sq, o_ss, o_var, o_std, o_done = (
            sem(n) for n in ("o_sum", "o_sq", "o_sumsq", "o_var", "o_std", "o_done"))
        out_stored = sem("out_stored")
        passed = sem("waits_passed")

        ROPE_CONSTS = [(work.bitcast(I32), a["positions"].partition_broadcast(P)), (inv_freq[:, :], a["inv_freq"])]
        CONSTS = [
            (cst[:, :], a["cst"]), (bias_p[:, :], a["bias_p"]), (xT[:, :], a["xT"]),
            (pool_scale[:, :], a["pool_scale"]), (pool_rec[:, :], a["pool_rec"]), (bias_g[:, :], a["bias_g"]),
            (w_router[:, :], a["w_router"]), (r_bias[:, :], a["router_bias"].partition_broadcast(P)),
            (blk_iota[:, :], a["blk_iota"]), (before[:, :], a["before"]), (ln_T[:, :], a["ln_T"]), (normw[:, :], a["normw"]),
            (conv_w[:, :], a["conv_w"]), (gn_w[:, :], a["gn_w"]), (qk_w[:, :], a["qk_w"]),
            (rel_b[:, :], a["rel_b"]),
            (alog[:, :], a["a_log"].partition_broadcast(P)), (dtb[:, :], a["dt_bias"].partition_broadcast(P)),
            (gtri[:, :], a["gtri"]),
        ]
        N_CONST = 16 * len(CONSTS)

        def alone(eng):
            eng.sem_inc(passed, 1)

        block = ctx.enter_context(nc.Block())

        @block.sync
        def _(sp):
            sp.dma_start(memT, a["memT"]).then_inc(mem_loaded, 16)
            with sp.Fori(0, DEPTH) as l:
                with sp.Fori(0, LAYER_STREAM // SLOTS) as i:
                    for s in range(SLOTS):
                        sp.wait_ge(slot_free, l * LAYER_PAIRS + i * SLOTS + s + 1)
                        sp.dma_start(ring[s][:, :], a["w_layer"][bass.ds(l * LAYER_STREAM + i * SLOTS + s, 1)]
                                     .rearrange("a p n -> p (a n)")).then_inc(w_loaded[s], 16)
                sp.wait_ge(route_ready, l + 1)
                alone(sp)

                def expert_pairs(b, first, count, at, slot):
                    e = sp.value_load(blk_e[0:1, bass.ds(b, 1)], min_val=0, max_val=N_EXP - 1)
                    for j in range(count):
                        u = (slot + j) % SLOTS
                        sp.wait_ge(slot_free, l * LAYER_PAIRS + LAYER_STREAM + at + j + 1)
                        sp.dma_start(ring[u][:, :], a["w_moe"][bass.ds((l * N_EXP + e) * MOE_PAIRS + first + j, 1)]
                                     .rearrange("a p n -> p (a n)")).then_inc(w_loaded[u], 16)

                expert_pairs(0, 0, UP_PAIRS, 0, 0)
                with sp.Fori(0, N_BLK - 1) as i:
                    expert_pairs(i + 1, 0, UP_PAIRS, UP_PAIRS + i * MOE_PAIRS, UP_PAIRS)
                    expert_pairs(i, UP_PAIRS, 2, 2 * UP_PAIRS + i * MOE_PAIRS, 2 * UP_PAIRS)
                expert_pairs(N_BLK - 1, UP_PAIRS, 2, UP_PAIRS + (N_BLK - 1) * MOE_PAIRS, UP_PAIRS)
            with sp.Fori(0, TAIL_PAIRS // SLOTS) as i:
                for s in range(SLOTS):
                    sp.wait_ge(slot_free, DEPTH * LAYER_PAIRS + i * SLOTS + s + 1)
                    sp.dma_start(ring[s][:, :], a["w_tail"][bass.ds(i * SLOTS + s, 1)]
                                 .rearrange("a p n -> p (a n)")).then_inc(w_loaded[s], 16)
            sp.wait_ge(xn_ready, 4)
            sp.dma_start(out, xn).then_inc(out_stored, 16)
            sp.wait_ge(out_stored, 16)

        @block.gpsimd
        def _(pool):
            zero = lnw[:, 0:D]
            nc.gpsimd.memset(zero, 0.0).then_inc(zero_ready, 1)
            pool.wait_ge(loaded, N_CONST)
            pool.dma_start(xtok[:, :], a["xtok"]).then_inc(xtok_loaded, 16)
            pool.wait_ge(zero_ready, 1)
            with pool.Fori(0, XS_BLK) as b:
                pool.dma_start(xs_dram[bass.ds(b * MOE_BLOCK, MOE_BLOCK), :], zero).then_inc(xs_zeroed, 16)
            for s in range(2):
                pool.dma_start(ys_dram[s * MOE_BLOCK:(s + 1) * MOE_BLOCK, :], zero).then_inc(y_stored[s], 16)

            def scale_rows(m):
                pool.wait_ge(ln_loaded, 16 * (m + 1))
                alone(pool)
                for t in range(NT):
                    pool.wait_ge(xtr_ready, m * NT + t + 1)
                    alone(pool)
                    x = grp(xtok, t, 1, D)
                    nc.gpsimd.tensor_tensor(x, x, ln_par[:, 0:D], ALU.mult)
                pool.drain()
                for t in range(NT):
                    x = grp(xtok, t, 1, D)
                    last = nc.gpsimd.tensor_tensor(x, x, ln_par[:, D:2 * D], ALU.add)
                last.then_inc(tok_done, 1)

            with pool.Fori(0, DEPTH) as l:
                pool.dma_start(adm, a["adm"]).then_inc(adm_loaded, 16)
                pool.wait_ge(pool_done, l + 1)
                pool.dma_start(cut(pw_b, P), a["pool_w"][bass.ds(l * 4, 4)].rearrange("g c e -> c g e")).then_inc(pool_w_loaded, 16)
                pool.wait_ge(att_done, l * NT + NT)
                pool.dma_start(ln_par, a["ln_par"][bass.ds(2 * l, 1), :].rearrange("a n -> (a n)").partition_broadcast(P)).then_inc(ln_loaded, 16)
                scale_rows(2 * l)
                pool.wait_ge(xs_zeroed, 16 * XS_BLK)
                pool.wait_ge(tok_done, 2 * l + 2)
                pool.wait_ge(dest_ready, l + 1)
                alone(pool)
                for k in range(2):
                    for t in range(NT):
                        pool.indirect_dma_start(
                            out=xs_dram, out_offset=bass.IndirectOffsetOnAxis(
                                ap=dest[:, k * NT + t:k * NT + t + 1].bitcast(U32), axis=0),
                            in_=grp(xtok, t, 1, D), in_offset=None).then_inc(xs_scattered, 16)
                pool.wait_ge(xs_scattered, l * 128 + 128)
                pool.dma_start(ln_par, a["ln_par"][bass.ds(2 * l + 1, 1), :].rearrange("a n -> (a n)").partition_broadcast(P)).then_inc(ln_loaded, 16)
                for s in range(2):
                    pool.dma_start(xs[s], xs_dram[s * MOE_BLOCK:(s + 1) * MOE_BLOCK, :]).then_inc(xs_loaded[s], 16)

                def load_behind(b, s):
                    pool.wait_ge(xs_tr, l * (N_BLK + 1) + b + 1)
                    alone(pool)
                    pool.dma_start(xs[s], xs_dram[bass.ds((b + 2) * MOE_BLOCK, MOE_BLOCK), :]).then_inc(xs_loaded[s], 16)

                def store_y(b, s):
                    pool.wait_ge(y_copied, 2 * (l * N_BLK + b + 1) + 1)
                    alone(pool)
                    pool.dma_start(ys_dram[bass.ds(b * MOE_BLOCK, MOE_BLOCK), :], ysb[s]).then_inc(y_stored[s], 16)

                for s in range(2):
                    load_behind(s, s)
                with pool.Fori(0, N_BLK // 2 - 1) as i:
                    for s in range(2):
                        load_behind(i * 2 + s + 2, s)
                        store_y(i * 2 + s, s)
                load_behind(N_BLK - 1, 0)
                for b in range(N_BLK - 3, N_BLK):
                    store_y(b, b % 2)
                for s in range(2):
                    pool.wait_ge(y_stored[s], 16 * YS_OF[s] * (l + 1) + 16)
                    pool.wait_ge(xs_loaded[s], 16 * XS_OF[s] * (l + 1))
                alone(pool)
                for t in range(NT):
                    if t >= 2:
                        pool.wait_ge(yg_used, l * NT + t - 1)
                        alone(pool)
                    for k in range(2):
                        pool.indirect_dma_start(
                            out=yg[t % 2][k], out_offset=None, in_=ys_dram,
                            in_offset=bass.IndirectOffsetOnAxis(
                                ap=dest[:, k * NT + t:k * NT + t + 1].bitcast(U32), axis=0)).then_inc(y_back[t % 2], 16)
                scale_rows(2 * l + 1)
            pool.dma_start(lnw[:, :], a["lnw"]).then_inc(lnw_loaded, 16)
            pool.wait_ge(xT_ready, 4 * KC + 1)
            pool.dma_start(rel_oh, a["rel_oh"]).then_inc(oh_loaded, 16)
            pool.wait_ge(rel_copied, 2)
            pool.dma_start(rel_dram.ap(), rel_row).then_inc(rel_stored, 16)
            pool.wait_ge(rel_stored, 16)
            pool.dma_start(cut(hank, 896), bass.AP(tensor=rel_dram, offset=0, ap=[[1, P], [1024, HEADS], [1, 896]])).then_inc(hank_loaded, 16)
            pool.wait_ge(n_done, 2)
            pool.dma_start(msk, a["msk"]).then_inc(masks_loaded, 16)

        @block.tensor
        def _(pe):
            mm = nc.tensor.matmul

            def pair(j, l=None, i=0, per=1):
                base = DEPTH * LAYER_USES if l is None else l * LAYER_USES
                pe.wait_ge(w_loaded[j % SLOTS], (base + (j // SLOTS + 1) + i * per) * 16)
                return ring[j % SLOTS]

            def unit(w, u, k):
                return w[:, (u * KC + k) * P:(u * KC + k + 1) * P]

            def linear(w, u, rhs, n, bank, cols=S):
                pe.wait_ge(lin_free, n + 1)
                for k in range(KC):
                    last = mm(pb[bank][:, 0:cols], unit(w, u, k), rhs[:, k * cols:(k + 1) * cols],
                              start=(k == 0), stop=(k == KC - 1))
                    if k == 0 and u == 0:
                        last.then_inc(slot_free, 1)
                last.then_inc(lin_ready, 1)

            def transpose_tile(m, t):
                pe.wait_ge(normed, m * NT + t + 1)
                if t >= 2:
                    pe.wait_ge(xT_ready, m * KC + 2 * (t - 1) + 1)
                alone(pe)
                for k in range(KC):
                    last = nc.tensor.transpose(pb[2 * (t % 2) + k // 4][:, k % 4 * P:(k % 4 + 1) * P], xtok[:, t * D + k * P:t * D + (k + 1) * P], identity)
                last.then_inc(xtr_ready, 1)

            def heads(n0, count, logits, values, tr, buf_p, buf_pT):
                for step in range(count + 3):
                    if step < count:
                        h = step
                        if h >= 3:
                            pe.wait_ge(lg_masked, n0 + h - 2)
                            alone(pe)
                        logits(h, pb[LOGIT_BANKS[h % 3]]).then_inc(lg_ready, 1)
                    if 2 <= step < count + 2:
                        h = step - 2
                        pe.wait_ge(p_ready, n0 + h + 1)
                        if h >= 2:
                            pe.wait_ge(pT_ready, n0 + h - 1)
                        for t in range(tr(h)):
                            last = nc.tensor.transpose(pb[2 + h % 2][:, t * P:(t + 1) * P], buf_p[h % 3][:, t * P:(t + 1) * P], identity)
                        last.then_inc(tr_ready, 1)
                    if step >= 3:
                        h = step - 3
                        pe.wait_ge(pT_ready, n0 + h + 1)
                        values(h, buf_pT[h % 2]).then_inc(pv_ready, 1)

            pe.sem_inc(slot_free, SLOTS - 1)
            for ahead in (xT_ready, y_copied, hid_ready, ht_ready, g_o, pool_done):
                pe.sem_inc(ahead, 1)
            pe.sem_inc(lin_free, 2)
            pe.sem_inc(gate_free, 2)
            pe.sem_inc(br_free, 2)
            pe.sem_inc(ff_free, 3)
            pe.sem_inc(dn_free, 2)
            pe.wait_ge(mem_loaded, 16)

            with pe.Fori(0, DEPTH) as l:
                pe.wait_ge(xT_ready, l * 2 * KC + 1)
                for j in range(4):
                    w = pair(j, l)
                    for u in range(2):
                        linear(w, u, memT, l * LIN_LAYER + 2 * j + u, u, N_MEM)
                pe.wait_ge(loaded, N_CONST)
                L0 = l * LIN_LAYER + MEM_GROUPS

                def rotate(n):
                    if n >= 4:
                        pe.wait_ge(rot_used, l * N_ROT + n - 3)
                        alone(pe)
                    mm(pb[2 + n % 4][:], rot, grp(big, ROT_GROUPS[n]), start=True, stop=True).then_inc(rot_ready, 1)

                for p in range(N_G):
                    linear(pair(4 + p // 2, l), p % 2, xT, L0 + p, p % 2)
                    if 2 <= p < 2 + ROT_IDX:
                        pe.wait_ge(lin_free, L0 + p - 2 + 1 + 2)
                        alone(pe)
                        rotate(p - 2)
                    if p == AT_MV:
                        for t in range(2):
                            for c in range(4):
                                last = nc.tensor.transpose(pb[6 + t][:, c * P:(c + 1) * P], mvf[:, c * N_MEM + t * P:c * N_MEM + (t + 1) * P], identity)
                        last.then_inc(vt_ready, 1)
                    if p == AT_IW:
                        pe.wait_ge(vt_copied, 3 * l + 1)
                        alone(pe)
                        for t in range(NT):
                            last = nc.tensor.transpose(pb[6][:, t * 8:(t + 1) * 8], big[0:8, G_IW * S + t * P:G_IW * S + (t + 1) * P], identity[0:8, 0:8])
                        last.then_inc(vt_ready, 1)
                    if p in AT_SCORE:
                        n0 = l * N_TOP + AT_SCORE[p] - 1
                        pe.wait_ge(iq_staged, n0 + 1)
                        alone(pe)
                        for h in range(HEADS):
                            r = 64 * (h % 2)
                            if h >= 2 or AT_SCORE[p] > 1:
                                pe.wait_ge(idx_copied, n0 * HEADS + h - 1)
                                alone(pe)
                            mm(pb[6 + h % 2][:], iq_b[r:r + 64, h // 2 * P:(h // 2 + 1) * P], big[r:r + 64, G_IK * S:(G_IK + 1) * S],
                               start=True, stop=True).then_inc(idx_ready, 1)
                    if p in AT_ROT:
                        for n in range(AT_ROT[p], AT_ROT[p] + 4):
                            rotate(n)
                    if p == AT_VT:
                        pe.wait_ge(rot_used, (l + 1) * N_ROT)
                        alone(pe)
                        for t in range(NT):
                            for c in range(4):
                                last = nc.tensor.transpose(pb[4 + t][:, c * P:(c + 1) * P], big[:, (G_V + c) * S + t * P:(G_V + c) * S + (t + 1) * P], identity)
                        last.then_inc(vt_ready, 1)
                pe.wait_ge(lin_free, (l + 1) * LIN_LAYER + 2)
                pe.wait_ge(vt_copied, 3 * l + 3)
                pe.wait_ge(pool_w_loaded, 16 * l + 16)
                for g in range(4):
                    pe.wait_ge(pool_in, l * 4 + g + 1)
                    mm(pb[4 + g][:], pw_b[:, g * P:(g + 1) * P], grp(big, G_POOL + g), start=True, stop=True).then_inc(pool_mixed, 1)
                pe.wait_ge(pool_done, l + 1 + 1)
                alone(pe)
                with pe.Fori(0, NT) as b:
                    pe.wait_ge(staged, l * NT + b + 1)
                    def logits(h, bank):
                        if h < HEADS:
                            r = 64 * (h % 2)
                            return mm(bank[:], q_b[r:r + 64, h // 2 * P:(h // 2 + 1) * P],
                                      big[r:r + 64, (G_K + h // 2) * S:(G_K + h // 2 + 1) * S], start=True, stop=True)
                        h -= HEADS
                        return mm(bank[:, 0:N_MEM], mq_b[:, h * P:(h + 1) * P], mk[:, h * N_MEM:(h + 1) * N_MEM], start=True, stop=True)

                    def values(h, pt):
                        if h < HEADS:
                            r = 64 * (h % 2)
                            for t in range(NT):
                                last = mm(pb[4][r:r + 64, h // 2 * P:(h // 2 + 1) * P], vtok[:, t * S + h * 64:t * S + (h + 1) * 64],
                                          pt[:, t * P:(t + 1) * P], start=(t == 0), stop=(t == NT - 1))
                            return last
                        h -= HEADS
                        for t in range(2):
                            last = mm(pb[5][:, h * P:(h + 1) * P], mv[:, t * S + h * P:t * S + (h + 1) * P],
                                      pt[:, t * P:(t + 1) * P], start=(t == 0), stop=(t == 1))
                        return last

                    heads((l * NT + b) * ATT, ATT, logits, values, lambda h: NT if h < HEADS else 2, lg, pT)
                pe.wait_ge(att_done, l * NT + NT)
                alone(pe)
                with pe.Fori(0, 3) as n:
                    for q in range(2):
                        for d in range(4):
                            c = (l * 3 + n) * 8 + 4 * q + d
                            u6 = 3 * (d // 2) + d % 2
                            j = 17 + 3 * q + u6 // 2
                            w = pair(j, l, n, 2)
                            pe.wait_ge(gate_free, c + 1)
                            for k in range(KC):
                                last = mm(pb[2 + d % 2][:], unit(w, u6 % 2, k), grp(xT, k), start=(k == 0), stop=(k == KC - 1))
                                if k == 0 and u6 % 2 == 0:
                                    last.then_inc(slot_free, 1)
                            last.then_inc(gate_ready, 1)
                            if d % 2:
                                ub = 3 * (d // 2) + 2
                                w = pair(17 + 3 * q + ub // 2, l, n, 2)
                                for e in range(2):
                                    pe.wait_ge(br_free, c + e)
                                    for k in range(4):
                                        last = mm(pb[4 + e][:], unit(w, ub % 2, e * 4 + k), grp(big, n * 4 + k), start=(k == 0), stop=(k == 3))
                                        if k == 0 and e == 0 and ub % 2 == 0:
                                            last.then_inc(slot_free, 1)
                                    last.then_inc(br_ready, 1)
                def route_tile(t):
                    pe.wait_ge(xT_ready, 2 * l * KC + 2 * (t + 1) + 1)
                    alone(pe)
                    for k in range(KC):
                        last = mm(pb[4][:, t * N_EXP:(t + 1) * N_EXP], xT[:, k * S + t * P:k * S + (t + 1) * P],
                                  w_router[:, k * N_EXP:(k + 1) * N_EXP], start=(k == 0), stop=(k == KC - 1))
                    return last

                pe.wait_ge(merged_ready, (l + 1) * 24)
                for n in range(2):
                    for j in range(2):
                        w = pair(35 + 2 * n + j, l)
                        for x in range(4 * NT):
                            t, k = (x // 4, x % 4) if j else (x % NT, x // NT)
                            last = mm(pb[4 * n + t][:], merged[:, (4 * j + k) * S + t * P:(4 * j + k) * S + (t + 1) * P],
                                      w[:, k * S:(k + 1) * S], start=(j == 0 and k == 0), stop=(j == 1 and k == 3))
                            if x == 0:
                                last.then_inc(slot_free, 1)
                            if j == 1 and k == 3:
                                last.then_inc(mix_ready, 1)
                                if n == 1 and t >= 1:
                                    transpose_tile(2 * l, t - 1)
                                if n == 1 and t >= 2:
                                    route_tile(t - 2)
                route_tile(NT - 2)
                transpose_tile(2 * l, NT - 1)
                route_tile(NT - 1).then_inc(sc_ready, 1)
                pe.wait_ge(pick_ready, l + 1)
                for t in range(NT):
                    for u in range(t + 1):
                        last = mm(pb[1][:, t * N_EXP:(t + 1) * N_EXP], tri if u == t else ones,
                                  r_pick[:, u * N_EXP:(u + 1) * N_EXP], start=(u == 0), stop=(u == t))
                for t in range(NT):
                    last = mm(pb[2][:, 0:N_EXP], ones, r_pick[:, t * N_EXP:(t + 1) * N_EXP], start=(t == 0), stop=(t == NT - 1))
                last.then_inc(rank_ready, 1)

                def transpose_xs(s, use):
                    pe.wait_ge(xs_loaded[s], 16 * (l * XS_OF[s] + use + 1))
                    for k in range(KC):
                        last = nc.tensor.transpose(pb[4 + k // 4][:, k % 4 * P:(k % 4 + 1) * P], xs[s][:, k * P:(k + 1) * P], identity)
                    last.then_inc(xs_tr, 1)

                def up(b, s, j0, i=0, per=1):
                    pe.wait_ge(xsT_ready, l * (N_BLK + 1) + b + 1)
                    for m in range(2):
                        for j in range(2):
                            w = pair(j0 + 2 * m + j, l, i, per)
                            for k in range(4):
                                c = 4 * j + k
                                last = mm(pb[m][:], xsT[s][:, c * P:(c + 1) * P], w[:, k * S:(k + 1) * S], start=(c == 0), stop=(c == KC - 1))
                                if k == 0:
                                    last.then_inc(slot_free, 1)
                        last.then_inc(up_ready, 1)

                def turn(b):
                    pe.wait_ge(hid_ready, l * N_BLK + b + 1 + 1)
                    for c in range(4):
                        last = nc.tensor.transpose(pb[6][:, c * P:(c + 1) * P], hid[:, c * P:(c + 1) * P], identity)
                    last.then_inc(ht_ready, 1)

                def down(b, j0, i=0, per=1):
                    pe.wait_ge(hT_ready, l * N_BLK + b + 1)
                    pe.wait_ge(y_copied, 2 * (l * N_BLK + b) + 1)
                    for j in range(2):
                        w = pair(j0 + j, l, i, per)
                        for k in range(4):
                            last = mm(pb[2 + j][:], hT[:, k * P:(k + 1) * P], w[:, k * S:(k + 1) * S], start=(k == 0), stop=(k == 3))
                            if k == 0:
                                last.then_inc(slot_free, 1)
                    last.then_inc(y_ready, 1)

                M0, per = LAYER_STREAM + UP_PAIRS, 2 * MOE_PAIRS // SLOTS
                transpose_xs(0, 0)
                up(0, 0, LAYER_STREAM)
                transpose_xs(1, 0)
                turn(0)
                with pe.Fori(0, N_BLK // 2) as i:
                    for s in range(2):
                        b = i * 2 + s + 1
                        up(b, 1 - s, M0 + s * MOE_PAIRS, i, per)
                        transpose_xs(s, i + 1)
                        down(b - 1, M0 + s * MOE_PAIRS + UP_PAIRS, i, per)
                        turn(b)
                down(N_BLK - 1, M0 + (N_BLK - 1) * MOE_PAIRS)
                for t in range(NT):
                    transpose_tile(2 * l + 1, t)

            def rms(n):
                for k in range(KC):
                    pe.wait_ge(sq_ready, n * KC + k + 1)
                    last = mm(pb[7][:], ones, sq2[k % 2], start=(k == 0), stop=(k == KC - 1))
                    last.then_inc(sq_used, 1)

            def feed_forward(n, j0):
                pe.wait_ge(xn_ready, 2 * n + 1)

                def half(w, f, s):
                    pe.wait_ge(ff_free, n * FC + f + 1)
                    for u in range(2):
                        for k in range(KC):
                            last = mm(pb[3 * u + s][:], unit(w, u, k), xn[:, k * S:(k + 1) * S], start=(k == 0), stop=(k == KC - 1))
                            if u == 0 and k == 0:
                                last.then_inc(slot_free, 1)
                    last.then_inc(ff_ready, 1)

                with pe.Fori(0, FC // 3) as i:
                    for s in range(3):
                        half(pair(j0 + s, None, i), i * 3 + s, s)
                half(pair(j0 + FC - 1), FC - 1, 0)
                pe.wait_ge(ff_free, (n + 1) * FC + 3)
                with pe.Fori(0, 4) as i:
                    for g in range(2):
                        d = n * KC + i * 2 + g
                        pe.wait_ge(dn_free, d + 1)
                        for c in range(FC):
                            u = 3 * g + c // KC
                            opens = c % KC == 0 and u % 2 == 0
                            if c == 0 or opens:
                                w = pair(j0 + FC + u // 2, None, i)
                            last = mm(pb[6 + g][:], unit(w, u % 2, c % KC), grp(big, c), start=(c == 0), stop=(c == FC - 1))
                            if opens:
                                last.then_inc(slot_free, 1)
                        last.then_inc(dn_ready, 1)
                pe.wait_ge(dn_free, (n + 1) * KC + 2)

            pe.wait_ge(xT_ready, 4 * KC + 1)
            pe.wait_ge(oh_loaded, 16)
            for c in range(2):
                last = mm(pb[c][0:HEADS, :], rel_b[:, :], rel_oh[:, c * S:(c + 1) * S], start=True, stop=True)
            last.then_inc(rel_ready, 1)
            rms(0)
            pe.wait_ge(rel_copied, 2)
            feed_forward(0, 0)
            rms(1)
            pe.wait_ge(xn_ready, 2)
            for g in range(N_H):
                linear(pair(34 + g // 2), g % 2, xn, DEPTH * LIN_LAYER + g, g % 2)
                c = g - 4
                if 0 <= c < N_NORM:
                    pe.wait_ge(nsq_ready, c + 1)
                    if c >= 4:
                        pe.wait_ge(nsum_used, c - 3)
                    mm(pb[2 + c % 4][:], ones if c < 8 else block_ones, nsq[c % 2], start=True, stop=True).then_inc(nsum_ready, 1)
            pe.wait_ge(lin_free, DEPTH * LIN_LAYER + N_H + 2)
            pe.wait_ge(nsum_used, N_NORM)
            for n in range(NCH):
                for r in range(2):
                    last = mm(pb[0][r * CH:(r + 1) * CH, n * 16:(n + 1) * 16], big[0:16, H_AB * S + n * CH:H_AB * S + (n + 1) * CH],
                              identity[0:16, 0:16], start=True, stop=True)
            last.then_inc(ab_tr, 1)
            for t in range(NT):
                for c in range(4):
                    last = nc.tensor.transpose(pb[4 + t][:, c * P:(c + 1) * P], big[:, (H_SV + c) * S + t * P:(H_SV + c) * S + (t + 1) * P], identity)
            last.then_inc(v2_tr, 1)
            pe.wait_ge(g_ready, 1)
            for r in range(2):
                h2 = slice(r * CH, (r + 1) * CH)
                last = mm(cut(pb[1][h2, 0:NCH * GH], GH), gtri[h2, :], cut(ga[h2, :], UN)[:, :, r * GH:(r + 1) * GH], start=True, stop=True)
            last.then_inc(gc_ready, 1)
            pe.wait_ge(gc_done, 1)
            pe.wait_ge(v2_ready, 1)
            pe.wait_ge(n_done, 2)
            pe.wait_ge(hank_loaded, 16)
            A0 = DEPTH * NT * ATT
            with pe.Fori(0, NT) as b:
                pe.wait_ge(staged, DEPTH * NT + b + 1)

                def logits2(h, bank):
                    r = 64 * (h % 2)
                    mm(bank[:], q2_b[r:r + 64, h // 2 * P:(h // 2 + 1) * P],
                       big[r:r + 64, (H_SK + h // 2) * S:(H_SK + h // 2 + 1) * S], start=True, stop=False)
                    return mm(bank[:], reverse, hank[:, bass.ds(h * 896 + (NT - 1) * P - b * P, S)], start=False, stop=True)

                def values2(h, pt):
                    r = 64 * (h % 2)
                    for t in range(NT):
                        last = mm(pb[4][r:r + 64, h // 2 * P:(h // 2 + 1) * P], v2[:, t * S + h * 64:t * S + (h + 1) * 64],
                                  pt[:, t * P:(t + 1) * P], start=(t == 0), stop=(t == NT - 1))
                    return last

                heads(A0 + b * HEADS, HEADS, logits2, values2, lambda h: NT, lg2, pT2)
            pe.wait_ge(att_done, DEPTH * NT + NT)
            UNITS = [(r, h) for r in range(2) for h in range(GH)]

            def blk(t, r, h, w=CH, c0=0):
                return t[r * CH:(r + 1) * CH, c0 + h * w:c0 + (h + 1) * w]

            def u64(t, r, h):
                u = r * GH + h
                return t[:, u * CH:(u + 1) * CH]

            def u128(t, r, h):
                u = r * GH + h
                return t[:, u * P:(u + 1) * P]

            def turn_chunk(n):
                pe.wait_ge(g_staged, n + 1)
                alone(pe)
                for bank, t in ((2, ks), (3, vs)):
                    for r, h in UNITS:
                        mm(blk(pb[bank], r, h, P), u64(t, r, h), identity, start=True, stop=True)

            def chunk_products(n):
                pe.wait_ge(g_diag, n + 1)
                alone(pe)
                for c0, t in ((0, ks), (LW, qs)):
                    for r, h in UNITS:
                        mm(blk(pb[0], r, h, CH, c0), u64(ks, r, h), u64(t, r, h), start=True, stop=True)
                for bank, t in ((4, dg), (1, db)):
                    for r in range(2):
                        mm(pb[bank][:, r * LW:(r + 1) * LW], half_ones[:, r * P:(r + 1) * P], t, start=True, stop=True)
                mm(pb[5][:, 0:LW], block_ones, dg, start=True, stop=True)
                mm(pb[5][:, LW:2 * LW], block_ones, db, start=True, stop=True).then_inc(g_rows, 1)

            def level(n, q, both):
                for g in range(2):
                    pe.wait_ge(g_tm, (n * LEVELS + q) * 2 + g + 1)
                    alone(pe)
                    for r in range(2):
                        for h in (2 * g, 2 * g + 1):
                            last = mm(blk(pb[g], r, h), blk(lbT, r, h), blk(Tm, r, h), start=True, stop=True)
                    last.then_inc(g_a, 1)
                for g in range(2):
                    pe.wait_ge(g_am, (n * (LEVELS - 1) + q) * 2 + g + 1)
                    alone(pe)
                    for r in range(2):
                        for h in (2 * g, 2 * g + 1):
                            if both:
                                mm(blk(pb[4 + g], r, h), blk(Mm, r, h), blk(Am, r, h), start=True, stop=True)
                            last = mm(blk(pb[4 + g], r, h, CH, LW), blk(Am, r, h), blk(Mm, r, h), start=True, stop=True)
                    last.then_inc(g_up, 1)

            def chunk(n, par, more):
                pe.wait_ge(g_mats, n + 1)
                alone(pe)
                for g in range(2):
                    for r in range(2):
                        for h in (2 * g, 2 * g + 1):
                            last = mm(blk(pb[4 + g], r, h), blk(lbT, r, h), id_pair[r * CH:(r + 1) * CH, :], start=True, stop=True)
                    last.then_inc(g_up, 1)
                with pe.Fori(0, LEVELS - 2) as q:
                    level(n, q, True)
                level(n, LEVELS - 2, False)
                pe.wait_ge(g_state, n + 1)
                alone(pe)
                if more:
                    turn_chunk(n + 1)
                pe.wait_ge(g_o, n + 1)
                alone(pe)
                for r, h in UNITS:
                    last = mm(blk(pb[6], r, h, P), u64(kbF, r, h), u128(st[par], r, h), start=True, stop=True)
                last.then_inc(g_r, 1)
                pe.wait_ge(g_tm, (n + 1) * LEVELS * 2)
                alone(pe)
                if more:
                    chunk_products(n + 1)
                pe.wait_ge(g_rsub, n + 1)
                alone(pe)
                for r, h in UNITS:
                    last = mm(blk(pb[7], r, h, P), blk(Mm, r, h), blk(resid, r, h, P), start=True, stop=True)
                last.then_inc(g_vnm, 1)
                pe.wait_ge(g_vn, n + 1)
                alone(pe)
                for r, h in UNITS:
                    o = pb[6 + r][:, h * CH:(h + 1) * CH]
                    mm(o, u128(st[par], r, h), u64(qg[par], r, h), start=True, stop=False)
                    mm(o, blk(vn, r, h, P), blk(inT[par], r, h), start=False, stop=True)
                if more:
                    pe.wait_ge(g_kv_used, n + 2)
                    alone(pe)
                for r, h in UNITS:
                    last = mm(pb[2 + r][:, h * P:(h + 1) * P], blk(kdec[par], r, h, P), blk(vn, r, h, P), start=True, stop=True)
                last.then_inc(g_out, 1)

            turn_chunk(0)
            chunk_products(0)
            with pe.Fori(0, NCH // 2 - 1) as i:
                for par in range(2):
                    chunk(i * 2 + par, par, True)
            chunk(NCH - 2, 0, True)
            chunk(NCH - 1, 1, False)
            for h in range(GH):
                pe.wait_ge(o_sq, h + 1)
                mm(pb[2 + h][:], ones, sq2[h % 2], start=True, stop=True).then_inc(o_ss, 1)
            def project(first, half, groups):
                for d in groups:
                    w = pair(49 + 2 * half + d // 4)
                    for k in range(4):
                        last = mm(pb[OUT_BANKS[d]][:], w[:, (d % 4 * 4 + k) * P:(d % 4 * 4 + k + 1) * P], grp(cat, 4 * (1 - half) + k),
                                  start=(first and k == 0), stop=(not first and k == 3))
                        if k == 0 and d % 4 == 0:
                            last.then_inc(slot_free, 1)
                    if not first:
                        last.then_inc(lin_ready, 1)

            pe.wait_ge(g_o, NCH + 1)
            project(True, 0, range(4))
            pe.wait_ge(o_var, 1)
            project(True, 0, range(4, 8))
            pe.wait_ge(o_done, 1)
            project(False, 1, range(8))
            pe.wait_ge(lin_free, DEPTH * LIN_LAYER + N_H + KC + 2)
            rms(2)
            feed_forward(1, 53)
            rms(3)

        @block.scalar
        def _(act):
            fn = nc.scalar.activation

            def heads(n0, count, width, scale, buf_p, buf_pT):
                for step in range(count + 2):
                    if step < count:
                        h = step
                        act.wait_ge(lg_masked, n0 + h + 1)
                        fn(buf_p[h % 3][:, 0:width(h)], buf_p[h % 3][:, 0:width(h)], ACT.Exp, scale=scale(h),
                           bias=stat[:, 8 + h % 3:9 + h % 3], accum_out=stat[:, 16 + h % 3:17 + h % 3]).then_inc(exp_done, 1)
                    if step >= 2:
                        h = step - 2
                        act.wait_ge(tr_ready, n0 + h + 1)
                        if h >= 2:
                            act.wait_ge(pv_ready, n0 + h - 1)
                        fn(buf_pT[h % 2][:, 0:width(h)], pb[2 + h % 2][:, 0:width(h)], ACT.Copy).then_inc(pT_ready, 1)

            def norm_rows(m):
                for t in range(NT + 1):
                    if t < NT:
                        x = grp(xtok, t, 1, D)
                        act.wait_ge(var_ready, m * NT + t + 1)
                        alone(act)
                        fn(ln_mv[:, 12 + t:13 + t], ln_mv[:, 8 + t:9 + t], ACT.Sqrt).then_inc(std_ready, 1)
                        act.wait_ge(shift_ready, m * NT + t + 1)
                        alone(act)
                        fn(x, x, ACT.Identity, scale=ln_mv[:, 8 + t:9 + t], bias=ln_mv[:, 16 + t:17 + t]).then_inc(normed, 1)
                    if t >= 1:
                        act.wait_ge(xtr_ready, m * NT + t)
                        alone(act)
                        for k in range(KC):
                            last = fn(xT[:, k * S + (t - 1) * P:k * S + t * P], pb[2 * ((t - 1) % 2) + k // 4][:, k % 4 * P:(k % 4 + 1) * P],
                                      ACT.Identity, scale=ln_T[:, bass.ds(m * 2 * KC + k, 1)], bias=ln_T[:, bass.ds(m * 2 * KC + KC + k, 1)])
                            if k % 4 == 3:
                                last.then_inc(xT_ready, 1)

            for dst, src in ROPE_CONSTS:
                act.dma_start(dst, src).then_inc(rope_loaded, 16)
            for dst, src in CONSTS:
                act.dma_start(dst, src).then_inc(loaded, 16)
            act.wait_ge(rope_arg, 1)
            fn(sin_t[:, :], relu2[0], ACT.Sin)
            fn(cos_t[:, :], relu2[1], ACT.Sin).then_inc(rope_sin, 1)

            act.wait_ge(loaded, N_CONST)
            with act.Fori(0, DEPTH) as l:
                for n in range(MEM_GROUPS):
                    act.wait_ge(lin_ready, l * LIN_LAYER + n + 1)
                    dst = mk if n < 4 else mvf
                    fn(dst[:, n % 4 * N_MEM:(n % 4 + 1) * N_MEM], pb[n % 2][:, 0:N_MEM], ACT.Copy).then_inc(lin_free, 1)
                L0 = l * LIN_LAYER + MEM_GROUPS
                act.wait_ge(tok_done, 2 * l + 1)
                alone(act)
                for p in range(N_G):
                    act.wait_ge(lin_ready, L0 + p + 1)
                    fn(grp(big, ORDER[p]), pb[p % 2][:], ACT.Identity, bias=bias_p[:, bass.ds(l * N_G + ORDER[p], 1)]).then_inc(lin_free, 1)
                    if p == AT_MV:
                        act.wait_ge(vt_ready, 3 * l + 1)
                        alone(act)
                        for t in range(2):
                            last = fn(mv[:, t * S:(t + 1) * S], pb[6 + t][:], ACT.Copy)
                        last.then_inc(vt_copied, 1)
                    if p == AT_IW:
                        act.wait_ge(vt_ready, 3 * l + 2)
                        fn(iw_tok[:, :], pb[6][:, 0:NT * 8], ACT.Copy, scale=float(HEADS ** -0.5 * HEAD_DIM ** -0.5)).then_inc(vt_copied, 1)
                    if p + 1 in AT_SCORE:
                        b = AT_SCORE[p + 1]
                        act.wait_ge(rot_used, l * N_ROT + ROT_IDX)
                        if b > 1:
                            act.wait_ge(idx_ready, (l * N_TOP + b - 1) * HEADS)
                        alone(act)
                        fn(cut(iq_b, P), cut(grp(big, G_IQ, 4), S)[:, :, b * P:(b + 1) * P], ACT.Copy).then_inc(iq_staged, 1)
                    if p in AT_SCORE:
                        for h in range(HEADS):
                            n = (l * N_TOP + AT_SCORE[p] - 1) * HEADS + h
                            act.wait_ge(idx_ready, n + 1)
                            if h >= 2 or AT_SCORE[p] > 1:
                                act.wait_ge(idx_used, n - 1)
                            alone(act)
                            fn(relu2[h % 2], pb[6 + h % 2][:], ACT.Relu).then_inc(idx_copied, 1)
                    if p == AT_VT:
                        act.wait_ge(vt_ready, 3 * l + 3)
                        alone(act)
                        for t in range(NT):
                            last = fn(vtok[:, t * S:(t + 1) * S], pb[4 + t][:], ACT.Copy)
                        last.then_inc(vt_copied, 1)
                for g in range(4):
                    act.wait_ge(pool_mixed, l * 4 + g + 1)
                    last = fn(grp(big, G_POOL + g), pb[4 + g][:], ACT.Copy, scale=pool_scale[:, bass.ds(l * 4 + g, 1)])
                last.then_inc(pool_done, 1)
                act.drain()
                act.wait_ge(masks_ready, (l + 1) * N_TOP)
                alone(act)
                with act.Fori(0, NT) as b:
                    fn(maskb, adm[:, bass.ds(b * S, S)], ACT.Copy)
                    for dst, g in ((q_b, G_Q), (mq_b, G_MQ)):
                        last = fn(cut(dst, P), cut(grp(big, g, 4), S)[:, :, bass.ds(b * P, P)], ACT.Copy)
                    last.then_inc(staged, 1)
                    heads((l * NT + b) * ATT, ATT, lambda h: S if h < HEADS else N_MEM,
                          lambda h: HEAD_DIM ** -0.5 if h < HEADS else MEM_DIM ** -0.5, lg, pT)
                    act.wait_ge(pv_ready, (l * NT + b + 1) * ATT)
                    alone(act)
                    fn(cut(grp(big, G_Q, 4), S)[:, :, bass.ds(b * P, P)], cut(pb[4][:], P), ACT.Copy)
                    fn(cut(grp(big, G_MQ, 4), S)[:, :, bass.ds(b * P, P)], cut(pb[5][:], P), ACT.Copy).then_inc(att_done, 1)
                with act.Fori(0, 12) as i:
                    for u in range(2):
                        c = l * 24 + i * 2 + u
                        act.wait_ge(gate_ready, c + 1)
                        act.wait_ge(br_free, c + 1)
                        fn(relu2[u], pb[2 + u][:], ACT.Sigmoid, bias=bias_g[:, bass.ds(c, 1)]).then_inc(gate_free, 1)
                norm_rows(2 * l)
                act.wait_ge(sc_ready, l + 1)
                fn(r_score, pb[4][:, 0:NT * N_EXP], ACT.Sigmoid).then_inc(sig_ready, 1)

                def copy_xsT(b, s):
                    act.wait_ge(xs_tr, l * (N_BLK + 1) + b + 1)
                    for k in range(2):
                        last = fn(xsT[s][:, k * S:(k + 1) * S], pb[4 + k][:], ACT.Copy)
                    last.then_inc(xsT_ready, 1)

                def gate_half(b):
                    act.wait_ge(up_ready, 2 * (l * N_BLK + b) + 1)
                    act.wait_ge(hid_ready, l * N_BLK + b + 1)
                    fn(sil, pb[0][:], ACT.Silu).then_inc(sil_ready, 1)

                def copy_hT(b):
                    act.wait_ge(ht_ready, l * N_BLK + b + 1 + 1)
                    fn(hT, pb[6][:], ACT.Copy).then_inc(hT_ready, 1)

                def copy_y(b, s, use):
                    act.wait_ge(y_ready, l * N_BLK + b + 1)
                    act.wait_ge(y_stored[s], 16 * (l * YS_OF[s] + use) + 16)
                    fn(ysb[s][:, 0:S], pb[2][:], ACT.Copy).then_inc(y_copied, 1)

                copy_xsT(0, 0)
                gate_half(0)
                copy_xsT(1, 1)
                copy_hT(0)
                with act.Fori(0, N_BLK // 2) as i:
                    for s in range(2):
                        b = i * 2 + s + 1
                        gate_half(b)
                        copy_xsT(b + 1, s)
                        copy_y(b - 1, s, i)
                        copy_hT(b)
                copy_y(N_BLK - 1, 0, N_BLK // 2)
                norm_rows(2 * l + 1)

            def rms(n):
                act.drain()
                for k in range(KC):
                    if k >= 2:
                        act.wait_ge(sq_used, n * KC + k - 1)
                    fn(sq2[k % 2], grp(xT, k), ACT.Square).then_inc(sq_ready, 1)
                act.wait_ge(rvar, n + 1)
                fn(rs, rs, ACT.Sqrt).then_inc(rstd, 1)

            def feed_forward(n):
                def half(f, s):
                    act.wait_ge(ff_ready, n * FC + f + 1)
                    fn(sgl[s], pb[s][:], ACT.Silu).then_inc(ff_silu, 1)

                with act.Fori(0, FC // 3) as i:
                    for s in range(3):
                        half(i * 3 + s, s)
                half(FC - 1, 0)

            act.wait_ge(rel_ready, 1)
            act.wait_ge(xT_ready, 4 * KC + 1)
            for c in range(2):
                fn(rel_row[:, c * S:(c + 1) * S], pb[c][0:HEADS, :], ACT.Copy).then_inc(rel_copied, 1)
            rms(0)
            feed_forward(0)
            act.wait_ge(dn_free, KC + 2)
            rms(1)
            for g in range(N_H):
                act.wait_ge(lin_ready, DEPTH * LIN_LAYER + g + 1)
                fn(grp(big, g), pb[g % 2][:], ACT.Copy).then_inc(lin_free, 1)
                if g - 2 in CONV_GROUPS:
                    c = CONV_GROUPS.index(g - 2)
                    act.wait_ge(conv_ready, c + 1)
                    fn(grp(big, g - 2), ctmp[c % 2], ACT.Silu).then_inc(conv_silu, 1)
                c = g - 3
                if 0 <= c < N_NORM:
                    act.drain()
                    if c >= 2:
                        act.wait_ge(nsum_ready, c - 1)
                    fn(nsq[c % 2], grp(big, c), ACT.Square).then_inc(nsq_ready, 1)
                if g in (13, 21):
                    n = (g - 13) // 8
                    act.wait_ge(nsum_used, (n + 1) * 8)
                    fn(nrm, nrm, ACT.Sqrt).then_inc(nstd, 1)
            act.drain()
            act.wait_ge(ab_ready, 1)
            fn(gbeta[:, :], gbeta[:, :], ACT.Sigmoid)
            fn(ga[:, :], ga[:, :], ACT.Exp, scale=-1.0)
            act.drain()
            fn(ga[:, :], ga[:, :], ACT.Ln, bias=1.0)
            fn(alog[:, :], alog[:, :], ACT.Exp).then_inc(sp_ready, 1)
            act.wait_ge(v2_tr, 1)
            for t in range(NT):
                last = fn(v2[:, t * S:(t + 1) * S], pb[4 + t][:], ACT.Copy)
            last.then_inc(v2_ready, 1)
            act.wait_ge(n_done, 2)
            act.wait_ge(lnw_loaded, 16)
            A0 = DEPTH * NT * ATT
            with act.Fori(0, NT) as b:
                fn(lnw_b, lnw[:, bass.ds(b * S, S)], ACT.Copy)
                fn(cut(q2_b, P), cut(grp(big, H_SQ, 4), S)[:, :, bass.ds(b * P, P)], ACT.Copy).then_inc(staged, 1)
                heads(A0 + b * HEADS, HEADS, lambda h: S, lambda h: 1.0, lg2, pT2)
                act.wait_ge(pv_ready, A0 + (b + 1) * HEADS)
                alone(act)
                fn(cut(cat[:, 4 * S:8 * S], S)[:, :, bass.ds(b * P, P)], cut(pb[4][:], P), ACT.Copy).then_inc(att_done, 1)

            def back(n):
                return (NCH - 1) * CH - n * CH

            def place(n, r):
                at = n * CH if r == 0 else back(n)
                return slice(at, at + CH) if isinstance(at, int) else bass.ds(at, CH)

            def stage(n):
                for dst, g in ((ks, H_K), (qs, H_Q), (vs, H_V)):
                    for r in range(2):
                        last = fn(cut(dst, CH)[:, r * GH:(r + 1) * GH, :], cut(grp(big, g, 4), S)[:, :, place(n, r)], ACT.Copy)
                last.then_inc(g_staged, 1)

            def exps(n, par):
                act.wait_ge(g_rows, n + 1)
                alone(act)
                fn(eg, pb[4][:], ACT.Exp)
                fn(gl[:, 0:GH].unsqueeze(2), cut(pb[4][:], CH)[:, 0:GH, CH - 1:CH], ACT.Copy)
                fn(gl[:, GH:UN].unsqueeze(2), cut(pb[4][:], CH)[:, GH:UN, 0:1], ACT.Copy)
                act.drain()
                fn(egl[par][:, :], gl[:, :], ACT.Exp).then_inc(g_eg, 1)

            def decays(n):
                act.wait_ge(g_diff, n + 1)
                alone(act)
                fn(dT, dT, ACT.Exp)
                fn(dfac[:, :], dfac[:, :], ACT.Exp).then_inc(g_dexp, 1)

            def chunk(n, par, more):
                if more:
                    act.wait_ge(g_mats, n + 1)
                    alone(act)
                    stage(n + 1)
                with act.Fori(0, LEVELS - 1) as q:
                    for g in range(2):
                        act.wait_ge(g_a, (n * (LEVELS - 1) + q) * 2 + g + 1)
                        alone(act)
                        half = slice(g * LW // 2, (g + 1) * LW // 2)
                        fn(Am[:, half], pb[g][:, half], ACT.Copy).then_inc(g_am, 1)
                if more:
                    exps(n + 1, 1 - par)
                act.wait_ge(g_vnm, n + 1)
                alone(act)
                fn(vn, pb[7][:], ACT.Copy).then_inc(g_vn, 1)
                if more:
                    decays(n + 1)
                act.wait_ge(g_out, n + 1)
                alone(act)
                fn(cut(of, S)[:, :, place(n, 0)], cut(pb[6][:, 0:LW], CH), ACT.Copy)
                fn(cut(ob, S)[:, :, place(n, 1)], cut(pb[7][:, 0:LW], CH), ACT.Copy).then_inc(g_o, 1)

            stage(0)
            exps(0, 0)
            decays(0)
            fn(grp(big, H_Z, 4), grp(big, H_Z, 4), ACT.Silu)
            with act.Fori(0, NCH // 2 - 1) as i:
                for par in range(2):
                    chunk(i * 2 + par, par, True)
            chunk(NCH - 2, 0, True)
            chunk(NCH - 1, 1, False)
            act.wait_ge(o_sum, 1)
            for h in range(GH):
                if h >= 2:
                    act.wait_ge(o_ss, h - 1)
                fn(sq2[h % 2], grp(cat, h), ACT.Square).then_inc(o_sq, 1)
            act.wait_ge(o_var, 1)
            fn(ob, ob, ACT.Sqrt).then_inc(o_std, 1)
            act.wait_ge(lin_free, DEPTH * LIN_LAYER + N_H + KC + 2)
            rms(2)
            feed_forward(1)
            act.wait_ge(dn_free, 2 * KC + 2)
            rms(3)

        @block.vector
        def _(dve):
            v = nc.vector

            def heads(n0, count, prepare, width, buf_p):
                for step in range(count + 1):
                    if step < count:
                        h = step
                        dve.wait_ge(lg_ready, n0 + h + 1)
                        if h >= 3:
                            dve.wait_ge(tr_ready, n0 + h - 2)
                        alone(dve)
                        prepare(h, stat[:, h % 3:h % 3 + 1], stat[:, 8 + h % 3:9 + h % 3]).then_inc(lg_masked, 1)
                    if step >= 1:
                        h = step - 1
                        r = stat[:, 24 + h % 3:25 + h % 3]
                        dve.wait_ge(exp_done, n0 + h + 1)
                        v.reciprocal(r, stat[:, 16 + h % 3:17 + h % 3])
                        dve.drain()
                        v.tensor_scalar(buf_p[h % 3][:, 0:width(h)], buf_p[h % 3][:, 0:width(h)], r, None, ALU.mult).then_inc(p_ready, 1)

            def row_stats(t, c):
                v.bn_stats(ln_st[:, t * 12 + c * 6:t * 12 + (c + 1) * 6], xtok[:, t * D + c * S:t * D + (c + 1) * S])

            def row_norm(m, t):
                dve.drain()
                v.bn_aggr(ln_mv[:, 2 * t:2 * t + 2], ln_st[:, t * 12:(t + 1) * 12])
                dve.drain()
                r = ln_mv[:, 8 + t:9 + t]
                v.tensor_scalar(r, ln_mv[:, 2 * t + 1:2 * t + 2], LN_EPS, None, ALU.add).then_inc(var_ready, 1)
                dve.wait_ge(std_ready, m * NT + t + 1)
                alone(dve)
                v.reciprocal(r, ln_mv[:, 12 + t:13 + t])
                dve.drain()
                v.tensor_scalar(ln_mv[:, 16 + t:17 + t], ln_mv[:, 2 * t:2 * t + 1], r, -1.0, ALU.mult, ALU.mult).then_inc(shift_ready, 1)

            dve.sem_inc(tok_done, 1)
            dve.wait_ge(rope_loaded, 16 * len(ROPE_CONSTS))
            ang, turns = score, maskb
            v.tensor_copy(ang, work.bitcast(I32))
            dve.drain()
            v.tensor_scalar(ang, ang, inv_freq[:, 0:1], None, ALU.mult)
            dve.drain()
            for c in range(2):
                v.tensor_scalar(turns, ang, 1.0 / TWO_PI, 0.25 * c, ALU.mult, ALU.add)
                dve.drain()
                v.tensor_scalar(turns, turns, ROUND, ROUND, ALU.add, ALU.subtract)
                dve.drain()
                r = relu2[c]
                v.scalar_tensor_tensor(out=r, in0=turns, scalar=-PI_A, in1=ang, op0=ALU.mult, op1=ALU.add)
                for part in (PI_B, PI_C):
                    dve.drain()
                    v.scalar_tensor_tensor(out=r, in0=turns, scalar=-part, in1=r, op0=ALU.mult, op1=ALU.add)
                dve.drain()
                if c:
                    v.tensor_scalar(r, r, TWO_PI / 4, None, ALU.add)
                    dve.drain()
                last = v.tensor_scalar(r, r, 3.1415925, -3.1415925, ALU.min, ALU.max)
            last.then_inc(rope_arg, 1)
            dve.wait_ge(rope_sin, 1)
            dve.wait_ge(loaded, N_CONST)

            with dve.Fori(0, DEPTH) as l:
                def rotate(n):
                    dve.wait_ge(rot_ready, l * N_ROT + n + 1)
                    alone(dve)
                    x = grp(big, ROT_GROUPS[n])
                    v.tensor_tensor(tmp[0], pb[2 + n % 4][:], sin_t[:, :], ALU.mult)
                    v.tensor_tensor(tmp[1], x, cos_t[:, :], ALU.mult)
                    dve.drain()
                    v.tensor_tensor(x, tmp[0], tmp[1], ALU.add).then_inc(rot_used, 1)
                    dve.drain()

                for n in range(ROT_IDX):
                    rotate(n)
                dve.wait_ge(adm_loaded, 16 * l + 16)
                dve.wait_ge(vt_copied, 3 * l + 2)
                alone(dve)
                for b in range(1, NT):
                    admb = adm[:, b * S:(b + 1) * S]
                    for h in range(HEADS):
                        dve.wait_ge(idx_copied, (l * N_TOP + b - 1) * HEADS + h + 1)
                        alone(dve)
                        v.scalar_tensor_tensor(out=score, in0=relu2[h % 2], scalar=iw_tok[:, b * 8 + h:b * 8 + h + 1],
                                               in1=score if h else admb, op0=ALU.mult, op1=ALU.add).then_inc(idx_used, 1)
                        dve.drain()
                    for r in range(N_SEL // 8):
                        v.max(top8[:, :], work if r else score)
                        dve.drain()
                        v.match_replace(out=work, in_to_replace=top8[:, :], in_values=work if r else score, imm_value=LOWEST)
                        dve.drain()
                    v.tensor_tensor(work, work, score, ALU.not_equal)
                    dve.drain()
                    v.tensor_scalar(work, work, 1.0, -BIG_NEG, ALU.subtract, ALU.mult)
                    dve.drain()
                    v.tensor_tensor(admb, work, admb, ALU.add).then_inc(masks_ready, 1)
                    dve.drain()
                    if b < 3:
                        for n in range(ROT_IDX + 4 * (b - 1), ROT_IDX + 4 * b):
                            rotate(n)
                dve.wait_ge(lin_free, l * LIN_LAYER + MEM_GROUPS + ORDER.index(G_POOL + 3) + 1 + 2)
                alone(dve)
                for g in range(4):
                    x, src = grp(big, G_POOL + g), grp(big, G_POOL + g)
                    w = 1
                    for s in range(g + 1):
                        dst = tmp[s % 2]
                        v.tensor_tensor(dst[:, w:S], src[:, w:S], src[:, 0:S - w], ALU.add)
                        v.tensor_copy(dst[:, 0:w], src[:, 0:w])
                        dve.drain()
                        src, w = dst, 2 * w
                    v.tensor_tensor(src[:, 0:16], src[:, 0:16], pool_rec[:, g * 16:(g + 1) * 16], ALU.mult)
                    dve.drain()
                    v.tensor_tensor(work[:, 0:16], src[:, 0:16], x[:, 0:16], ALU.subtract)
                    v.scalar_tensor_tensor(out=x[:, 16:S], in0=src[:, 16:S], scalar=1.0 / w, in1=x[:, 16:S], op0=ALU.mult, op1=ALU.subtract)
                    dve.drain()
                    v.tensor_copy(x[:, 0:16], work[:, 0:16]).then_inc(pool_in, 1)
                    dve.drain()
                with dve.Fori(0, NT) as b:
                    dve.wait_ge(staged, l * NT + b + 1)
                    def prepare(h, top, neg):
                        if h < HEADS:
                            v.tensor_tensor_reduce(out=lg[h % 3], in0=pb[LOGIT_BANKS[h % 3]][:], in1=maskb, scale=1.0, scalar=LOWEST,
                                                   op0=ALU.add, op1=ALU.max, accum_out=top)
                            scale = HEAD_DIM ** -0.5
                        else:
                            v.tensor_copy(lg[h % 3][:, 0:N_MEM], pb[LOGIT_BANKS[h % 3]][:, 0:N_MEM])
                            v.tensor_reduce(top, pb[LOGIT_BANKS[h % 3]][:, 0:N_MEM], AX.X, ALU.max)
                            scale = MEM_DIM ** -0.5
                        dve.drain()
                        return v.tensor_scalar(neg, top, -scale, None, ALU.mult)

                    heads((l * NT + b) * ATT, ATT, prepare, lambda h: S if h < HEADS else N_MEM, lg)
                dve.wait_ge(att_done, l * NT + NT)
                v.memset(merged, 0.0)
                dve.drain()
                with dve.Fori(0, 3) as n:
                    for d in range(8):
                        c = (l * 3 + n) * 8 + d
                        dve.wait_ge(br_ready, c + 1)
                        dve.wait_ge(gate_free, c + 3)
                        v.tensor_tensor(tmp[d % 2], pb[4 + d % 2][:], relu2[d % 2], ALU.mult).then_inc(br_free, 1)
                        dve.drain()
                        m = merged[:, d * S:(d + 1) * S]
                        v.tensor_tensor(m, m, tmp[d % 2], ALU.add).then_inc(merged_ready, 1)
                    dve.drain()
                dve.wait_ge(xtok_loaded, 16)
                dve.wait_ge(tok_done, 2 * l + 1)
                alone(dve)
                for n in range(2):
                    for t in range(NT):
                        dve.wait_ge(mix_ready, l * 2 * NT + n * NT + t + 1)
                        alone(dve)
                        x = xtok[:, t * D + n * S:t * D + (n + 1) * S]
                        v.scalar_tensor_tensor(out=x, in0=x, scalar=DN_ALPHA, in1=pb[4 * n + t][:], op0=ALU.mult, op1=ALU.add)
                        dve.drain()
                        row_stats(t, n)
                        if n == 1:
                            row_norm(2 * l, t)
                dve.wait_ge(sig_ready, l + 1)
                r4 = lambda t: t.rearrange("p (t g e) -> p (t g) e", t=NT, e=PER_GROUP)
                v.tensor_tensor(cut(r_biased, N_EXP), cut(r_score, N_EXP), r_bias[:, :].unsqueeze(1).to_broadcast([P, NT, N_EXP]), ALU.add)
                dve.drain()

                def ranks(rank, val, sets, c):
                    n4 = [P, sets, PER_GROUP, PER_GROUP]
                    cmp = lambda t: t[:, 0:sets * 16].rearrange("p (s x y) -> p s x y", x=PER_GROUP, y=PER_GROUP)
                    one, other = val.unsqueeze(3).to_broadcast(n4), val.unsqueeze(2).to_broadcast(n4)
                    v.tensor_tensor(cmp(c[0]), other, one, ALU.is_gt)
                    v.tensor_tensor(cmp(c[1]), other, one, ALU.is_equal)
                    dve.drain()
                    v.tensor_tensor(cut(c[1][:, 0:sets * 16], 16), cut(c[1][:, 0:sets * 16], 16), before[:, :].unsqueeze(1).to_broadcast([P, sets, 16]), ALU.mult)
                    dve.drain()
                    v.tensor_tensor(c[0][:, 0:sets * 16], c[0][:, 0:sets * 16], c[1][:, 0:sets * 16], ALU.add)
                    dve.drain()
                    v.tensor_reduce(rank, c[0][:, 0:sets * 16].rearrange("p (s x) -> p s x", x=PER_GROUP), AX.X, ALU.add)
                    dve.drain()

                ranks(r_rank, r4(r_biased), NT * GROUPS, r_cmp)
                v.tensor_scalar(r_pick, r_rank, 2.0, None, ALU.is_lt)
                dve.drain()
                v.tensor_tensor(r_t, r_pick, r_biased, ALU.mult)
                dve.drain()
                v.tensor_reduce(r_gsum, r4(r_t), AX.X, ALU.add)
                dve.drain()
                ranks(r_grank, cut(r_gsum, GROUPS), NT, r_cmp)
                v.tensor_scalar(r_gsum, r_grank, 0.0, None, ALU.is_equal)
                dve.drain()
                best = r_gsum.unsqueeze(2).to_broadcast([P, NT * GROUPS, PER_GROUP])
                v.tensor_tensor(r4(r_pick), r4(r_pick), best, ALU.mult).then_inc(pick_ready, 1)
                for k in range(2):
                    v.tensor_scalar(r_one[k], r_rank, float(k), None, ALU.is_equal)
                dve.drain()
                for k in range(2):
                    v.tensor_tensor(r4(r_one[k]), r4(r_one[k]), best, ALU.mult)
                dve.wait_ge(rank_ready, l + 1)
                v.tensor_scalar(r_end, pb[2][:, 0:N_EXP], 1.0 / MOE_BLOCK, None, ALU.mult)
                dve.drain()
                full = S // MOE_BLOCK
                some = cut(r_cmp[0][:, 0:N_EXP * full], full)
                v.tensor_tensor(some, r_end.unsqueeze(2).to_broadcast([P, N_EXP, full]), blk_iota[:, 0:full].unsqueeze(1).to_broadcast([P, N_EXP, full]), ALU.is_gt)
                v.memset(r_grank, 1.0)
                dve.drain()
                v.tensor_reduce(r_nblk, some, AX.X, ALU.add)
                dve.drain()
                v.tensor_tensor_scan(r_end, r_grank, r_nblk, 0.0, op0=ALU.mult, op1=ALU.add)
                dve.drain()
                v.tensor_tensor(r_nblk, r_end, r_nblk, ALU.subtract)
                dve.drain()
                v.tensor_scalar(r_nblk, r_nblk, float(MOE_BLOCK), None, ALU.mult)
                dve.drain()
                v.tensor_tensor(cut(r_t, N_EXP), cut(pb[1][:, 0:NT * N_EXP], N_EXP), r_nblk.unsqueeze(1).to_broadcast([P, NT, N_EXP]), ALU.add)
                dve.drain()
                for k in range(2):
                    v.tensor_tensor(r_u[k], r_one[k], r_t, ALU.mult)
                dve.drain()
                for k in range(2):
                    v.tensor_reduce(r_dest[:, k * NT:(k + 1) * NT], cut(r_u[k], N_EXP), AX.X, ALU.add)
                dve.drain()
                v.tensor_copy(dest[:, :], r_dest).then_inc(dest_ready, 1)
                ends = cut(r_cmp[1][:, 0:N_BLK * N_EXP], N_EXP)
                v.tensor_tensor(ends, blk_iota[:, :].unsqueeze(2).to_broadcast([P, N_BLK, N_EXP]), r_end.unsqueeze(1).to_broadcast([P, N_BLK, N_EXP]), ALU.is_ge)
                dve.drain()
                v.tensor_reduce(r_blk, ends, AX.X, ALU.add)
                dve.drain()
                v.tensor_scalar(r_blk, r_blk, float(N_EXP - 1), None, ALU.min)
                dve.drain()
                v.tensor_copy(blk_e[:, :], r_blk).then_inc(route_ready, 1)
                v.tensor_tensor(r_t, r_pick, r_score, ALU.mult)
                for k in range(2):
                    v.tensor_tensor(r_u[k], r_one[k], r_score, ALU.mult)
                dve.drain()
                v.tensor_reduce(r_sum, cut(r_t, N_EXP), AX.X, ALU.add)
                for k in range(2):
                    v.tensor_reduce(gate2[:, k * NT:(k + 1) * NT], cut(r_u[k], N_EXP), AX.X, ALU.add)
                dve.drain()
                v.reciprocal(r_sum, r_sum)
                dve.drain()
                for k in range(2):
                    v.tensor_tensor(gate2[:, k * NT:(k + 1) * NT], gate2[:, k * NT:(k + 1) * NT], r_sum, ALU.mult)
                dve.wait_ge(tok_done, 2 * l + 2)
                dve.wait_ge(xs_scattered, l * 128 + 128)
                alone(dve)
                for t in range(NT):
                    x = grp(xtok, t, 1, D)
                    v.tensor_scalar(x, x, DN_ALPHA, None, ALU.mult)
                def hidden(b):
                    dve.wait_ge(up_ready, 2 * (l * N_BLK + b) + 2)
                    dve.wait_ge(sil_ready, l * N_BLK + b + 1)
                    dve.wait_ge(ht_ready, l * N_BLK + b + 1)
                    v.tensor_tensor(hid, pb[1][:], sil, ALU.mult).then_inc(hid_ready, 1)

                def copy_y(b, s, use):
                    dve.wait_ge(y_ready, l * N_BLK + b + 1)
                    dve.wait_ge(y_stored[s], 16 * (l * YS_OF[s] + use) + 16)
                    v.tensor_copy(ysb[s][:, S:D], pb[3][:]).then_inc(y_copied, 1)

                hidden(0)
                with dve.Fori(0, N_BLK // 2) as i:
                    for s in range(2):
                        hidden(i * 2 + s + 1)
                        copy_y(i * 2 + s, s, i)
                copy_y(N_BLK - 1, 0, N_BLK // 2)
                for t in range(NT):
                    dve.wait_ge(y_back[t % 2], 64 * l + 32 * (t // 2 + 1))
                    x = grp(xtok, t, 1, D)
                    for k in range(2):
                        last = v.scalar_tensor_tensor(out=x, in0=yg[t % 2][k], scalar=gate2[:, k * NT + t:k * NT + t + 1], in1=x, op0=ALU.mult, op1=ALU.add)
                        if k == 1:
                            last.then_inc(yg_used, 1)
                        dve.drain()
                    for c in range(2):
                        row_stats(t, c)
                    row_norm(2 * l + 1, t)

            def rms(n):
                dve.wait_ge(sq_used, (n + 1) * KC)
                v.tensor_scalar(rs, pb[7][:], 1.0 / D, EPS, ALU.mult, ALU.add).then_inc(rvar, 1)
                dve.wait_ge(rstd, n + 1)
                v.reciprocal(rs, rs)
                dve.drain()
                for k in range(KC):
                    last = v.scalar_tensor_tensor(out=grp(xtok, k), in0=grp(xT, k), scalar=normw[:, n * KC + k:n * KC + k + 1], in1=rs, op0=ALU.mult, op1=ALU.mult)
                last.then_inc(xn_ready, 1)

            def feed_forward(n):
                def half(f, s):
                    dve.wait_ge(ff_silu, n * FC + f + 1)
                    v.tensor_tensor(grp(big, f), pb[3 + s][:], sgl[s], ALU.mult).then_inc(ff_free, 1)

                with dve.Fori(0, FC // 3) as i:
                    for s in range(3):
                        half(i * 3 + s, s)
                half(FC - 1, 0)
                with dve.Fori(0, 4) as i:
                    for g in range(2):
                        d = i * 2 + g
                        dve.wait_ge(dn_ready, n * KC + d + 1)
                        x = grp(xT, d)
                        v.scalar_tensor_tensor(out=x, in0=pb[6 + g][:], scalar=0.5, in1=x, op0=ALU.mult, op1=ALU.add).then_inc(dn_free, 1)
                dve.drain()

            dve.wait_ge(tok_done, 2 * DEPTH + 1)
            dve.wait_ge(xT_ready, 4 * KC + 1)
            rms(0)
            feed_forward(0)
            rms(1)
            dve.wait_ge(rel_stored, 16)

            def convolve(g):
                c = CONV_GROUPS.index(g)
                x, y = grp(big, g), ctmp[c % 2]
                dve.wait_ge(lin_free, DEPTH * LIN_LAYER + g + 1 + 2)
                if c >= 2:
                    dve.wait_ge(conv_silu, c - 1)
                wc = lambda j: conv_w[:, c * CONV + j:c * CONV + j + 1]
                last = v.tensor_scalar(y, x, wc(2), None, ALU.mult)
                for j in (0, 1, 3, 4):
                    o = j - CONV // 2
                    lo, hi = max(0, -o), S - max(0, o)
                    dve.drain()
                    last = v.scalar_tensor_tensor(out=y[:, lo:hi], in0=x[:, lo + o:hi + o], scalar=wc(j), in1=y[:, lo:hi], op0=ALU.mult, op1=ALU.add)
                last.then_inc(conv_ready, 1)

            def apply_norm(n):
                dve.wait_ge(nstd, n + 1)
                v.reciprocal(nrm, nrm)
                if n:
                    v.tensor_scalar(qk_w[:, 0:1], qk_w[:, 0:1], HEAD_DIM ** -0.5, None, ALU.mult)
                dve.drain()
                for c in range(8):
                    x = grp(big, n * 8 + c)
                    scale = qk_w[:, c // 4:c // 4 + 1] if n else (P ** -0.5 if c < 4 else 1.0)
                    last = v.scalar_tensor_tensor(out=x, in0=x, scalar=scale, in1=grp(nrm, c), op0=ALU.mult, op1=ALU.mult)
                last.then_inc(n_done, 1)
                dve.drain()

            for g in range(N_NORM + 5):
                if g in CONV_GROUPS:
                    convolve(g)
                c = g - 5
                if c >= 0:
                    dve.wait_ge(nsum_ready, c + 1)
                    v.tensor_scalar(grp(nrm, c % 8), pb[2 + c % 4][:], 1.0 / HEAD_DIM if c >= 8 else 1.0, EPS, ALU.mult, ALU.add).then_inc(nsum_used, 1)
                    if c % 8 == 7:
                        apply_norm(c // 8)
            dve.wait_ge(ab_tr, 1)
            v.tensor_copy(ab[:, :], pb[0][:, 0:NCH * 16])
            dve.drain()
            av = cut(ab[:, :], 16)

            v.tensor_copy(cut(gbeta[0:CH, :], GH), av[0:CH, :, UN:UN + GH])
            for n in range(NCH):
                v.tensor_copy(gbeta[CH:P, n * GH:(n + 1) * GH], av[CH:P, NCH - 1 - n, UN + GH:2 * UN])
            v.tensor_tensor(av[:, :, 0:UN], av[:, :, 0:UN], dtb[:, :].unsqueeze(1).to_broadcast([P, NCH, UN]), ALU.add)
            dve.drain()
            v.tensor_scalar(av[:, :, UN:16], av[:, :, 0:UN], -1.0, None, ALU.mult)
            dve.drain()
            v.tensor_tensor(cut(ga[:, :], UN), av[:, :, 0:UN], av[:, :, UN:16], ALU.max).then_inc(ab_ready, 1)
            dve.wait_ge(sp_ready, 1)
            v.scalar_tensor_tensor(out=cut(ga[:, :], UN), in0=av[:, :, 0:UN], scalar=0.0, in1=cut(ga[:, :], UN), op0=ALU.max, op1=ALU.add)
            v.tensor_scalar(alog[:, :], alog[:, :], -1.0, None, ALU.mult)
            dve.drain()
            v.tensor_tensor(cut(ga[:, :], UN), cut(ga[:, :], UN), alog[:, :].unsqueeze(1).to_broadcast([P, NCH, UN]), ALU.mult).then_inc(g_ready, 1)
            dve.wait_ge(gc_ready, 1)
            for r in range(2):
                v.tensor_copy(cut(half_ones[:, r * P:(r + 1) * P], CH), block_ones[:, r * CH:(r + 1) * CH].unsqueeze(1).to_broadcast([P, 2, CH]))
            v.tensor_tensor(id_pair[:, :], identity[:, 0:CH], identity[:, CH:P], ALU.add)
            v.tensor_copy(gg[0:CH, :], pb[1][0:CH, 0:NCH * GH])
            for n in range(NCH):
                last = v.tensor_copy(gg[CH:P, n * GH:(n + 1) * GH], pb[1][CH:P, (NCH - 1 - n) * GH:(NCH - n) * GH])
            last.then_inc(gc_done, 1)
            A0 = DEPTH * NT * ATT
            dve.wait_ge(hank_loaded, 16)
            with dve.Fori(0, NT) as b:
                def prepare2(h, top, neg):
                    v.tensor_tensor_reduce(out=lg2[h % 3], in0=pb[LOGIT_BANKS[h % 3]][:], in1=lnw_b, scale=1.0, scalar=LOWEST,
                                           op0=ALU.add, op1=ALU.max, accum_out=top)
                    dve.drain()
                    return v.tensor_scalar(neg, top, -1.0, None, ALU.mult)

                dve.wait_ge(staged, DEPTH * NT + b + 1)
                heads(A0 + b * HEADS, HEADS, prepare2, lambda h: S, lg2)
            dve.wait_ge(att_done, DEPTH * NT + NT)
            v.memset(st[0], 0.0).then_inc(g_state, 1)
            dve.wait_ge(masks_loaded, 16)
            dve.drain()
            incl = msk[:, LEVELS * LW:]

            def ident(heads):
                return id_pair[:, :].unsqueeze(1).to_broadcast([P, heads, CH])

            def over(t, n, w=GH):
                return t.unsqueeze(2).to_broadcast([P, w, n])

            def diagonals(n):
                v.tensor_copy(gs[:, :], gg[:, bass.ds(n * GH, GH)])
                v.tensor_copy(bs[:, :], gbeta[:, bass.ds(n * GH, GH)])
                dve.drain()
                v.tensor_tensor(cut(dg, CH), ident(GH), over(gs[:, :], CH), ALU.mult)
                v.tensor_tensor(cut(db, CH), ident(GH), over(bs[:, :], CH), ALU.mult).then_inc(g_diag, 1)

            def prepare_chunk(n, par, first):
                dve.wait_ge(g_rows, n + 1)
                dve.wait_ge(g_eg, n + 1)
                alone(dve)
                own = cut(pb[5][:, 0:LW], CH)
                v.tensor_copy(gend[0:CH, :].unsqueeze(2), own[0:CH, :, CH - 1:CH])
                v.tensor_copy(gend[CH:P, :].unsqueeze(2), own[CH:P, :, 0:1])
                v.tensor_tensor(cut(dT, CH), own, over(gs[:, :], CH), ALU.subtract)
                dve.drain()
                v.tensor_tensor(dT, dT, incl, ALU.mult)
                v.tensor_tensor(dfac[:, :], gend[:, :], gs[:, :], ALU.subtract).then_inc(g_diff, 1)
                v.tensor_tensor(kbF, eg, pb[1][:], ALU.mult)
                v.tensor_tensor(cut(vB, P), cut(pb[3][:], P), over(bs[:, :], P), ALU.mult)
                v.tensor_tensor(qg[par], qs, eg, ALU.mult)
                dve.drain()
                v.tensor_tensor(kbF, ks, kbF, ALU.mult)
                dve.wait_ge(g_dexp, n + 1)
                alone(dve)
                v.tensor_tensor(dT, dT, incl, ALU.mult)
                v.tensor_tensor(cut(kdec[par], P), cut(pb[2][:], P), over(dfac[:, :], P), ALU.mult).then_inc(g_kv_used, 1)
                dve.drain()
                v.tensor_tensor(lT, pb[0][:, 0:LW], dT, ALU.mult)
                v.tensor_tensor(inT[par], pb[0][:, LW:2 * LW], dT, ALU.mult)
                dve.drain()
                v.tensor_tensor(lT, pb[5][:, LW:2 * LW], lT, ALU.mult)
                dve.drain()
                v.tensor_tensor(lbT, lT, msk[:, 0:LW], ALU.mult)
                if not first:
                    dve.wait_ge(g_vnm, n)
                    alone(dve)
                dve.drain()
                v.tensor_tensor(cut(Mm, CH), ident(GH), cut(lbT, CH), ALU.subtract).then_inc(g_mats, 1)

            def half(t, g, c0=0):
                return t[:, c0 + g * LW // 2:c0 + (g + 1) * LW // 2]

            def first_level(n):
                for g in range(2):
                    dve.wait_ge(g_up, n * LEVELS * 2 + g + 1)
                    alone(dve)
                    v.tensor_tensor(cut(half(Tm, g), CH), ident(GH // 2), cut(half(pb[4 + g], g), CH), ALU.subtract)
                    v.tensor_tensor(half(lbT, g), half(lT, g), half(msk, g, LW), ALU.mult).then_inc(g_tm, 1)

            def chunk(n, par, left):
                with dve.Fori(0, LEVELS - 2) as q:
                    dve.drain()
                    for g in range(2):
                        dve.wait_ge(g_up, (n * LEVELS + q + 1) * 2 + g + 1)
                        alone(dve)
                        v.tensor_tensor(half(Tm, g), half(Tm, g), half(pb[4 + g], g), ALU.subtract)
                        v.tensor_tensor(half(lbT, g), half(lT, g), msk[:, bass.ds((q + 2) * LW + g * (LW // 2), LW // 2)], ALU.mult)
                        v.tensor_tensor(half(Mm, g), half(Mm, g), half(pb[4 + g], g, LW), ALU.subtract).then_inc(g_tm, 1)
                dve.drain()
                for g in range(2):
                    dve.wait_ge(g_up, (n * LEVELS + LEVELS - 1) * 2 + g + 1)
                    alone(dve)
                    v.tensor_tensor(half(Mm, g), half(Mm, g), half(pb[4 + g], g, LW), ALU.subtract).then_inc(g_tm, 1)
                dve.wait_ge(g_r, n + 1)
                alone(dve)
                v.tensor_tensor(resid, vB, pb[6][:], ALU.subtract).then_inc(g_rsub, 1)
                if not left:
                    return
                prepare_chunk(n + 1, 1 - par, False)
                v.tensor_tensor(cut(st[1 - par], P), cut(st[par], P), over(egl[par][:, :], P, UN), ALU.mult)
                if left > 1:
                    diagonals(n + 2)
                first_level(n + 1)
                dve.wait_ge(g_out, n + 1)
                alone(dve)
                dve.drain()
                for r in range(2):
                    x = st[1 - par][:, r * S:(r + 1) * S]
                    last = v.tensor_tensor(x, x, pb[2 + r][:], ALU.add)
                last.then_inc(g_state, 1)

            diagonals(0)
            prepare_chunk(0, 0, True)
            diagonals(1)
            first_level(0)
            with dve.Fori(0, NCH // 2 - 1) as i:
                for par in range(2):
                    chunk(i * 2 + par, par, 2)
            chunk(NCH - 2, 0, 1)
            chunk(NCH - 1, 1, 0)
            dve.wait_ge(g_o, NCH + 1)
            v.tensor_tensor(of, of, ob, ALU.add).then_inc(o_sum, 1)
            for h in range(GH):
                dve.wait_ge(o_ss, h + 1)
                last = v.tensor_scalar(grp(ob, h), pb[2 + h][:], 1.0 / P, EPS, ALU.mult, ALU.add)
            last.then_inc(o_var, 1)
            dve.wait_ge(o_std, 1)
            v.reciprocal(ob, ob)
            dve.drain()
            v.scalar_tensor_tensor(out=ob, in0=ob, scalar=gn_w[:, 0:1], in1=grp(big, H_Z, 4), op0=ALU.mult, op1=ALU.mult)
            dve.drain()
            v.tensor_tensor(of, of, ob, ALU.mult).then_inc(o_done, 1)
            for d in range(KC):
                dve.wait_ge(lin_ready, DEPTH * LIN_LAYER + N_H + d + 1)
                x = grp(xT, d)
                v.tensor_tensor(x, x, pb[OUT_BANKS[d]][:], ALU.add).then_inc(lin_free, 1)
            dve.drain()
            rms(2)
            feed_forward(1)
            rms(3)


def _bucket(rel):
    import math
    import numpy as np
    nb, far = 16, 1024
    exact = nb // 2
    n = np.abs(rel)
    large = exact + (np.log(np.maximum(n, 1) / exact) / math.log(far / exact) * (nb - exact)).astype(np.int32)
    return (rel > 0).astype(np.int32) * nb + np.where(n < exact, n, np.minimum(large, nb - 1))


def _constants():
    import numpy as np
    f = np.float32
    i = np.arange(P)
    rot = np.zeros((P, P), f)
    half = i % HEAD_DIM < HEAD_DIM // 2
    rot[i[half] + HEAD_DIM // 2, i[half]] = -1.0
    rot[i[~half] - HEAD_DIM // 2, i[~half]] = 1.0
    cst = np.stack([np.eye(P), np.ones((P, P)), i[:, None] // 64 == i // 64, rot, np.eye(P)[::-1], i[:, None] < i], 1)
    t = np.arange(S)
    adm = np.where(t // 64 <= t[:, None] // 64, 0.0, BIG_NEG)
    far = np.abs(t - t[:, None])
    count = (far <= 64).astype(int) + ((far % 4 == 0) & (far // 4 <= 64)) + ((far % 16 == 0) & (far // 16 <= 64))
    lnw = np.where(count > 0, np.log(np.maximum(count, 1)), BIG_NEG)
    by_tile = lambda m: m.reshape(NT, P, S).transpose(1, 0, 2).reshape(P, NT * S).astype(f)
    rec = 1.0 / np.minimum(np.arange(16) + 1, np.array([[2], [4], [8], [16]]))
    c = np.arange(CH)
    both = lambda m: np.concatenate([np.tile(m, GH), np.tile(m.T, GH)], 0)
    upper = c[:, None] < c
    levels = [both(upper & (c[:, None] // (2 << q) == c // (2 << q)) & (c[:, None] >> q != c >> q)) for q in range(LEVELS)]
    incl = c[:, None] <= c
    oh = (_bucket(np.arange(1024) - (S - 1)) == np.arange(32)[:, None])
    freq = (10000.0 ** (-(i % 32).astype(f) / f(32))).astype(f)
    return {
        "cst": cst.reshape(P, 6 * P).astype(f), "adm": by_tile(adm), "lnw": by_tile(lnw),
        "pool_rec": np.broadcast_to(rec.reshape(1, 64), (P, 64)).astype(f),
        "msk": np.concatenate(levels + [both(incl)], 1).astype(f),
        "gtri": np.concatenate([incl, incl.T], 0).astype(f), "rel_oh": oh.astype(f),
        "inv_freq": freq[:, None], "before": np.broadcast_to(np.arange(4) < np.arange(4)[:, None], (P, 4, 4)).reshape(P, 16).astype(f), "blk_iota": np.broadcast_to(np.arange(N_BLK), (P, N_BLK)).astype(f),
    }


def _layout(a):
    import numpy as np
    cat = np.concatenate

    def by_feature(m):
        return m.T.reshape(-1, P, m.shape[0]).transpose(1, 0, 2).reshape(P, -1)

    def unit(w):
        return w.reshape(-1, P, w.shape[1]).transpose(1, 0, 2).reshape(P, -1)

    def units(w):
        return [unit(w[:, g * P:(g + 1) * P]) for g in range(w.shape[1] // P)]

    def pairs(us):
        return [cat(us[j:j + 2], 1) for j in range(0, len(us), 2)]

    def wide(w, n, j):
        return unit(w[j * 512:(j + 1) * 512, n * 512:(n + 1) * 512])

    cuts = np.cumsum([512, 512, 512, 512, 512, 64, 8, 512])

    def in_columns(w):
        pool, q, k, v, iq, ik, iw, mq, gates = np.split(w, cuts, axis=-1)
        return cat([pool, q, mq, k, iq, ik, ik, v] + [iw] * 16, -1), gates

    out = {}
    x = a["x"][0]
    out["xT"], out["xtok"] = by_feature(x), x.reshape(NT, P, D).transpose(1, 0, 2).reshape(P, NT * D)
    out["memT"], out["positions"] = by_feature(a["mem"][0]), a["positions"][0]
    layers, bp, bg = [], [], []
    for l in range(DEPTH):
        main, gates = in_columns(a["w_in"][l])
        main = cat([main[:, g * P:(g + 1) * P] for g in ORDER], 1)
        gate = units(gates)
        stream = pairs(units(a["w_mem_kv"][l]) + units(main))
        mixed = []
        for n in range(3):
            br = [unit(a["w_br"][l, n][:, d * P:(d + 1) * P]) for d in range(KC)]
            for d in range(0, KC, 2):
                mixed += [gate[n * KC + d], gate[n * KC + d + 1], cat(br[d:d + 2], 1)]
        stream += pairs(mixed) + [wide(a["w_out"][l], n, j) for n in range(2) for j in range(2)]
        layers += stream
        b_main, b_gates = in_columns(a["b_in"][l])
        bp.append(b_main.reshape(N_G, P).T)
        bg.append(b_gates.reshape(24, P).T)
    out["w_layer"], out["bias_p"], out["bias_g"] = np.stack(layers), cat(bp, 1), cat(bg, 1)
    out["w_moe"] = np.stack([
        m for l in range(DEPTH) for e in range(N_EXP)
        for m in [wide(a["w1"][l, e], 0, 0), wide(a["w1"][l, e], 0, 1), wide(a["w3"][l, e], 0, 0), wide(a["w3"][l, e], 0, 1),
                  wide(a["w2"][l, e], 0, 0), wide(a["w2"][l, e], 1, 0)]])
    gap = np.zeros((P, 2 * P), np.float32)

    def ffn(g, u, d):
        up = [m for pair in zip(units(g), units(u)) for m in pair]
        down = [m for w in units(d) for m in np.split(cat([w, gap], 1), 3, axis=1)]
        return pairs(up) + pairs(down)

    qkv, z, ab, swa = np.split(a["w_in_2"][0], [1536, 2048, 2064], axis=1)
    tail = ffn(a["ffn1_w_gate_2"][0], a["ffn1_w_up_2"][0], a["ffn1_w_down_2"][0])
    tail += pairs(units(cat([qkv[:, :1024], swa[:, :1024], qkv[:, 1024:], z, swa[:, 1024:]] + [ab] * 16, 1)))
    tail += [unit4 for half in (1, 0) for g in (0, 4) for unit4 in [
        cat([unit(a["w_out_2"][0][half * 512:(half + 1) * 512, d * P:(d + 1) * P]) for d in range(g, g + 4)], 1)]]
    tail += ffn(a["ffn2_w_gate_2"][0], a["ffn2_w_up_2"][0], a["ffn2_w_down_2"][0])
    out["w_tail"] = np.stack(tail)
    out["pool_w"] = a["pool_w"].reshape(DEPTH * 4, P, P)
    out["pool_scale"] = a["pool_scale"].reshape(DEPTH * 4, P).T
    out["w_router"], out["router_bias"] = unit(a["w_router"]), a["router_bias"]
    out["ln_par"] = np.stack([cat([a[f"ln{n}_g"][l], a[f"ln{n}_b"][l]]) for l in range(DEPTH) for n in (1, 2)])
    out["ln_T"] = cat([a[f"ln{n}_{x}"][l].reshape(KC, P).T for l in range(DEPTH) for n in (1, 2) for x in "gb"], 1)
    out["normw"] = cat([a[n][0].reshape(KC, P).T for n in ("ffn1_norm_2", "mix_norm_2", "ffn2_norm_2", "final_norm_2")], 1)
    out["conv_w"] = a["conv_w_2"][0].reshape(12, P, CONV).transpose(1, 0, 2).reshape(P, 12 * CONV)
    out["gn_w"] = a["gdn_norm_w_2"].reshape(P, 1)
    out["qk_w"] = np.stack([cat([a[n][0]] * 2) for n in ("q_norm_w_2", "k_norm_w_2")], 1)
    out["rel_b"] = a["rel_bias_2"]
    out["a_log"], out["dt_bias"] = a["a_log_2"].reshape(UN), a["dt_bias_2"].reshape(UN)
    return out


def kernel(**inputs):
    import numpy as np
    import concourse.bacc as bacc
    from concourse.bass_utils import run_bass_kernel_spmd

    arrays = {**_constants(), **_layout({k: np.asarray(v) for k, v in inputs.items()})}
    arrays = {k: np.ascontiguousarray(v) for k, v in arrays.items()}
    nc = bacc.Bacc("TRN2", target_bir_lowering=False, num_devices=1)
    aps = {k: nc.dram_tensor(f"in_{k}", v.shape, mybir.dt.from_np(v.dtype), kind="ExternalInput").ap() for k, v in arrays.items()}
    out = nc.dram_tensor("out", (P, KC * S), F32, kind="ExternalOutput").ap()
    two_blocks(nc, aps, out)
    r = run_bass_kernel_spmd(nc, [{f"in_{k}": v for k, v in arrays.items()}], core_ids=[0])
    got = r.results[0]["out"]
    return got.reshape(P, KC, S).transpose(2, 1, 0).reshape(1, S, D)
```

```python
import concourse.bass as bass
import concourse.mybir as mybir
from contextlib import ExitStack

F32 = mybir.dt.float32
I32 = mybir.dt.int32
U32 = mybir.dt.uint32
ACT = mybir.ActivationFunctionType
ALU = mybir.AluOpType
AX = mybir.AxisListType

P = 128
S = 512
D = 1024
KC = D // P
NT = S // P
DEPTH = 2
N_MEM = 256
HEADS, HEAD_DIM = 8, 64
MEM_HEADS, MEM_DIM = 4, 128
N_SEL = 128
N_EXP, GROUPS, PER_GROUP = 16, 4, 4
D_EXP = 512
MOE_BLOCK = 128
N_BLK = (2 * S + N_EXP * (MOE_BLOCK - 1)) // MOE_BLOCK
IN_OF = OUT_OF = N_BLK // 2
LAST = (N_BLK - 1) * MOE_BLOCK
assert N_BLK % 2 == 1
DN_ALPHA = (2 * DEPTH) ** 0.25
LN_EPS, EPS = 1e-5, 1e-6
D_FF = 2816
FC = D_FF // P
CH = 64
NCH = S // CH
GH = 4
UN = 2 * GH
LEVELS = 6
CONV = 5
BIG_NEG = -1e30
LOWEST = -3e38

SLOTS, PAIR = 3, 2 * KC * P
LAYER_STREAM = 39
MOE_PAIRS = 6
UP_PAIRS = 4
LAYER_PAIRS = LAYER_STREAM + MOE_PAIRS * N_BLK
LAYER_USES = LAYER_PAIRS // SLOTS
TAIL_PAIRS = 87
assert LAYER_STREAM % SLOTS == LAYER_PAIRS % SLOTS == TAIL_PAIRS % SLOTS == MOE_PAIRS % SLOTS == 0

G_POOL, G_Q, G_MQ, G_K, G_IQ, G_IK, G_V, G_IW, N_G = 0, 4, 8, 12, 16, 20, 21, 25, 26
MEM_GROUPS = 8
LIN_LAYER = MEM_GROUPS + N_G
ROT_GROUPS = [*range(G_IQ, G_IQ + 4), G_IK, *range(G_Q, G_Q + 4), *range(G_K, G_K + 4)]
N_ROT, ROT_IDX = len(ROT_GROUPS), 5
ORDER = [*range(G_IQ, G_IQ + 4), G_IK, G_IW, *range(G_Q, G_Q + 4), *range(G_K, G_K + 4), *range(G_POOL, G_POOL + 4),
         *range(G_V, G_V + 4), *range(G_MQ, G_MQ + 4)]
AT_MV, AT_IW, AT_SCORE, AT_ROT, AT_VT = 5, 7, {8: 1, 13: 2, 18: 3}, {12: 5, 17: 9}, 24
N_TOP = NT - 1
assert P <= N_SEL
H_Q, H_K, H_SQ, H_SK, H_V, H_Z, H_SV, H_AB, N_H = 0, 4, 8, 12, 16, 20, 24, 28, 30
CONV_GROUPS = [*range(H_Q, H_Q + 8), *range(H_V, H_V + 4)]
N_NORM = 16

ATT = HEADS + MEM_HEADS


def keys(b):
    return (b + 1) * P


LOGIT_BANKS = (0, 1, 6)
OUT_BANKS = (0, 1, 6, 7, 2, 3, 4, 5)

TWO_PI = 6.283185307179586
PI_A, PI_B = 6.28125, 0.0019350051879882812
PI_C = TWO_PI - PI_A - PI_B
ROUND = 12582912.0



def two_blocks(nc, a, out):
    ctx = ExitStack()
    with ctx:
        def sb(name, cols, dt=F32, rows=P):
            return ctx.enter_context(nc.sbuf_tensor(name, [rows, cols], dt))

        def sem(name):
            return ctx.enter_context(nc.semaphore(name))

        cst = sb("cst", 6 * P)
        identity, ones, block_ones, rot, reverse, tri = (cst[:, c * P:(c + 1) * P] for c in range(6))
        cos_t, sin_t = sb("cos_t", S), sb("sin_t", S)
        ring = [sb(f"ring{s}", PAIR) for s in range(SLOTS)]
        xT = sb("xT", KC * S)
        xtok = sb("xtok", NT * D)
        big = sb("big", 30 * S)
        am = sb("am", KC * S)
        lnw = sb("lnw", NT * S)
        sr = sb("sr", 13312)
        bias_p, bias_g = sb("bias_p", DEPTH * N_G), sb("bias_g", DEPTH * 24)
        pool_scale, pool_rec = sb("pool_scale", DEPTH * 4), sb("pool_rec", 4 * 16)
        w_router, r_bias = sb("w_router", KC * N_EXP), sb("r_bias", N_EXP)
        inv_freq, blk_iota = sb("inv_freq", 1), sb("blk_iota", N_BLK)
        before = sb("before", PER_GROUP * PER_GROUP)
        iw_tok = sb("iw_tok", NT * 8)
        top8 = sb("top8", 8)
        stat = sb("stat", 64)
        ln_st, ln_mv = sb("ln_st", NT * 12), sb("ln_mv", NT * 5)
        ln_T = sb("ln_T", 2 * DEPTH * 2 * KC)
        dest = sb("dest", 2 * NT, I32)
        blk_e = sb("blk_e", N_BLK, I32)
        gate2 = sb("gate2", 2 * NT)
        normw = sb("normw", 4 * KC)
        conv_w = sb("conv_w", 12 * CONV)
        gn_w, qk_w = sb("gn_w", 1), sb("qk_w", 2)
        rel_b = sb("rel_b", HEADS, rows=32)
        ab, ga = sb("ab", NCH * 16), sb("ga", NCH * UN)
        gg, gbeta = sb("gg", NCH * GH), sb("gbeta", NCH * GH)
        alog, dtb = sb("alog", UN), sb("dtb", UN)
        gtri, id_pair, half_ones = sb("gtri", CH), sb("id_pair", CH), sb("half_ones", 2 * P)
        gs, bs, gend, dfac = (sb(n, GH) for n in ("gs", "bs", "gend", "dfac"))
        gl, egl = sb("gl", UN), [sb(f"egl{i}", UN) for i in range(2)]
        pb = [ctx.enter_context(nc.psum_tensor(f"pb{i}", [P, S], F32)) for i in range(8)]

        xs_dram = nc.dram_tensor("xs_dram", (N_BLK * MOE_BLOCK, D), F32).ap()
        ys_dram = nc.dram_tensor("ys_dram", (N_BLK * MOE_BLOCK, D), F32).ap()
        rel_dram = nc.dram_tensor("rel_dram", (HEADS, 1024), F32)

        def grp(t, g, n=1, w=S):
            if isinstance(g, int):
                return t[:, g * w:(g + n) * w]
            return t[:, bass.ds(g * w, n * w)]

        def cut(ap, n):
            return ap.rearrange("p (g n) -> p g n", n=n)

        at = [0]

        def take(cols, rows=P):
            at[0] += cols
            assert at[0] <= 13312, at[0]
            return sr[0:rows, at[0] - cols:at[0]]

        adm = am[:, 0:NT * S]
        memT = am[:, NT * S:NT * S + KC * N_MEM]
        mk, mv, mvf = take(4 * N_MEM), take(2 * S), take(4 * N_MEM)
        at_idx = at[0]
        relu2 = [take(S) for _ in range(2)]
        score, work = take(S), take(S)
        lg = [take(S) for _ in range(3)]
        pT = [take(S) for _ in range(2)]
        tmp = [take(S) for _ in range(2)]
        pw_b = take(S)
        vtok = grp(big, N_G, 4)
        merged = grp(big, G_K, 8)
        ln_par = grp(big, G_IK, 4)
        xs = [grp(big, 0, 2), grp(big, 2, 2)]
        xsT = [grp(big, 4, 2), grp(big, 6, 2)]
        sil, hid, hT = grp(big, 8), grp(big, 9), grp(big, 10)
        ysb = [grp(big, 11, 2), grp(big, 13, 2)]
        yg = [[grp(big, 15, 2), grp(big, 17, 2)], [grp(big, 24, 2), grp(big, 26, 2)], xs, [sr[:, at_idx:at_idx + D], sr[:, at_idx + D:at_idx + 2 * D]]]
        sel = score
        last_sel, last_selT = lg[0], lg[2]
        rt = take(1024)
        rat = [0]

        def rtile(cols):
            rat[0] += cols
            return rt[:, rat[0] - cols:rat[0]]

        r_score, r_biased, r_rank, r_pick, r_t = (rtile(NT * N_EXP) for _ in range(5))
        r_one, r_u = [rtile(NT * N_EXP) for _ in range(2)], [rtile(NT * N_EXP) for _ in range(2)]
        r_gsum, r_grank, r_nblk, r_end = (rtile(N_EXP) for _ in range(4))
        r_cmp = tmp
        r_sum, r_dest, r_last, r_blk = rtile(NT), rtile(2 * NT), rtile(2 * NT), rtile(N_BLK)
        assert rat[0] <= 1024 and max(NT * GROUPS * PER_GROUP ** 2, N_BLK * N_EXP) <= S
        xns = [sr[:, 0:KC * S], xtok[:, :], xtok[:, :], xtok[:, :]]
        sq_sum = am[:, 0:S]
        primed = stat[:, 63:64]
        at[0] = HEADS * 896 + NT * S + 2 * S
        sgl = [take(S) for _ in range(3)]
        sq2 = [take(S) for _ in range(2)]
        rs = take(S)
        at[0] = 0
        hank = take(HEADS * 896)
        v2 = take(NT * S)
        rel_oh = v2[0:32, 0:1024]
        rel_row = sr[0:HEADS, at[0]:at[0] + 1024]
        lg2 = [take(S) for _ in range(3)]
        pT2 = [take(S) for _ in range(2)]
        q2_b, lnw_b = take(S), take(S)
        ctmp = [pT2[0], pT2[1]]
        nsq = lg2[0:2]
        nrm = am[:, :]
        at[0] = 0
        ks, qs, vs, eg, kbF = (take(UN * CH) for _ in range(5))
        qg = [take(UN * CH) for _ in range(2)]
        dg, db, dT, lT, lbT, Tm, Mm, Am = (take(GH * CH) for _ in range(8))
        inT = [take(GH * CH) for _ in range(2)]
        vB, resid, vn = (take(GH * P) for _ in range(3))
        kdec = [take(GH * P) for _ in range(2)]
        st = [take(UN * P) for _ in range(2)]
        LW = GH * CH
        msk = am[:, 0:(LEVELS + 1) * LW]
        cat = xtok[:, :]
        of, ob = cat[:, 0:4 * S], lnw[:, :]

        loaded, rope_loaded, mem_loaded, x_loaded = sem("constants_loaded"), sem("positions_loaded"), sem("memory_loaded"), sem("x_loaded")
        xtok_loaded, lnw_loaded = sem("xtok_loaded"), sem("lnw_loaded")
        masks_loaded, hank_loaded, rel_stored = sem("masks_loaded"), sem("hank_loaded"), sem("rel_stored")
        xs_zeroed, zero_ready = sem("xs_zeroed"), sem("zero_ready")
        w_loaded = [sem(f"weights_loaded{s}") for s in range(SLOTS)]
        slot_free = sem("slot_free")
        rope_arg, rope_sin = sem("rope_arg"), sem("rope_sin")
        lin_ready, lin_free = sem("lin_ready"), sem("lin_free")
        rot_ready, rot_used = sem("rot_ready"), sem("rot_used")
        vt_ready, vt_copied = sem("v_transposed"), sem("v_copied")
        pool_w_loaded, oh_loaded = sem("pool_w_loaded"), sem("buckets_loaded")
        pool_in, pool_mixed, pool_done = sem("pool_in"), sem("pool_mixed"), sem("pool_done")
        adm_loaded, masks_ready, sparse_done = sem("adm_loaded"), sem("masks_ready"), sem("sparse_done")
        staged, idx_ready, idx_copied, idx_used = sem("staged"), sem("idx_ready"), sem("idx_copied"), sem("idx_used")
        lg_ready, lg_masked, exp_done, p_ready = sem("logits_ready"), sem("logits_masked"), sem("exp_done"), sem("p_ready")
        tr_ready, pT_ready, pv_ready, att_done = sem("p_transposed"), sem("pT_ready"), sem("pv_ready"), sem("att_done")
        merged_ready = sem("merged_ready")
        gate_ready, gate_free, br_ready, br_free = sem("gate_ready"), sem("gate_free"), sem("br_ready"), sem("br_free")
        mix_ready = sem("mix_ready")
        ln_loaded, var_ready, std_ready, shift_ready = sem("ln_loaded"), sem("var_ready"), sem("std_ready"), sem("shift_ready")
        normed, tok_done = sem("rows_normed"), sem("rows_scaled")
        xtr_ready, xT_ready = sem("xtr_ready"), sem("xT_ready")
        sc_ready, sig_ready, pick_ready, rank_ready, dest_ready, route_ready = (
            sem(n) for n in ("router_logits", "router_scores", "picks_ready", "ranks_ready", "dest_ready", "route_ready"))
        sel_ready = sem("first_block_picked")
        last_picked, last_turned, last_copied = sem("last_block_picked"), sem("last_block_turned"), sem("last_block_copied")
        last_summed, last_added = sem("last_block_summed"), sem("last_block_added")
        xs_scattered = sem("xs_scattered")
        xs_loaded = [sem(f"xs_loaded{s}") for s in range(2)]
        xs_tr, xsT_ready = sem("xs_transposed"), sem("xsT_ready")
        up_ready, sil_ready, hid_ready = sem("up_ready"), sem("sil_ready"), sem("hid_ready")
        ht_ready, hT_ready, y_ready, y_copied = sem("h_transposed"), sem("hT_ready"), sem("y_ready"), sem("y_copied")
        y_stored = [sem(f"y_stored{s}") for s in range(2)]
        y_back = [sem(f"y_back{t}") for t in range(NT)]
        sq_ready, sq_used, sq_summed, ss_ready, rvar, rstd, xn_ready = (
            sem(n) for n in ("sq_ready", "sq_used", "squares_summed", "sums_ready", "rms_var", "rms_std", "xn_ready"))
        ff_ready, ff_silu, ff_free = sem("ff_ready"), sem("ff_silu"), sem("ff_free")
        dn_ready, dn_free = sem("down_ready"), sem("down_free")
        conv_ready, conv_silu = sem("conv_ready"), sem("conv_silu")
        nsq_ready, nsum_ready, nsum_used, nstd, n_done = (
            sem(n) for n in ("norm_sq", "norm_sums", "norm_sums_used", "norm_std", "norm_done"))
        rel_ready, rel_copied = sem("rel_ready"), sem("rel_copied")
        v2_tr, v2_ready = sem("v2_transposed"), sem("v2_ready")
        ab_tr, ab_ready, sp_ready, g_ready, gc_ready, gc_done = (
            sem(n) for n in ("ab_transposed", "ab_ready", "softplus_ready", "g_ready", "g_cumsum", "g_done"))
        g_staged, g_diag, g_rows, g_eg, g_diff, g_dexp = (sem("delta_" + n) for n in (
            "staged", "diagonals", "rows", "row_exps", "differences", "decays"))
        g_kv_used, g_mats = sem("delta_kv_used"), sem("delta_mats")
        g_a, g_am, g_up, g_tm = (sem("delta_" + n) for n in ("level_product", "level_copied", "level_update", "level_done"))
        g_r, g_rsub, g_vnm, g_vn, g_out, g_o, g_state = (sem("delta_" + n) for n in (
            "state_part", "residual", "new_values", "new_values_copied", "output", "output_copied", "state"))
        o_sum, o_sq, o_ss, o_var, o_std, o_done = (
            sem(n) for n in ("o_sum", "o_sq", "o_sumsq", "o_var", "o_std", "o_done"))
        out_stored = sem("out_stored")
        passed = sem("waits_passed")

        ROPE_CONSTS = [(work.bitcast(I32), a["positions"].partition_broadcast(P)), (inv_freq[:, :], a["inv_freq"])]
        CONSTS = [
            (cst[:, :], a["cst"]), (bias_p[:, :], a["bias_p"]),
            (pool_scale[:, :], a["pool_scale"]), (pool_rec[:, :], a["pool_rec"]), (bias_g[:, :], a["bias_g"]),
            (w_router[:, :], a["w_router"]), (r_bias[:, :], a["router_bias"].partition_broadcast(P)),
            (blk_iota[:, :], a["blk_iota"]), (before[:, :], a["before"]), (ln_T[:, :], a["ln_T"]), (normw[:, :], a["normw"]),
            (conv_w[:, :], a["conv_w"]), (gn_w[:, :], a["gn_w"]), (qk_w[:, :], a["qk_w"]),
            (rel_b[:, :], a["rel_b"]),
            (alog[:, :], a["a_log"].partition_broadcast(P)), (dtb[:, :], a["dt_bias"].partition_broadcast(P)),
            (gtri[:, :], a["gtri"]),
        ]
        N_CONST = 16 * len(CONSTS)

        def alone(eng):
            eng.sem_inc(passed, 1)

        block = ctx.enter_context(nc.Block())

        @block.sync
        def _(sp):
            sp.dma_start(memT, a["memT"]).then_inc(mem_loaded, 16)
            with sp.Fori(0, DEPTH) as l:
                with sp.Fori(0, LAYER_STREAM // SLOTS) as i:
                    for s in range(SLOTS):
                        sp.wait_ge(slot_free, l * LAYER_PAIRS + i * SLOTS + s + 1)
                        sp.dma_start(ring[s][:, :], a["w_layer"][bass.ds(l * LAYER_STREAM + i * SLOTS + s, 1)]
                                     .rearrange("a p n -> p (a n)")).then_inc(w_loaded[s], 16)
                sp.wait_ge(route_ready, l + 1)
                alone(sp)

                def expert_pairs(b, first, count, at, slot):
                    e = sp.value_load(blk_e[0:1, bass.ds(b, 1)], min_val=0, max_val=N_EXP - 1)
                    for j in range(count):
                        u = (slot + j) % SLOTS
                        sp.wait_ge(slot_free, l * LAYER_PAIRS + LAYER_STREAM + at + j + 1)
                        sp.dma_start(ring[u][:, :], a["w_moe"][bass.ds((l * N_EXP + e) * MOE_PAIRS + first + j, 1)]
                                     .rearrange("a p n -> p (a n)")).then_inc(w_loaded[u], 16)

                expert_pairs(0, 0, UP_PAIRS, 0, 0)
                with sp.Fori(0, N_BLK - 2) as i:
                    expert_pairs(i + 1, 0, UP_PAIRS, UP_PAIRS + i * MOE_PAIRS, UP_PAIRS)
                    expert_pairs(i, UP_PAIRS, 2, 2 * UP_PAIRS + i * MOE_PAIRS, 2 * UP_PAIRS)
                at = UP_PAIRS + (N_BLK - 2) * MOE_PAIRS
                expert_pairs(N_BLK - 2, UP_PAIRS, 2, at, at)
                expert_pairs(N_BLK - 1, 0, UP_PAIRS, at + 2, at + 2)
                expert_pairs(N_BLK - 1, UP_PAIRS, 2, at + 2 + UP_PAIRS, at + 2 + UP_PAIRS)
            with sp.Fori(0, TAIL_PAIRS // SLOTS) as i:
                for s in range(SLOTS):
                    sp.wait_ge(slot_free, DEPTH * LAYER_PAIRS + i * SLOTS + s + 1)
                    sp.dma_start(ring[s][:, :], a["w_tail"][bass.ds(i * SLOTS + s, 1)]
                                 .rearrange("a p n -> p (a n)")).then_inc(w_loaded[s], 16)
            for c in range(4):
                w = KC // 4 * S
                sp.wait_ge(xn_ready, 3 * KC + KC // 4 * (c + 1))
                sp.dma_start(out[:, c * w:(c + 1) * w], xns[3][:, c * w:(c + 1) * w]).then_inc(out_stored, 16)
            sp.wait_ge(out_stored, 4 * 16)

        @block.gpsimd
        def _(pool):
            zero = lnw[:, 0:D]
            nc.gpsimd.memset(zero, 0.0).then_inc(zero_ready, 1)
            pool.wait_ge(x_loaded, 16)
            pool.dma_start(xtok[:, :], a["xtok"]).then_inc(xtok_loaded, 16)
            pool.wait_ge(zero_ready, 1)
            with pool.Fori(0, N_BLK) as b:
                pool.dma_start(xs_dram[bass.ds(b * MOE_BLOCK, MOE_BLOCK), :], zero).then_inc(xs_zeroed, 16)
            pool.dma_start(ys_dram[LAST:LAST + MOE_BLOCK, :], zero).then_inc(xs_zeroed, 16)
            for s in range(2):
                pool.dma_start(ys_dram[s * MOE_BLOCK:(s + 1) * MOE_BLOCK, :], zero).then_inc(y_stored[s], 16)

            def scale_rows(m):
                pool.wait_ge(ln_loaded, 16 * (m + 1))
                alone(pool)
                for t in range(NT):
                    pool.wait_ge(xtr_ready, m * NT + t + 1)
                    alone(pool)
                    x = grp(xtok, t, 1, D)
                    nc.gpsimd.tensor_tensor(x, x, ln_par[:, 0:D], ALU.mult)
                pool.drain()
                for t in range(NT):
                    x = grp(xtok, t, 1, D)
                    last = nc.gpsimd.tensor_tensor(x, x, ln_par[:, D:2 * D], ALU.add)
                last.then_inc(tok_done, 1)

            with pool.Fori(0, DEPTH) as l:
                pool.dma_start(adm, a["adm"]).then_inc(adm_loaded, 16)
                pool.wait_ge(pool_done, l + 1)
                pool.dma_start(cut(pw_b, P), a["pool_w"][bass.ds(l * 4, 4)].rearrange("g c e -> c g e")).then_inc(pool_w_loaded, 16)
                pool.wait_ge(att_done, l * NT + NT)
                pool.dma_start(ln_par, a["ln_par"][bass.ds(2 * l, 1), :].rearrange("a n -> (a n)").partition_broadcast(P)).then_inc(ln_loaded, 16)
                scale_rows(2 * l)
                pool.wait_ge(xs_zeroed, 16 * (N_BLK + 1))
                pool.wait_ge(tok_done, 2 * l + 2)
                pool.wait_ge(dest_ready, l + 1)
                alone(pool)
                for k in range(2):
                    for t in range(NT):
                        pool.indirect_dma_start(
                            out=xs_dram, out_offset=bass.IndirectOffsetOnAxis(
                                ap=dest[:, k * NT + t:k * NT + t + 1].bitcast(U32), axis=0),
                            in_=grp(xtok, t, 1, D), in_offset=None).then_inc(xs_scattered, 16)
                pool.wait_ge(xs_scattered, l * 128 + 128)
                pool.dma_start(ln_par, a["ln_par"][bass.ds(2 * l + 1, 1), :].rearrange("a n -> (a n)").partition_broadcast(P)).then_inc(ln_loaded, 16)
                for s in (1, 0):
                    pool.dma_start(xs[s], xs_dram[(2 - s) * MOE_BLOCK:(3 - s) * MOE_BLOCK, :]).then_inc(xs_loaded[s], 16)

                def load_behind(b, s):
                    pool.wait_ge(xs_tr, l * N_BLK + b + 1)
                    alone(pool)
                    pool.dma_start(xs[s], xs_dram[bass.ds((b + 2) * MOE_BLOCK, MOE_BLOCK), :]).then_inc(xs_loaded[s], 16)

                def store_y(b, s):
                    pool.wait_ge(y_copied, 2 * (l * N_BLK + b + 1) + 1)
                    alone(pool)
                    pool.dma_start(ys_dram[bass.ds(b * MOE_BLOCK, MOE_BLOCK), :], ysb[s]).then_inc(y_stored[s], 16)

                load_behind(1, 1)
                with pool.Fori(0, N_BLK // 2 - 2) as i:
                    for s in range(2):
                        load_behind(i * 2 + s + 2, s)
                        store_y(i * 2 + s, s)
                load_behind(N_BLK - 3, 0)
                for b in range(N_BLK - 5, N_BLK - 1):
                    store_y(b, b % 2)
                for s in range(2):
                    pool.wait_ge(y_stored[s], 16 * OUT_OF * (l + 1) + 16)
                    pool.wait_ge(xs_loaded[s], 16 * IN_OF * (l + 1))
                alone(pool)
                for t in range(NT):
                    for k in range(2):
                        pool.indirect_dma_start(
                            out=yg[t][k], out_offset=None, in_=ys_dram,
                            in_offset=bass.IndirectOffsetOnAxis(
                                ap=dest[:, k * NT + t:k * NT + t + 1].bitcast(U32), axis=0)).then_inc(y_back[t], 16)
                scale_rows(2 * l + 1)
            pool.dma_start(lnw[:, :], a["lnw"]).then_inc(lnw_loaded, 16)
            pool.wait_ge(xT_ready, 4 * KC + 1)
            pool.dma_start(rel_oh, a["rel_oh"]).then_inc(oh_loaded, 16)
            pool.wait_ge(rel_copied, 2)
            pool.dma_start(rel_dram.ap(), rel_row).then_inc(rel_stored, 16)
            pool.wait_ge(rel_stored, 16)
            pool.wait_ge(dn_free, 3)
            pool.dma_start(cut(hank, 896), bass.AP(tensor=rel_dram, offset=0, ap=[[1, P], [1024, HEADS], [1, 896]])).then_inc(hank_loaded, 16)
            pool.wait_ge(n_done, 2)
            pool.dma_start(msk, a["msk"]).then_inc(masks_loaded, 16)

        @block.tensor
        def _(pe):
            mm = nc.tensor.matmul

            def pair(j, l=None, i=0, per=1):
                base = DEPTH * LAYER_USES if l is None else l * LAYER_USES
                pe.wait_ge(w_loaded[j % SLOTS], (base + (j // SLOTS + 1) + i * per) * 16)
                return ring[j % SLOTS]

            def unit(w, u, k):
                return w[:, (u * KC + k) * P:(u * KC + k + 1) * P]

            def linear(w, u, rhs, n, bank, cols=S, norm=None):
                pe.wait_ge(lin_free, n + 1)
                for k in range(KC):
                    if norm is not None:
                        pe.wait_ge(xn_ready, norm * KC + k + 1)
                    last = mm(pb[bank][:, 0:cols], unit(w, u, k), rhs[:, k * cols:(k + 1) * cols],
                              start=(k == 0), stop=(k == KC - 1))
                    if k == 0 and u == 0:
                        last.then_inc(slot_free, 1)
                last.then_inc(lin_ready, 1)

            def transpose_tile(m, t):
                pe.wait_ge(normed, m * NT + t + 1)
                if t >= 2:
                    pe.wait_ge(xT_ready, m * KC + 2 * (t - 1) + 1)
                alone(pe)
                for k in range(KC):
                    last = nc.tensor.transpose(pb[2 * (t % 2) + k // 4][:, k % 4 * P:(k % 4 + 1) * P], xtok[:, t * D + k * P:t * D + (k + 1) * P], identity)
                last.then_inc(xtr_ready, 1)

            def heads(n0, count, logits, values, tr, buf_p, buf_pT):
                for step in range(count + 3):
                    if step < count:
                        h = step
                        if h >= 3:
                            pe.wait_ge(lg_masked, n0 + h - 2)
                            alone(pe)
                        logits(h, pb[LOGIT_BANKS[h % 3]]).then_inc(lg_ready, 1)
                    if 2 <= step < count + 2:
                        h = step - 2
                        pe.wait_ge(p_ready, n0 + h + 1)
                        if h >= 2:
                            pe.wait_ge(pT_ready, n0 + h - 1)
                        for t in range(tr(h)):
                            last = nc.tensor.transpose(pb[2 + h % 2][:, t * P:(t + 1) * P], buf_p[h % 3][:, t * P:(t + 1) * P], identity)
                        last.then_inc(tr_ready, 1)
                    if step >= 3:
                        h = step - 3
                        pe.wait_ge(pT_ready, n0 + h + 1)
                        values(h, buf_pT[h % 2]).then_inc(pv_ready, 1)

            pe.sem_inc(slot_free, SLOTS - 1)
            for ahead in (xT_ready, y_copied, hid_ready, ht_ready, g_o, pool_done):
                pe.sem_inc(ahead, 1)
            pe.sem_inc(lin_free, 2)
            pe.sem_inc(gate_free, 2)
            pe.sem_inc(br_free, 2)
            pe.sem_inc(ff_free, 3)
            pe.sem_inc(dn_free, 2)
            pe.wait_ge(mem_loaded, 16)

            with pe.Fori(0, DEPTH) as l:
                pe.wait_ge(xT_ready, l * 2 * KC + 1)
                for j in range(4):
                    w = pair(j, l)
                    for u in range(2):
                        linear(w, u, memT, l * LIN_LAYER + 2 * j + u, u, N_MEM)
                pe.wait_ge(loaded, N_CONST)
                L0 = l * LIN_LAYER + MEM_GROUPS

                def rotate(n):
                    if n >= 4:
                        pe.wait_ge(rot_used, l * N_ROT + n - 3)
                        alone(pe)
                    mm(pb[2 + n % 4][:], rot, grp(big, ROT_GROUPS[n]), start=True, stop=True).then_inc(rot_ready, 1)

                pe.wait_ge(x_loaded, 16)
                for p in range(N_G):
                    linear(pair(4 + p // 2, l), p % 2, xT, L0 + p, p % 2)
                    if 2 <= p < 2 + ROT_IDX:
                        pe.wait_ge(lin_free, L0 + p - 2 + 1 + 2)
                        alone(pe)
                        rotate(p - 2)
                    if p == AT_MV:
                        for t in range(2):
                            for c in range(4):
                                last = nc.tensor.transpose(pb[6 + t][:, c * P:(c + 1) * P], mvf[:, c * N_MEM + t * P:c * N_MEM + (t + 1) * P], identity)
                        last.then_inc(vt_ready, 1)
                    if p == AT_IW:
                        pe.wait_ge(vt_copied, 3 * l + 1)
                        alone(pe)
                        for t in range(NT):
                            last = nc.tensor.transpose(pb[6][:, t * 8:(t + 1) * 8], big[0:8, G_IW * S + t * P:G_IW * S + (t + 1) * P], identity[0:8, 0:8])
                        last.then_inc(vt_ready, 1)
                    if p in AT_SCORE:
                        n0 = l * N_TOP + AT_SCORE[p] - 1
                        b = AT_SCORE[p]
                        pe.wait_ge(rot_used, l * N_ROT + ROT_IDX)
                        alone(pe)
                        pe.wait_ge(vt_copied, 3 * l + 2)
                        alone(pe)
                        for h in range(HEADS):
                            r = 64 * (h % 2)
                            if h >= 2 or AT_SCORE[p] > 1:
                                pe.wait_ge(idx_copied, n0 * HEADS + h - 1)
                                alone(pe)
                            mm(pb[6 + h % 2][:, 0:keys(b)], big[r:r + 64, (G_IQ + h // 2) * S + b * P:(G_IQ + h // 2) * S + (b + 1) * P],
                               big[r:r + 64, G_IK * S:G_IK * S + keys(b)], start=True, stop=True).then_inc(idx_ready, 1)
                    if p in AT_ROT:
                        for n in range(AT_ROT[p], AT_ROT[p] + 4):
                            rotate(n)
                    if p == AT_VT:
                        pe.wait_ge(rot_used, (l + 1) * N_ROT)
                        alone(pe)
                        for t in range(NT):
                            for c in range(4):
                                last = nc.tensor.transpose(pb[4 + t][:, c * P:(c + 1) * P], big[:, (G_V + c) * S + t * P:(G_V + c) * S + (t + 1) * P], identity)
                        last.then_inc(vt_ready, 1)
                pe.wait_ge(lin_free, (l + 1) * LIN_LAYER + 2)
                pe.wait_ge(vt_copied, 3 * l + 3)
                pe.wait_ge(pool_w_loaded, 16 * l + 16)
                for g in range(4):
                    pe.wait_ge(pool_in, l * 4 + g + 1)
                    mm(pb[4 + g][:], pw_b[:, g * P:(g + 1) * P], grp(big, G_POOL + g), start=True, stop=True).then_inc(pool_mixed, 1)
                pe.wait_ge(pool_done, l + 1 + 1)
                alone(pe)
                pe.wait_ge(masks_ready, (l + 1) * N_TOP)
                alone(pe)

                def logits(x, bank):
                    b, h = divmod(x, ATT)
                    if h < HEADS:
                        r, c = 64 * (h % 2), h // 2 * S
                        return mm(bank[:, 0:keys(b)], big[r:r + 64, G_Q * S + c + b * P:G_Q * S + c + (b + 1) * P],
                                  big[r:r + 64, G_K * S + c:G_K * S + c + keys(b)], start=True, stop=True)
                    h -= HEADS
                    return mm(bank[:, 0:N_MEM], big[:, (G_MQ + h) * S + b * P:(G_MQ + h) * S + (b + 1) * P], mk[:, h * N_MEM:(h + 1) * N_MEM], start=True, stop=True)

                def values(x, pt):
                    b, h = divmod(x, ATT)
                    if h in (0, HEADS) and b:
                        pe.wait_ge(sparse_done if h == 0 else att_done, l * NT + b)
                        alone(pe)
                    if h < HEADS:
                        r = 64 * (h % 2)
                        for t in range(b + 1):
                            last = mm(pb[4][r:r + 64, h // 2 * P:(h // 2 + 1) * P], vtok[:, t * S + h * 64:t * S + (h + 1) * 64],
                                      pt[:, t * P:(t + 1) * P], start=(t == 0), stop=(t == b))
                        return last
                    h -= HEADS
                    for t in range(2):
                        last = mm(pb[5][:, h * P:(h + 1) * P], mv[:, t * S + h * P:t * S + (h + 1) * P],
                                  pt[:, t * P:(t + 1) * P], start=(t == 0), stop=(t == 1))
                    return last

                heads(l * NT * ATT, NT * ATT, logits, values, lambda x: x // ATT + 1 if x % ATT < HEADS else N_MEM // P, lg, pT)
                pe.wait_ge(att_done, l * NT + NT)
                alone(pe)
                with pe.Fori(0, 3) as n:
                    for q in range(2):
                        for d in range(4):
                            c = (l * 3 + n) * 8 + 4 * q + d
                            u6 = 3 * (d // 2) + d % 2
                            j = 17 + 3 * q + u6 // 2
                            w = pair(j, l, n, 2)
                            pe.wait_ge(gate_free, c + 1)
                            for k in range(KC):
                                last = mm(pb[2 + d % 2][:], unit(w, u6 % 2, k), grp(xT, k), start=(k == 0), stop=(k == KC - 1))
                                if k == 0 and u6 % 2 == 0:
                                    last.then_inc(slot_free, 1)
                            last.then_inc(gate_ready, 1)
                            if d % 2:
                                ub = 3 * (d // 2) + 2
                                w = pair(17 + 3 * q + ub // 2, l, n, 2)
                                for e in range(2):
                                    pe.wait_ge(br_free, c + e)
                                    for k in range(4):
                                        last = mm(pb[4 + e][:], unit(w, ub % 2, e * 4 + k), grp(big, n * 4 + k), start=(k == 0), stop=(k == 3))
                                        if k == 0 and e == 0 and ub % 2 == 0:
                                            last.then_inc(slot_free, 1)
                                    last.then_inc(br_ready, 1)
                def route_tile(t):
                    pe.wait_ge(xT_ready, 2 * l * KC + 2 * (t + 1) + 1)
                    alone(pe)
                    for k in range(KC):
                        last = mm(pb[4][:, t * N_EXP:(t + 1) * N_EXP], xT[:, k * S + t * P:k * S + (t + 1) * P],
                                  w_router[:, k * N_EXP:(k + 1) * N_EXP], start=(k == 0), stop=(k == KC - 1))
                    return last

                pe.wait_ge(merged_ready, (l + 1) * 24)
                for n in range(2):
                    for j in range(2):
                        w = pair(35 + 2 * n + j, l)
                        for x in range(4 * NT):
                            t, k = (x // 4, x % 4) if j else (x % NT, x // NT)
                            last = mm(pb[4 * n + t][:], merged[:, (4 * j + k) * S + t * P:(4 * j + k) * S + (t + 1) * P],
                                      w[:, k * S:(k + 1) * S], start=(j == 0 and k == 0), stop=(j == 1 and k == 3))
                            if x == 0:
                                last.then_inc(slot_free, 1)
                            if j == 1 and k == 3:
                                last.then_inc(mix_ready, 1)
                                if n == 1 and t >= 1:
                                    transpose_tile(2 * l, t - 1)
                                if n == 1 and t >= 2:
                                    route_tile(t - 2)
                route_tile(NT - 2)
                transpose_tile(2 * l, NT - 1)
                route_tile(NT - 1).then_inc(sc_ready, 1)
                pe.wait_ge(pick_ready, l + 1)
                for t in range(NT):
                    for u in range(t + 1):
                        last = mm(pb[1][:, t * N_EXP:(t + 1) * N_EXP], tri if u == t else ones,
                                  r_pick[:, u * N_EXP:(u + 1) * N_EXP], start=(u == 0), stop=(u == t))
                for t in range(NT):
                    mm(pb[2][:, 0:N_EXP], ones, r_pick[:, t * N_EXP:(t + 1) * N_EXP], start=(t == 0), stop=(t == NT - 1))
                mm(pb[2][:, P:2 * P], ones, tri, start=True, stop=True).then_inc(rank_ready, 1)

                def transpose_xs(s, use):
                    pe.wait_ge(xs_loaded[s], 16 * (l * IN_OF + use + 1))
                    for k in range(KC):
                        last = nc.tensor.transpose(pb[4 + k // 4][:, k % 4 * P:(k % 4 + 1) * P], xs[s][:, k * P:(k + 1) * P], identity)
                    last.then_inc(xs_tr, 1)

                def up(b, s, j0, i=0, per=1):
                    pe.wait_ge(xsT_ready, l * N_BLK + b + 1)
                    for m in range(2):
                        for j in range(2):
                            w = pair(j0 + 2 * m + j, l, i, per)
                            for k in range(4):
                                c = 4 * j + k
                                last = mm(pb[m][:], xsT[s][:, c * P:(c + 1) * P], w[:, k * S:(k + 1) * S], start=(c == 0), stop=(c == KC - 1))
                                if k == 0:
                                    last.then_inc(slot_free, 1)
                        last.then_inc(up_ready, 1)

                def turn(b):
                    pe.wait_ge(hid_ready, l * N_BLK + b + 1 + 1)
                    for c in range(4):
                        last = nc.tensor.transpose(pb[6][:, c * P:(c + 1) * P], hid[:, c * P:(c + 1) * P], identity)
                    last.then_inc(ht_ready, 1)

                def down(b, j0, i=0, per=1):
                    pe.wait_ge(hT_ready, l * N_BLK + b + 1)
                    pe.wait_ge(y_copied, 2 * (l * N_BLK + b) + 1)
                    for j in range(2):
                        w = pair(j0 + j, l, i, per)
                        for k in range(4):
                            last = mm(pb[2 + j][:], hT[:, k * P:(k + 1) * P], w[:, k * S:(k + 1) * S], start=(k == 0), stop=(k == 3))
                            if k == 0:
                                last.then_inc(slot_free, 1)
                    last.then_inc(y_ready, 1)

                M0, per = LAYER_STREAM + UP_PAIRS, 2 * MOE_PAIRS // SLOTS
                pe.wait_ge(tok_done, 2 * l + 2)
                pe.wait_ge(sel_ready, l + 1)
                for c in range(KC):
                    for t in range(NT):
                        last = mm(pb[4 + c // 4][:, c % 4 * P:(c % 4 + 1) * P], xtok[:, t * D + c * P:t * D + (c + 1) * P],
                                  sel[:, t * P:(t + 1) * P], start=(t == 0), stop=(t == NT - 1))
                last.then_inc(xs_tr, 1)
                up(0, 0, LAYER_STREAM)
                transpose_xs(1, 0)
                pe.wait_ge(last_picked, l + 1)
                for t in range(NT):
                    last = nc.tensor.transpose(pb[7][:, t * P:(t + 1) * P], last_sel[:, t * P:(t + 1) * P], identity)
                last.then_inc(last_turned, 1)
                turn(0)
                with pe.Fori(0, N_BLK // 2 - 1) as i:
                    for s in range(2):
                        b = i * 2 + s + 1
                        up(b, 1 - s, M0 + s * MOE_PAIRS, i, per)
                        transpose_xs(s, i + s)
                        down(b - 1, M0 + s * MOE_PAIRS + UP_PAIRS, i, per)
                        turn(b)
                up(N_BLK - 2, 1, M0, N_BLK // 2 - 1, per)
                transpose_xs(0, IN_OF - 1)
                down(N_BLK - 3, M0 + UP_PAIRS, N_BLK // 2 - 1, per)
                turn(N_BLK - 2)
                at = M0 + (N_BLK - 2) * MOE_PAIRS
                down(N_BLK - 2, at)
                up(N_BLK - 1, 0, at + 2)
                turn(N_BLK - 1)
                down(N_BLK - 1, at + 2 + UP_PAIRS)

                def last_tile(t):
                    if t >= 2:
                        pe.wait_ge(last_added, l * NT + t - 1)
                        alone(pe)
                    for c in range(2):
                        last = mm(pb[4 + 2 * (t % 2) + c][:], last_selT[:, t * P:(t + 1) * P], ysb[0][:, c * S:(c + 1) * S], start=True, stop=True)
                    last.then_inc(last_summed, 1)

                pe.wait_ge(last_copied, l + 1)
                pe.wait_ge(y_copied, 2 * (l + 1) * N_BLK + 1)
                for t in range(3):
                    last_tile(t)
                transpose_tile(2 * l + 1, 0)
                last_tile(3)
                for t in range(1, NT):
                    transpose_tile(2 * l + 1, t)

            def rms(m):
                pe.wait_ge(sq_summed, m + 1)
                mm(pb[7][:], ones, sq_sum, start=True, stop=True).then_inc(ss_ready, 1)

            def feed_forward(n, j0):
                xn = xns[2 * n]

                def half(w, f, s, first=False):
                    pe.wait_ge(ff_free, n * FC + f + 1)
                    for u in range(2):
                        for k in range(KC):
                            if first and u == 0:
                                pe.wait_ge(xn_ready, 2 * n * KC + k + 1)
                            last = mm(pb[3 * u + s][:], unit(w, u, k), xn[:, k * S:(k + 1) * S], start=(k == 0), stop=(k == KC - 1))
                            if u == 0 and k == 0:
                                last.then_inc(slot_free, 1)
                    last.then_inc(ff_ready, 1)

                half(pair(j0), 0, 0, True)
                with pe.Fori(0, FC // 3) as i:
                    for s in range(1, 4):
                        half(pair(j0 + s, None, i), i * 3 + s, s % 3)
                pe.wait_ge(ff_free, (n + 1) * FC + 3)
                if n == 0:
                    pe.wait_ge(oh_loaded, 16)
                    for c in range(2):
                        last = mm(pb[c][0:HEADS, :], rel_b[:, :], rel_oh[:, c * S:(c + 1) * S], start=True, stop=True)
                    last.then_inc(rel_ready, 1)
                with pe.Fori(0, 4) as i:
                    for g in range(2):
                        d = n * KC + i * 2 + g
                        pe.wait_ge(dn_free, d + 1)
                        for c in range(FC):
                            u = 3 * g + c // KC
                            opens = c % KC == 0 and u % 2 == 0
                            if c == 0 or opens:
                                w = pair(j0 + FC + u // 2, None, i)
                            last = mm(pb[6 + g][:], unit(w, u % 2, c % KC), grp(big, c), start=(c == 0), stop=(c == FC - 1))
                            if opens:
                                last.then_inc(slot_free, 1)
                        last.then_inc(dn_ready, 1)
                pe.wait_ge(dn_free, (n + 1) * KC + 2)

            pe.wait_ge(xT_ready, 4 * KC + 1)
            rms(0)
            feed_forward(0, 0)
            rms(1)
            pe.wait_ge(rel_copied, 2)
            for g in range(N_H):
                linear(pair(34 + g // 2), g % 2, xns[1], DEPTH * LIN_LAYER + g, g % 2, norm=1 if g == 0 else None)
                c = g - 4
                if 0 <= c < N_NORM:
                    pe.wait_ge(nsq_ready, c + 1)
                    if c >= 4:
                        pe.wait_ge(nsum_used, c - 3)
                    mm(pb[2 + c % 4][:], ones if c < 8 else block_ones, nsq[c % 2], start=True, stop=True).then_inc(nsum_ready, 1)
            pe.wait_ge(lin_free, DEPTH * LIN_LAYER + N_H + 2)
            pe.wait_ge(nsum_used, N_NORM)
            for n in range(NCH):
                for r in range(2):
                    last = mm(pb[0][r * CH:(r + 1) * CH, n * 16:(n + 1) * 16], big[0:16, H_AB * S + n * CH:H_AB * S + (n + 1) * CH],
                              identity[0:16, 0:16], start=True, stop=True)
            last.then_inc(ab_tr, 1)
            for t in range(NT):
                for c in range(4):
                    last = nc.tensor.transpose(pb[4 + t][:, c * P:(c + 1) * P], big[:, (H_SV + c) * S + t * P:(H_SV + c) * S + (t + 1) * P], identity)
            last.then_inc(v2_tr, 1)
            pe.wait_ge(g_ready, 1)
            for r in range(2):
                h2 = slice(r * CH, (r + 1) * CH)
                last = mm(cut(pb[1][h2, 0:NCH * GH], GH), gtri[h2, :], cut(ga[h2, :], UN)[:, :, r * GH:(r + 1) * GH], start=True, stop=True)
            last.then_inc(gc_ready, 1)
            pe.wait_ge(gc_done, 1)
            pe.wait_ge(v2_ready, 1)
            pe.wait_ge(n_done, 2)
            pe.wait_ge(hank_loaded, 16)
            A0 = DEPTH * NT * ATT
            with pe.Fori(0, NT) as b:
                pe.wait_ge(staged, b + 1)

                def logits2(h, bank):
                    r = 64 * (h % 2)
                    mm(bank[:], q2_b[r:r + 64, h // 2 * P:(h // 2 + 1) * P],
                       big[r:r + 64, (H_SK + h // 2) * S:(H_SK + h // 2 + 1) * S], start=True, stop=False)
                    return mm(bank[:], reverse, hank[:, bass.ds(h * 896 + (NT - 1) * P - b * P, S)], start=False, stop=True)

                def values2(h, pt):
                    r = 64 * (h % 2)
                    for t in range(NT):
                        last = mm(pb[4][r:r + 64, h // 2 * P:(h // 2 + 1) * P], v2[:, t * S + h * 64:t * S + (h + 1) * 64],
                                  pt[:, t * P:(t + 1) * P], start=(t == 0), stop=(t == NT - 1))
                    return last

                heads(A0 + b * HEADS, HEADS, logits2, values2, lambda h: NT, lg2, pT2)
            pe.wait_ge(att_done, DEPTH * NT + NT)
            UNITS = [(r, h) for r in range(2) for h in range(GH)]

            def blk(t, r, h, w=CH, c0=0):
                return t[r * CH:(r + 1) * CH, c0 + h * w:c0 + (h + 1) * w]

            def u64(t, r, h):
                u = r * GH + h
                return t[:, u * CH:(u + 1) * CH]

            def u128(t, r, h):
                u = r * GH + h
                return t[:, u * P:(u + 1) * P]

            def turn_chunk(n):
                pe.wait_ge(g_staged, n + 1)
                alone(pe)
                for bank, t in ((2, ks), (3, vs)):
                    for r, h in UNITS:
                        mm(blk(pb[bank], r, h, P), u64(t, r, h), identity, start=True, stop=True)

            def chunk_products(n):
                pe.wait_ge(g_diag, n + 1)
                alone(pe)
                for c0, t in ((0, ks), (LW, qs)):
                    for r, h in UNITS:
                        mm(blk(pb[0], r, h, CH, c0), u64(ks, r, h), u64(t, r, h), start=True, stop=True)
                for bank, t in ((4, dg), (1, db)):
                    for r in range(2):
                        mm(pb[bank][:, r * LW:(r + 1) * LW], half_ones[:, r * P:(r + 1) * P], t, start=True, stop=True)
                mm(pb[5][:, 0:LW], block_ones, dg, start=True, stop=True)
                mm(pb[5][:, LW:2 * LW], block_ones, db, start=True, stop=True).then_inc(g_rows, 1)

            def level(n, q, both):
                for g in range(2):
                    pe.wait_ge(g_tm, (n * LEVELS + q) * 2 + g + 1)
                    alone(pe)
                    for r in range(2):
                        for h in (2 * g, 2 * g + 1):
                            last = mm(blk(pb[g], r, h), blk(lbT, r, h), blk(Tm, r, h), start=True, stop=True)
                    last.then_inc(g_a, 1)
                for g in range(2):
                    pe.wait_ge(g_am, (n * (LEVELS - 1) + q) * 2 + g + 1)
                    alone(pe)
                    for r in range(2):
                        for h in (2 * g, 2 * g + 1):
                            if both:
                                mm(blk(pb[4 + g], r, h), blk(Mm, r, h), blk(Am, r, h), start=True, stop=True)
                            last = mm(blk(pb[4 + g], r, h, CH, LW), blk(Am, r, h), blk(Mm, r, h), start=True, stop=True)
                    last.then_inc(g_up, 1)

            def chunk(n, par, more):
                pe.wait_ge(g_mats, n + 1)
                alone(pe)
                for g in range(2):
                    for r in range(2):
                        for h in (2 * g, 2 * g + 1):
                            last = mm(blk(pb[4 + g], r, h), blk(lbT, r, h), id_pair[r * CH:(r + 1) * CH, :], start=True, stop=True)
                    last.then_inc(g_up, 1)
                with pe.Fori(0, LEVELS - 2) as q:
                    level(n, q, True)
                level(n, LEVELS - 2, False)
                pe.wait_ge(g_state, n + 1)
                alone(pe)
                if more:
                    turn_chunk(n + 1)
                pe.wait_ge(g_o, n + 1)
                alone(pe)
                for r, h in UNITS:
                    last = mm(blk(pb[6], r, h, P), u64(kbF, r, h), u128(st[par], r, h), start=True, stop=True)
                last.then_inc(g_r, 1)
                pe.wait_ge(g_tm, (n + 1) * LEVELS * 2)
                alone(pe)
                if more:
                    chunk_products(n + 1)
                pe.wait_ge(g_rsub, n + 1)
                alone(pe)
                for r, h in UNITS:
                    last = mm(blk(pb[7], r, h, P), blk(Mm, r, h), blk(resid, r, h, P), start=True, stop=True)
                last.then_inc(g_vnm, 1)
                pe.wait_ge(g_vn, n + 1)
                alone(pe)
                for r, h in UNITS:
                    o = pb[6 + r][:, h * CH:(h + 1) * CH]
                    mm(o, u128(st[par], r, h), u64(qg[par], r, h), start=True, stop=False)
                    mm(o, blk(vn, r, h, P), blk(inT[par], r, h), start=False, stop=True)
                if more:
                    pe.wait_ge(g_kv_used, n + 2)
                    alone(pe)
                for r, h in UNITS:
                    last = mm(pb[2 + r][:, h * P:(h + 1) * P], blk(kdec[par], r, h, P), blk(vn, r, h, P), start=True, stop=True)
                last.then_inc(g_out, 1)

            turn_chunk(0)
            chunk_products(0)
            with pe.Fori(0, NCH // 2 - 1) as i:
                for par in range(2):
                    chunk(i * 2 + par, par, True)
            chunk(NCH - 2, 0, True)
            chunk(NCH - 1, 1, False)
            for h in range(GH):
                pe.wait_ge(o_sq, h + 1)
                mm(pb[2 + h][:], ones, sq2[h % 2], start=True, stop=True).then_inc(o_ss, 1)
            def project(first, half, groups):
                for d in groups:
                    w = pair(49 + 2 * half + d // 4)
                    for k in range(4):
                        last = mm(pb[OUT_BANKS[d]][:], w[:, (d % 4 * 4 + k) * P:(d % 4 * 4 + k + 1) * P], grp(cat, 4 * (1 - half) + k),
                                  start=(first and k == 0), stop=(not first and k == 3))
                        if k == 0 and d % 4 == 0:
                            last.then_inc(slot_free, 1)
                    if not first:
                        last.then_inc(lin_ready, 1)

            pe.wait_ge(g_o, NCH + 1)
            project(True, 0, range(4))
            pe.wait_ge(o_var, 1)
            project(True, 0, range(4, 8))
            pe.wait_ge(o_done, 1)
            project(False, 1, range(8))
            pe.wait_ge(lin_free, DEPTH * LIN_LAYER + N_H + KC + 2)
            rms(2)
            feed_forward(1, 53)
            rms(3)

        @block.scalar
        def _(act):
            fn = nc.scalar.activation

            def heads(n0, count, width, buf_p, buf_pT, result=None):
                for step in range(count + 2):
                    if step < count:
                        h = step
                        act.wait_ge(lg_masked, n0 + h + 1)
                        fn(buf_p[h % 3][:, 0:width(h)], buf_p[h % 3][:, 0:width(h)], ACT.Exp, scale=-1.0,
                           bias=stat[:, 8 + h % 3:9 + h % 3], accum_out=stat[:, 16 + h % 3:17 + h % 3]).then_inc(exp_done, 1)
                    if step >= 2:
                        h = step - 2
                        act.wait_ge(tr_ready, n0 + h + 1)
                        if h >= 2:
                            act.wait_ge(pv_ready, n0 + h - 1)
                        fn(buf_pT[h % 2][:, 0:width(h)], pb[2 + h % 2][:, 0:width(h)], ACT.Copy).then_inc(pT_ready, 1)
                    if result and step >= 4:
                        result(step - 4)
                if result:
                    for h in range(count - 2, count):
                        result(h)

            def norm_rows(m):
                fn(primed, ones[:, 0:1], ACT.Sqrt)
                for t in range(NT + 1):
                    if t < NT:
                        x = grp(xtok, t, 1, D)
                        act.wait_ge(var_ready, m * NT + t + 1)
                        alone(act)
                        fn(ln_mv[:, 12 + t:13 + t], ln_mv[:, 8 + t:9 + t], ACT.Sqrt).then_inc(std_ready, 1)
                        act.wait_ge(shift_ready, m * NT + t + 1)
                        alone(act)
                        fn(x, x, ACT.Identity, scale=ln_mv[:, 8 + t:9 + t], bias=ln_mv[:, 16 + t:17 + t]).then_inc(normed, 1)
                    if t >= 1:
                        act.wait_ge(xtr_ready, m * NT + t)
                        alone(act)
                        for k in range(KC):
                            last = fn(xT[:, k * S + (t - 1) * P:k * S + t * P], pb[2 * ((t - 1) % 2) + k // 4][:, k % 4 * P:(k % 4 + 1) * P],
                                      ACT.Identity, scale=ln_T[:, bass.ds(m * 2 * KC + k, 1)], bias=ln_T[:, bass.ds(m * 2 * KC + KC + k, 1)])
                            if k % 4 == 3:
                                last.then_inc(xT_ready, 1)

            for dst, src in ROPE_CONSTS:
                act.dma_start(dst, src).then_inc(rope_loaded, 16)
            for dst, src in CONSTS:
                act.dma_start(dst, src).then_inc(loaded, 16)
            act.wait_ge(w_loaded[0], 16)
            act.dma_start(xT[:, :], a["xT"]).then_inc(x_loaded, 16)
            act.wait_ge(rope_arg, 1)
            fn(sin_t[:, :], relu2[0], ACT.Sin)
            fn(cos_t[:, :], relu2[1], ACT.Sin).then_inc(rope_sin, 1)

            act.wait_ge(loaded, N_CONST)
            with act.Fori(0, DEPTH) as l:
                for n in range(MEM_GROUPS):
                    act.wait_ge(lin_ready, l * LIN_LAYER + n + 1)
                    dst = mk if n < 4 else mvf
                    fn(dst[:, n % 4 * N_MEM:(n % 4 + 1) * N_MEM], pb[n % 2][:, 0:N_MEM], ACT.Copy).then_inc(lin_free, 1)
                L0 = l * LIN_LAYER + MEM_GROUPS
                act.wait_ge(tok_done, 2 * l + 1)
                alone(act)
                for p in range(N_G):
                    act.wait_ge(lin_ready, L0 + p + 1)
                    fn(grp(big, ORDER[p]), pb[p % 2][:], ACT.Identity, bias=bias_p[:, bass.ds(l * N_G + ORDER[p], 1)]).then_inc(lin_free, 1)
                    if p == AT_MV:
                        act.wait_ge(vt_ready, 3 * l + 1)
                        alone(act)
                        for t in range(2):
                            last = fn(mv[:, t * S:(t + 1) * S], pb[6 + t][:], ACT.Copy)
                        last.then_inc(vt_copied, 1)
                    if p == AT_IW:
                        act.wait_ge(vt_ready, 3 * l + 2)
                        fn(iw_tok[:, :], pb[6][:, 0:NT * 8], ACT.Copy, scale=float(HEADS ** -0.5 * HEAD_DIM ** -0.5)).then_inc(vt_copied, 1)
                    if p in AT_SCORE:
                        for h in range(HEADS):
                            n = (l * N_TOP + AT_SCORE[p] - 1) * HEADS + h
                            act.wait_ge(idx_ready, n + 1)
                            if h >= 2 or AT_SCORE[p] > 1:
                                act.wait_ge(idx_used, n - 1)
                            alone(act)
                            w = keys(AT_SCORE[p])
                            fn(relu2[h % 2][:, 0:w], pb[6 + h % 2][:, 0:w], ACT.Relu).then_inc(idx_copied, 1)
                    if p == AT_VT:
                        act.wait_ge(vt_ready, 3 * l + 3)
                        alone(act)
                        for t in range(NT):
                            last = fn(vtok[:, t * S:(t + 1) * S], pb[4 + t][:], ACT.Copy)
                        last.then_inc(vt_copied, 1)
                for g in range(4):
                    act.wait_ge(pool_mixed, l * 4 + g + 1)
                    last = fn(grp(big, G_POOL + g), pb[4 + g][:], ACT.Copy, scale=pool_scale[:, bass.ds(l * 4 + g, 1)])
                last.then_inc(pool_done, 1)
                act.drain()

                def result(x):
                    b, h = divmod(x, ATT)
                    if h in (HEADS - 1, ATT - 1):
                        act.wait_ge(pv_ready, l * NT * ATT + x + 1)
                        alone(act)
                        g, bank, done = (G_Q, 4, sparse_done) if h < HEADS else (G_MQ, 5, att_done)
                        fn(cut(grp(big, g, 4), S)[:, :, b * P:(b + 1) * P], cut(pb[bank][:], P), ACT.Copy).then_inc(done, 1)

                heads(l * NT * ATT, NT * ATT, lambda x: keys(x // ATT) if x % ATT < HEADS else N_MEM,
                      lg, pT, result)
                with act.Fori(0, 12) as i:
                    for u in range(2):
                        c = l * 24 + i * 2 + u
                        act.wait_ge(gate_ready, c + 1)
                        act.wait_ge(br_free, c + 1)
                        fn(relu2[u], pb[2 + u][:], ACT.Sigmoid, bias=bias_g[:, bass.ds(c, 1)]).then_inc(gate_free, 1)
                norm_rows(2 * l)
                fn(primed, ones[:, 0:1], ACT.Sigmoid)
                act.wait_ge(sc_ready, l + 1)
                fn(r_score, pb[4][:, 0:NT * N_EXP], ACT.Sigmoid).then_inc(sig_ready, 1)

                def copy_xsT(b, s):
                    act.wait_ge(xs_tr, l * N_BLK + b + 1)
                    for k in range(2):
                        last = fn(xsT[s][:, k * S:(k + 1) * S], pb[4 + k][:], ACT.Copy)
                    last.then_inc(xsT_ready, 1)

                def gate_half(b):
                    act.wait_ge(up_ready, 2 * (l * N_BLK + b) + 1)
                    act.wait_ge(hid_ready, l * N_BLK + b + 1)
                    fn(sil, pb[0][:], ACT.Silu).then_inc(sil_ready, 1)

                def copy_hT(b):
                    act.wait_ge(ht_ready, l * N_BLK + b + 1 + 1)
                    fn(hT, pb[6][:], ACT.Copy).then_inc(hT_ready, 1)

                def copy_y(b, s, use):
                    act.wait_ge(y_ready, l * N_BLK + b + 1)
                    act.wait_ge(y_stored[s], 16 * (l * OUT_OF + use) + 16)
                    fn(ysb[s][:, 0:S], pb[2][:], ACT.Copy).then_inc(y_copied, 1)

                copy_xsT(0, 0)
                gate_half(0)
                copy_xsT(1, 1)
                act.wait_ge(last_turned, l + 1)
                fn(last_selT, pb[7][:], ACT.Copy).then_inc(last_copied, 1)
                copy_hT(0)
                with act.Fori(0, N_BLK // 2 - 1) as i:
                    for s in range(2):
                        b = i * 2 + s + 1
                        gate_half(b)
                        copy_xsT(b + 1, s)
                        copy_y(b - 1, s, i)
                        copy_hT(b)
                gate_half(N_BLK - 2)
                copy_xsT(N_BLK - 1, 0)
                copy_y(N_BLK - 3, 0, OUT_OF - 1)
                copy_hT(N_BLK - 2)
                copy_y(N_BLK - 2, 1, OUT_OF - 1)
                gate_half(N_BLK - 1)
                copy_hT(N_BLK - 1)
                copy_y(N_BLK - 1, 0, OUT_OF)
                norm_rows(2 * l + 1)

            def rms(m, source=None, n0=0):
                fn(primed, ones[:, 0:1], ACT.Sqrt)
                act.drain()
                for k in range(KC):
                    if source:
                        act.wait_ge(source, n0 + k + 1)
                    if k >= 3:
                        act.wait_ge(sq_used, m * (KC - 2) + k - 2)
                    fn(sq2[k % 2] if k else sq_sum, grp(xT, k), ACT.Square).then_inc(sq_ready, 1)
                act.wait_ge(rvar, m + 1)
                fn(rs, rs, ACT.Sqrt).then_inc(rstd, 1)

            def feed_forward(n):
                def half(f, s):
                    act.wait_ge(ff_ready, n * FC + f + 1)
                    fn(sgl[s], pb[s][:], ACT.Silu).then_inc(ff_silu, 1)

                with act.Fori(0, FC // 3) as i:
                    for s in range(3):
                        half(i * 3 + s, s)
                half(FC - 1, 0)

            act.wait_ge(xT_ready, 4 * KC + 1)
            rms(0)
            feed_forward(0)
            act.wait_ge(rel_ready, 1)
            for c in range(2):
                fn(rel_row[:, c * S:(c + 1) * S], pb[c][0:HEADS, :], ACT.Copy).then_inc(rel_copied, 1)
            rms(1, dn_free, 2)
            for g in range(N_H):
                act.wait_ge(lin_ready, DEPTH * LIN_LAYER + g + 1)
                fn(grp(big, g), pb[g % 2][:], ACT.Copy).then_inc(lin_free, 1)
                if g - 2 in CONV_GROUPS:
                    c = CONV_GROUPS.index(g - 2)
                    act.wait_ge(conv_ready, c + 1)
                    fn(grp(big, g - 2), ctmp[c % 2], ACT.Silu).then_inc(conv_silu, 1)
                c = g - 3
                if 0 <= c < N_NORM:
                    act.drain()
                    if c >= 2:
                        act.wait_ge(nsum_ready, c - 1)
                    fn(nsq[c % 2], grp(big, c), ACT.Square).then_inc(nsq_ready, 1)
                if g in (13, 21):
                    n = (g - 13) // 8
                    act.wait_ge(nsum_used, (n + 1) * 8)
                    fn(nrm, nrm, ACT.Sqrt).then_inc(nstd, 1)
            act.drain()
            act.wait_ge(ab_ready, 1)
            fn(gbeta[:, :], gbeta[:, :], ACT.Sigmoid)
            fn(ga[:, :], ga[:, :], ACT.Exp, scale=-1.0)
            act.drain()
            fn(ga[:, :], ga[:, :], ACT.Ln, bias=1.0)
            fn(alog[:, :], alog[:, :], ACT.Exp).then_inc(sp_ready, 1)
            act.wait_ge(v2_tr, 1)
            for t in range(NT):
                last = fn(v2[:, t * S:(t + 1) * S], pb[4 + t][:], ACT.Copy)
            last.then_inc(v2_ready, 1)
            act.wait_ge(n_done, 2)
            act.wait_ge(lnw_loaded, 16)
            A0 = DEPTH * NT * ATT
            with act.Fori(0, NT) as b:
                fn(lnw_b, lnw[:, bass.ds(b * S, S)], ACT.Copy)
                fn(cut(q2_b, P), cut(grp(big, H_SQ, 4), S)[:, :, bass.ds(b * P, P)], ACT.Copy).then_inc(staged, 1)
                heads(A0 + b * HEADS, HEADS, lambda h: S, lg2, pT2)
                act.wait_ge(pv_ready, A0 + (b + 1) * HEADS)
                alone(act)
                fn(cut(cat[:, 4 * S:8 * S], S)[:, :, bass.ds(b * P, P)], cut(pb[4][:], P), ACT.Copy).then_inc(att_done, 1)

            def back(n):
                return (NCH - 1) * CH - n * CH

            def place(n, r):
                at = n * CH if r == 0 else back(n)
                return slice(at, at + CH) if isinstance(at, int) else bass.ds(at, CH)

            def stage(n):
                for dst, g in ((ks, H_K), (qs, H_Q), (vs, H_V)):
                    for r in range(2):
                        last = fn(cut(dst, CH)[:, r * GH:(r + 1) * GH, :], cut(grp(big, g, 4), S)[:, :, place(n, r)], ACT.Copy)
                last.then_inc(g_staged, 1)

            def exps(n, par):
                act.wait_ge(g_rows, n + 1)
                alone(act)
                fn(eg, pb[4][:], ACT.Exp)
                fn(gl[:, 0:GH].unsqueeze(2), cut(pb[4][:], CH)[:, 0:GH, CH - 1:CH], ACT.Copy)
                fn(gl[:, GH:UN].unsqueeze(2), cut(pb[4][:], CH)[:, GH:UN, 0:1], ACT.Copy)
                act.drain()
                fn(egl[par][:, :], gl[:, :], ACT.Exp).then_inc(g_eg, 1)

            def decays(n):
                act.wait_ge(g_diff, n + 1)
                alone(act)
                fn(dT, dT, ACT.Exp)
                fn(dfac[:, :], dfac[:, :], ACT.Exp).then_inc(g_dexp, 1)

            def chunk(n, par, more):
                if more:
                    act.wait_ge(g_mats, n + 1)
                    alone(act)
                    stage(n + 1)
                with act.Fori(0, LEVELS - 1) as q:
                    for g in range(2):
                        act.wait_ge(g_a, (n * (LEVELS - 1) + q) * 2 + g + 1)
                        alone(act)
                        half = slice(g * LW // 2, (g + 1) * LW // 2)
                        fn(Am[:, half], pb[g][:, half], ACT.Copy).then_inc(g_am, 1)
                if more:
                    exps(n + 1, 1 - par)
                act.wait_ge(g_vnm, n + 1)
                alone(act)
                fn(vn, pb[7][:], ACT.Copy).then_inc(g_vn, 1)
                if more:
                    decays(n + 1)
                act.wait_ge(g_out, n + 1)
                alone(act)
                fn(cut(of, S)[:, :, place(n, 0)], cut(pb[6][:, 0:LW], CH), ACT.Copy)
                fn(cut(ob, S)[:, :, place(n, 1)], cut(pb[7][:, 0:LW], CH), ACT.Copy).then_inc(g_o, 1)

            stage(0)
            exps(0, 0)
            decays(0)
            fn(grp(big, H_Z, 4), grp(big, H_Z, 4), ACT.Silu)
            with act.Fori(0, NCH // 2 - 1) as i:
                for par in range(2):
                    chunk(i * 2 + par, par, True)
            chunk(NCH - 2, 0, True)
            chunk(NCH - 1, 1, False)
            act.wait_ge(o_sum, 1)
            for h in range(GH):
                if h >= 2:
                    act.wait_ge(o_ss, h - 1)
                fn(sq2[h % 2], grp(cat, h), ACT.Square).then_inc(o_sq, 1)
            act.wait_ge(o_var, 1)
            fn(ob, ob, ACT.Sqrt).then_inc(o_std, 1)
            rms(2, lin_free, DEPTH * LIN_LAYER + N_H + 2)
            feed_forward(1)
            rms(3, dn_free, KC + 2)

        @block.vector
        def _(dve):
            v = nc.vector

            def heads(n0, count, prepare, width, buf_p):
                for step in range(count + 1):
                    if step < count:
                        h = step
                        dve.wait_ge(lg_ready, n0 + h + 1)
                        if h >= 3:
                            dve.wait_ge(tr_ready, n0 + h - 2)
                        alone(dve)
                        prepare(h, stat[:, 8 + h % 3:9 + h % 3]).then_inc(lg_masked, 1)
                    if step >= 1:
                        h = step - 1
                        r = stat[:, 24 + h % 3:25 + h % 3]
                        dve.wait_ge(exp_done, n0 + h + 1)
                        v.reciprocal(r, stat[:, 16 + h % 3:17 + h % 3])
                        dve.drain()
                        v.tensor_scalar(buf_p[h % 3][:, 0:width(h)], buf_p[h % 3][:, 0:width(h)], r, None, ALU.mult).then_inc(p_ready, 1)

            def row_stats(t, c):
                v.bn_stats(ln_st[:, t * 12 + c * 6:t * 12 + (c + 1) * 6], xtok[:, t * D + c * S:t * D + (c + 1) * S])

            def row_norm(m, t):
                dve.drain()
                v.bn_aggr(ln_mv[:, 2 * t:2 * t + 2], ln_st[:, t * 12:(t + 1) * 12])
                dve.drain()
                r = ln_mv[:, 8 + t:9 + t]
                v.tensor_scalar(r, ln_mv[:, 2 * t + 1:2 * t + 2], LN_EPS, None, ALU.add).then_inc(var_ready, 1)
                dve.wait_ge(std_ready, m * NT + t + 1)
                alone(dve)
                v.reciprocal(r, ln_mv[:, 12 + t:13 + t])
                dve.drain()
                v.tensor_scalar(ln_mv[:, 16 + t:17 + t], ln_mv[:, 2 * t:2 * t + 1], r, -1.0, ALU.mult, ALU.mult).then_inc(shift_ready, 1)

            dve.sem_inc(tok_done, 1)
            dve.wait_ge(rope_loaded, 16 * len(ROPE_CONSTS))
            ang, turns = score, lg[0]
            v.tensor_copy(ang, work.bitcast(I32))
            dve.drain()
            v.tensor_scalar(ang, ang, inv_freq[:, 0:1], None, ALU.mult)
            dve.drain()
            for c in range(2):
                v.tensor_scalar(turns, ang, 1.0 / TWO_PI, 0.25 * c, ALU.mult, ALU.add)
                dve.drain()
                v.tensor_scalar(turns, turns, ROUND, ROUND, ALU.add, ALU.subtract)
                dve.drain()
                r = relu2[c]
                v.scalar_tensor_tensor(out=r, in0=turns, scalar=-PI_A, in1=ang, op0=ALU.mult, op1=ALU.add)
                for part in (PI_B, PI_C):
                    dve.drain()
                    v.scalar_tensor_tensor(out=r, in0=turns, scalar=-part, in1=r, op0=ALU.mult, op1=ALU.add)
                dve.drain()
                if c:
                    v.tensor_scalar(r, r, TWO_PI / 4, None, ALU.add)
                    dve.drain()
                last = v.tensor_scalar(r, r, 3.1415925, -3.1415925, ALU.min, ALU.max)
            last.then_inc(rope_arg, 1)
            dve.wait_ge(rope_sin, 1)
            dve.wait_ge(loaded, N_CONST)

            with dve.Fori(0, DEPTH) as l:
                def rotate(n):
                    dve.wait_ge(rot_ready, l * N_ROT + n + 1)
                    alone(dve)
                    x = grp(big, ROT_GROUPS[n])
                    v.tensor_tensor(tmp[0], pb[2 + n % 4][:], sin_t[:, :], ALU.mult)
                    v.tensor_tensor(tmp[1], x, cos_t[:, :], ALU.mult)
                    dve.drain()
                    v.tensor_tensor(x, tmp[0], tmp[1], ALU.add).then_inc(rot_used, 1)
                    dve.drain()

                for n in range(ROT_IDX):
                    rotate(n)
                dve.wait_ge(adm_loaded, 16 * l + 16)
                dve.wait_ge(vt_copied, 3 * l + 2)
                alone(dve)
                for b in range(1, NT):
                    w = keys(b)
                    admb, sc, wk = adm[:, b * S:b * S + w], score[:, 0:w], work[:, 0:w]
                    for h in range(HEADS):
                        dve.wait_ge(idx_copied, (l * N_TOP + b - 1) * HEADS + h + 1)
                        alone(dve)
                        v.scalar_tensor_tensor(out=sc, in0=relu2[h % 2][:, 0:w], scalar=iw_tok[:, b * 8 + h:b * 8 + h + 1],
                                               in1=sc if h else admb, op0=ALU.mult, op1=ALU.add).then_inc(idx_used, 1)
                        dve.drain()
                    for r in range(N_SEL // 8):
                        v.max(top8[:, :], wk if r else sc)
                        dve.drain()
                        v.match_replace(out=wk, in_to_replace=top8[:, :], in_values=wk if r else sc, imm_value=LOWEST)
                        dve.drain()
                    v.tensor_tensor(wk, wk, sc, ALU.not_equal)
                    dve.drain()
                    v.tensor_scalar(wk, wk, 1.0, -BIG_NEG, ALU.subtract, ALU.mult)
                    dve.drain()
                    v.tensor_tensor(admb, wk, admb, ALU.add).then_inc(masks_ready, 1)
                    dve.drain()
                    if b < 3:
                        for n in range(ROT_IDX + 4 * (b - 1), ROT_IDX + 4 * b):
                            rotate(n)
                dve.wait_ge(lin_free, l * LIN_LAYER + MEM_GROUPS + ORDER.index(G_POOL + 3) + 1 + 2)
                alone(dve)
                for g in range(4):
                    x, src = grp(big, G_POOL + g), grp(big, G_POOL + g)
                    w = 1
                    for s in range(g + 1):
                        dst = tmp[s % 2]
                        v.tensor_tensor(dst[:, w:S], src[:, w:S], src[:, 0:S - w], ALU.add)
                        v.tensor_copy(dst[:, 0:w], src[:, 0:w])
                        dve.drain()
                        src, w = dst, 2 * w
                    v.tensor_tensor(src[:, 0:16], src[:, 0:16], pool_rec[:, g * 16:(g + 1) * 16], ALU.mult)
                    dve.drain()
                    v.tensor_tensor(work[:, 0:16], src[:, 0:16], x[:, 0:16], ALU.subtract)
                    v.scalar_tensor_tensor(out=x[:, 16:S], in0=src[:, 16:S], scalar=1.0 / w, in1=x[:, 16:S], op0=ALU.mult, op1=ALU.subtract)
                    dve.drain()
                    v.tensor_copy(x[:, 0:16], work[:, 0:16]).then_inc(pool_in, 1)
                    dve.drain()

                def prepare(x, low):
                    b, h = divmod(x, ATT)
                    bank = pb[LOGIT_BANKS[x % 3]]
                    if h < HEADS:
                        w = keys(b)
                        return v.tensor_tensor_reduce(out=lg[x % 3][:, 0:w], in0=bank[:, 0:w], in1=adm[:, b * S:b * S + w], scale=-HEAD_DIM ** -0.5,
                                                      scalar=-LOWEST, op0=ALU.add, op1=ALU.min, accum_out=low)
                    return v.tensor_scalar(lg[x % 3][:, 0:N_MEM], bank[:, 0:N_MEM], -MEM_DIM ** -0.5, None, ALU.mult, ALU.min, accum_out=low)

                heads(l * NT * ATT, NT * ATT, prepare, lambda x: keys(x // ATT) if x % ATT < HEADS else N_MEM, lg)
                dve.wait_ge(att_done, l * NT + NT)
                v.memset(merged, 0.0)
                dve.drain()
                with dve.Fori(0, 3) as n:
                    for d in range(8):
                        c = (l * 3 + n) * 8 + d
                        dve.wait_ge(br_ready, c + 1)
                        dve.wait_ge(gate_free, c + 3)
                        v.tensor_tensor(tmp[d % 2], pb[4 + d % 2][:], relu2[d % 2], ALU.mult).then_inc(br_free, 1)
                        dve.drain()
                        m = merged[:, d * S:(d + 1) * S]
                        v.tensor_tensor(m, m, tmp[d % 2], ALU.add).then_inc(merged_ready, 1)
                    dve.drain()
                dve.wait_ge(xtok_loaded, 16)
                dve.wait_ge(tok_done, 2 * l + 1)
                alone(dve)
                for n in range(2):
                    for t in range(NT):
                        dve.wait_ge(mix_ready, l * 2 * NT + n * NT + t + 1)
                        alone(dve)
                        x = xtok[:, t * D + n * S:t * D + (n + 1) * S]
                        v.scalar_tensor_tensor(out=x, in0=x, scalar=DN_ALPHA, in1=pb[4 * n + t][:], op0=ALU.mult, op1=ALU.add)
                        dve.drain()
                        row_stats(t, n)
                        if n == 1:
                            row_norm(2 * l, t)
                dve.wait_ge(sig_ready, l + 1)
                r4 = lambda t: t.rearrange("p (t g e) -> p (t g) e", t=NT, e=PER_GROUP)
                v.tensor_tensor(cut(r_biased, N_EXP), cut(r_score, N_EXP), r_bias[:, :].unsqueeze(1).to_broadcast([P, NT, N_EXP]), ALU.add)
                dve.drain()

                def ranks(rank, val, sets, c):
                    n4 = [P, sets, PER_GROUP, PER_GROUP]
                    cmp = lambda t: t[:, 0:sets * 16].rearrange("p (s x y) -> p s x y", x=PER_GROUP, y=PER_GROUP)
                    one, other = val.unsqueeze(3).to_broadcast(n4), val.unsqueeze(2).to_broadcast(n4)
                    v.tensor_tensor(cmp(c[0]), other, one, ALU.is_gt)
                    v.tensor_tensor(cmp(c[1]), other, one, ALU.is_equal)
                    dve.drain()
                    v.tensor_tensor(cut(c[1][:, 0:sets * 16], 16), cut(c[1][:, 0:sets * 16], 16), before[:, :].unsqueeze(1).to_broadcast([P, sets, 16]), ALU.mult)
                    dve.drain()
                    v.tensor_tensor(c[0][:, 0:sets * 16], c[0][:, 0:sets * 16], c[1][:, 0:sets * 16], ALU.add)
                    dve.drain()
                    v.tensor_reduce(rank, c[0][:, 0:sets * 16].rearrange("p (s x) -> p s x", x=PER_GROUP), AX.X, ALU.add)
                    dve.drain()

                ranks(r_rank, r4(r_biased), NT * GROUPS, r_cmp)
                v.tensor_scalar(r_pick, r_rank, 2.0, None, ALU.is_lt)
                dve.drain()
                v.tensor_tensor(r_t, r_pick, r_biased, ALU.mult)
                dve.drain()
                v.tensor_reduce(r_gsum, r4(r_t), AX.X, ALU.add)
                dve.drain()
                ranks(r_grank, cut(r_gsum, GROUPS), NT, r_cmp)
                v.tensor_scalar(r_gsum, r_grank, 0.0, None, ALU.is_equal)
                dve.drain()
                best = r_gsum.unsqueeze(2).to_broadcast([P, NT * GROUPS, PER_GROUP])
                v.tensor_tensor(r4(r_pick), r4(r_pick), best, ALU.mult).then_inc(pick_ready, 1)
                for k in range(2):
                    v.tensor_scalar(r_one[k], r_rank, float(k), None, ALU.is_equal)
                dve.drain()
                for k in range(2):
                    v.tensor_tensor(r4(r_one[k]), r4(r_one[k]), best, ALU.mult)
                dve.wait_ge(rank_ready, l + 1)
                v.tensor_scalar(r_end, pb[2][:, 0:N_EXP], 1.0 / MOE_BLOCK, None, ALU.mult)
                dve.drain()
                full = S // MOE_BLOCK
                some = cut(r_cmp[0][:, 0:N_EXP * full], full)
                v.tensor_tensor(some, r_end.unsqueeze(2).to_broadcast([P, N_EXP, full]), blk_iota[:, 0:full].unsqueeze(1).to_broadcast([P, N_EXP, full]), ALU.is_gt)
                v.memset(r_grank, 1.0)
                dve.drain()
                v.tensor_reduce(r_nblk, some, AX.X, ALU.add)
                dve.drain()
                v.tensor_tensor_scan(r_end, r_grank, r_nblk, 0.0, op0=ALU.mult, op1=ALU.add)
                dve.drain()
                v.tensor_tensor(r_nblk, r_end, r_nblk, ALU.subtract)
                dve.drain()
                v.tensor_scalar(r_nblk, r_nblk, float(MOE_BLOCK), None, ALU.mult)
                dve.drain()
                v.tensor_tensor(cut(r_t, N_EXP), cut(pb[1][:, 0:NT * N_EXP], N_EXP), r_nblk.unsqueeze(1).to_broadcast([P, NT, N_EXP]), ALU.add)
                dve.drain()
                for k in range(2):
                    v.tensor_tensor(r_u[k], r_one[k], r_t, ALU.mult)
                dve.drain()
                for k in range(2):
                    v.tensor_reduce(r_dest[:, k * NT:(k + 1) * NT], cut(r_u[k], N_EXP), AX.X, ALU.add)
                dve.drain()
                v.tensor_copy(dest[:, :], r_dest).then_inc(dest_ready, 1)
                ends = cut(r_cmp[1][:, 0:N_BLK * N_EXP], N_EXP)
                v.tensor_tensor(ends, blk_iota[:, :].unsqueeze(2).to_broadcast([P, N_BLK, N_EXP]), r_end.unsqueeze(1).to_broadcast([P, N_BLK, N_EXP]), ALU.is_ge)
                dve.drain()
                v.tensor_reduce(r_blk, ends, AX.X, ALU.add)
                dve.drain()
                v.tensor_scalar(r_blk, r_blk, float(N_EXP - 1), None, ALU.min)
                dve.drain()
                v.tensor_copy(blk_e[:, :], r_blk).then_inc(route_ready, 1)
                n3 = [P, NT, MOE_BLOCK]
                for k in range(2):
                    v.tensor_tensor(cut(work if k else sel, MOE_BLOCK), pb[2][:, P:P + MOE_BLOCK].unsqueeze(1).to_broadcast(n3),
                                    r_dest[:, k * NT:(k + 1) * NT].unsqueeze(2).to_broadcast(n3), ALU.is_equal)
                dve.drain()
                v.tensor_tensor(sel, sel, work, ALU.add).then_inc(sel_ready, 1)
                v.tensor_tensor(r_t, r_pick, r_score, ALU.mult)
                for k in range(2):
                    v.tensor_tensor(r_u[k], r_one[k], r_score, ALU.mult)
                dve.drain()
                v.tensor_reduce(r_sum, cut(r_t, N_EXP), AX.X, ALU.add)
                for k in range(2):
                    v.tensor_reduce(gate2[:, k * NT:(k + 1) * NT], cut(r_u[k], N_EXP), AX.X, ALU.add)
                dve.drain()
                v.reciprocal(r_sum, r_sum)
                dve.drain()
                for k in range(2):
                    v.tensor_tensor(gate2[:, k * NT:(k + 1) * NT], gate2[:, k * NT:(k + 1) * NT], r_sum, ALU.mult)
                v.tensor_scalar(r_last, r_dest, float(LAST), None, ALU.subtract)
                dve.drain()
                picked = [cut(last_sel, MOE_BLOCK), cut(lg[1], MOE_BLOCK)]
                over = lambda t, k: t[:, k * NT:(k + 1) * NT].unsqueeze(2).to_broadcast(n3)
                for k in range(2):
                    v.tensor_tensor(picked[k], pb[2][:, P:P + MOE_BLOCK].unsqueeze(1).to_broadcast(n3), over(r_last, k), ALU.is_equal)
                dve.drain()
                for k in range(2):
                    v.tensor_tensor(picked[k], picked[k], over(gate2, k), ALU.mult)
                dve.drain()
                v.tensor_tensor(last_sel, last_sel, lg[1], ALU.add).then_inc(last_picked, 1)
                v.tensor_scalar(r_last, r_last, 0.0, None, ALU.is_lt)
                dve.drain()
                v.tensor_tensor(gate2[:, :], gate2[:, :], r_last, ALU.mult)
                dve.drain()
                dve.wait_ge(xs_tr, l * N_BLK + 1)
                dve.wait_ge(tok_done, 2 * l + 2)
                dve.wait_ge(xs_scattered, l * 128 + 128)
                alone(dve)
                for t in range(NT):
                    x = grp(xtok, t, 1, D)
                    v.tensor_scalar(x, x, DN_ALPHA, None, ALU.mult)
                def hidden(b):
                    dve.wait_ge(up_ready, 2 * (l * N_BLK + b) + 2)
                    dve.wait_ge(sil_ready, l * N_BLK + b + 1)
                    dve.wait_ge(ht_ready, l * N_BLK + b + 1)
                    v.tensor_tensor(hid, pb[1][:], sil, ALU.mult).then_inc(hid_ready, 1)

                def copy_y(b, s, use):
                    dve.wait_ge(y_ready, l * N_BLK + b + 1)
                    dve.wait_ge(y_stored[s], 16 * (l * OUT_OF + use) + 16)
                    v.tensor_copy(ysb[s][:, S:D], pb[3][:]).then_inc(y_copied, 1)

                hidden(0)
                with dve.Fori(0, N_BLK // 2 - 1) as i:
                    for s in range(2):
                        hidden(i * 2 + s + 1)
                        copy_y(i * 2 + s, s, i)

                def add_gathered(t):
                    dve.wait_ge(y_back[t], 32 * l + 32)
                    x = grp(xtok, t, 1, D)
                    for k in range(2):
                        v.scalar_tensor_tensor(out=x, in0=yg[t][k], scalar=gate2[:, k * NT + t:k * NT + t + 1], in1=x, op0=ALU.mult, op1=ALU.add)
                        dve.drain()

                hidden(N_BLK - 2)
                copy_y(N_BLK - 3, 0, OUT_OF - 1)
                copy_y(N_BLK - 2, 1, OUT_OF - 1)
                hidden(N_BLK - 1)
                for t in range(2):
                    add_gathered(t)
                copy_y(N_BLK - 1, 0, OUT_OF)
                for t in range(2, NT):
                    add_gathered(t)
                for t in range(NT):
                    dve.wait_ge(last_summed, l * NT + t + 1)
                    alone(dve)
                    for c in range(2):
                        x = xtok[:, t * D + c * S:t * D + (c + 1) * S]
                        last = v.tensor_tensor(x, x, pb[4 + 2 * (t % 2) + c][:], ALU.add)
                    last.then_inc(last_added, 1)
                    dve.drain()
                    for c in range(2):
                        row_stats(t, c)
                    row_norm(2 * l + 1, t)

            def add_square(m, k):
                if k:
                    dve.wait_ge(sq_ready, m * KC + k + 1)
                    dve.drain()
                    v.tensor_tensor(sq_sum, sq_sum, sq2[k % 2], ALU.add).then_inc(sq_summed if k == KC - 1 else sq_used, 1)

            def rms(m):
                dve.wait_ge(ss_ready, m + 1)
                v.tensor_scalar(rs, pb[7][:], 1.0 / D, EPS, ALU.mult, ALU.add).then_inc(rvar, 1)
                dve.wait_ge(rstd, m + 1)
                v.reciprocal(rs, rs)
                dve.drain()
                for k in range(KC):
                    v.scalar_tensor_tensor(out=grp(xns[m], k), in0=grp(xT, k), scalar=normw[:, m * KC + k:m * KC + k + 1], in1=rs, op0=ALU.mult, op1=ALU.mult).then_inc(xn_ready, 1)

            def feed_forward(n):
                def half(f, s):
                    dve.wait_ge(ff_silu, n * FC + f + 1)
                    v.tensor_tensor(grp(big, f), pb[3 + s][:], sgl[s], ALU.mult).then_inc(ff_free, 1)

                with dve.Fori(0, FC // 3) as i:
                    for s in range(3):
                        half(i * 3 + s, s)
                half(FC - 1, 0)
                for d in range(KC):
                    dve.wait_ge(dn_ready, n * KC + d + 1)
                    x = grp(xT, d)
                    v.scalar_tensor_tensor(out=x, in0=pb[6 + d % 2][:], scalar=0.5, in1=x, op0=ALU.mult, op1=ALU.add).then_inc(dn_free, 1)
                    if d:
                        add_square(2 * n + 1, d - 1)
                add_square(2 * n + 1, KC - 1)

            dve.wait_ge(xT_ready, 4 * KC + 1)
            for k in range(KC):
                add_square(0, k)
            rms(0)
            dve.wait_ge(tok_done, 2 * DEPTH + 1)
            feed_forward(0)
            rms(1)
            dve.wait_ge(rel_stored, 16)

            def convolve(g):
                c = CONV_GROUPS.index(g)
                x, y = grp(big, g), ctmp[c % 2]
                dve.wait_ge(lin_free, DEPTH * LIN_LAYER + g + 1 + 2)
                if c >= 2:
                    dve.wait_ge(conv_silu, c - 1)
                wc = lambda j: conv_w[:, c * CONV + j:c * CONV + j + 1]
                last = v.tensor_scalar(y, x, wc(2), None, ALU.mult)
                for j in (0, 1, 3, 4):
                    o = j - CONV // 2
                    lo, hi = max(0, -o), S - max(0, o)
                    dve.drain()
                    last = v.scalar_tensor_tensor(out=y[:, lo:hi], in0=x[:, lo + o:hi + o], scalar=wc(j), in1=y[:, lo:hi], op0=ALU.mult, op1=ALU.add)
                last.then_inc(conv_ready, 1)

            def apply_norm(n, c):
                if c == 0:
                    dve.wait_ge(nstd, n + 1)
                    if n:
                        v.tensor_scalar(qk_w[:, 0:1], qk_w[:, 0:1], HEAD_DIM ** -0.5, None, ALU.mult)
                        dve.drain()
                r = grp(nrm, c)
                v.reciprocal(r, r)
                dve.drain()
                x = grp(big, n * 8 + c)
                scale = qk_w[:, c // 4:c // 4 + 1] if n else (P ** -0.5 if c < 4 else 1.0)
                last = v.scalar_tensor_tensor(out=x, in0=x, scalar=scale, in1=r, op0=ALU.mult, op1=ALU.mult)
                if c == 7:
                    last.then_inc(n_done, 1)

            for g in range(N_NORM + 5):
                if g in CONV_GROUPS:
                    convolve(g)
                c = g - 5
                if c >= 0:
                    if c >= 8:
                        apply_norm(0, c - 8)
                        dve.drain()
                    dve.wait_ge(nsum_ready, c + 1)
                    v.tensor_scalar(grp(nrm, c % 8), pb[2 + c % 4][:], 1.0 / HEAD_DIM if c >= 8 else 1.0, EPS, ALU.mult, ALU.add).then_inc(nsum_used, 1)
            for c in range(8):
                apply_norm(1, c)
            dve.drain()
            dve.wait_ge(ab_tr, 1)
            v.tensor_copy(ab[:, :], pb[0][:, 0:NCH * 16])
            dve.drain()
            av = cut(ab[:, :], 16)

            v.tensor_copy(cut(gbeta[0:CH, :], GH), av[0:CH, :, UN:UN + GH])
            for n in range(NCH):
                v.tensor_copy(gbeta[CH:P, n * GH:(n + 1) * GH], av[CH:P, NCH - 1 - n, UN + GH:2 * UN])
            v.tensor_tensor(av[:, :, 0:UN], av[:, :, 0:UN], dtb[:, :].unsqueeze(1).to_broadcast([P, NCH, UN]), ALU.add)
            dve.drain()
            v.tensor_scalar(av[:, :, UN:16], av[:, :, 0:UN], -1.0, None, ALU.mult)
            dve.drain()
            v.tensor_tensor(cut(ga[:, :], UN), av[:, :, 0:UN], av[:, :, UN:16], ALU.max).then_inc(ab_ready, 1)
            dve.wait_ge(sp_ready, 1)
            v.scalar_tensor_tensor(out=cut(ga[:, :], UN), in0=av[:, :, 0:UN], scalar=0.0, in1=cut(ga[:, :], UN), op0=ALU.max, op1=ALU.add)
            v.tensor_scalar(alog[:, :], alog[:, :], -1.0, None, ALU.mult)
            dve.drain()
            v.tensor_tensor(cut(ga[:, :], UN), cut(ga[:, :], UN), alog[:, :].unsqueeze(1).to_broadcast([P, NCH, UN]), ALU.mult).then_inc(g_ready, 1)
            dve.wait_ge(gc_ready, 1)
            for r in range(2):
                v.tensor_copy(cut(half_ones[:, r * P:(r + 1) * P], CH), block_ones[:, r * CH:(r + 1) * CH].unsqueeze(1).to_broadcast([P, 2, CH]))
            v.tensor_tensor(id_pair[:, :], identity[:, 0:CH], identity[:, CH:P], ALU.add)
            v.tensor_copy(gg[0:CH, :], pb[1][0:CH, 0:NCH * GH])
            for n in range(NCH):
                last = v.tensor_copy(gg[CH:P, n * GH:(n + 1) * GH], pb[1][CH:P, (NCH - 1 - n) * GH:(NCH - n) * GH])
            last.then_inc(gc_done, 1)
            A0 = DEPTH * NT * ATT
            dve.wait_ge(hank_loaded, 16)
            with dve.Fori(0, NT) as b:
                def prepare2(h, low):
                    return v.tensor_tensor_reduce(out=lg2[h % 3], in0=pb[LOGIT_BANKS[h % 3]][:], in1=lnw_b, scale=-1.0, scalar=-LOWEST,
                                                  op0=ALU.add, op1=ALU.min, accum_out=low)

                dve.wait_ge(staged, b + 1)
                heads(A0 + b * HEADS, HEADS, prepare2, lambda h: S, lg2)
            dve.wait_ge(att_done, DEPTH * NT + NT)
            v.memset(st[0], 0.0).then_inc(g_state, 1)
            dve.wait_ge(masks_loaded, 16)
            dve.drain()
            incl = msk[:, LEVELS * LW:]

            def ident(heads):
                return id_pair[:, :].unsqueeze(1).to_broadcast([P, heads, CH])

            def over(t, n, w=GH):
                return t.unsqueeze(2).to_broadcast([P, w, n])

            def diagonals(n):
                v.tensor_copy(gs[:, :], gg[:, bass.ds(n * GH, GH)])
                v.tensor_copy(bs[:, :], gbeta[:, bass.ds(n * GH, GH)])
                dve.drain()
                v.tensor_tensor(cut(dg, CH), ident(GH), over(gs[:, :], CH), ALU.mult)
                v.tensor_tensor(cut(db, CH), ident(GH), over(bs[:, :], CH), ALU.mult).then_inc(g_diag, 1)

            def prepare_chunk(n, par, first):
                dve.wait_ge(g_rows, n + 1)
                dve.wait_ge(g_eg, n + 1)
                alone(dve)
                own = cut(pb[5][:, 0:LW], CH)
                v.tensor_copy(gend[0:CH, :].unsqueeze(2), own[0:CH, :, CH - 1:CH])
                v.tensor_copy(gend[CH:P, :].unsqueeze(2), own[CH:P, :, 0:1])
                v.tensor_tensor(cut(dT, CH), own, over(gs[:, :], CH), ALU.subtract)
                dve.drain()
                v.tensor_tensor(dT, dT, incl, ALU.mult)
                v.tensor_tensor(dfac[:, :], gend[:, :], gs[:, :], ALU.subtract).then_inc(g_diff, 1)
                v.tensor_tensor(kbF, eg, pb[1][:], ALU.mult)
                v.tensor_tensor(cut(vB, P), cut(pb[3][:], P), over(bs[:, :], P), ALU.mult)
                v.tensor_tensor(qg[par], qs, eg, ALU.mult)
                dve.drain()
                v.tensor_tensor(kbF, ks, kbF, ALU.mult)
                dve.wait_ge(g_dexp, n + 1)
                alone(dve)
                v.tensor_tensor(dT, dT, incl, ALU.mult)
                v.tensor_tensor(cut(kdec[par], P), cut(pb[2][:], P), over(dfac[:, :], P), ALU.mult).then_inc(g_kv_used, 1)
                dve.drain()
                v.tensor_tensor(lT, pb[0][:, 0:LW], dT, ALU.mult)
                v.tensor_tensor(inT[par], pb[0][:, LW:2 * LW], dT, ALU.mult)
                dve.drain()
                v.tensor_tensor(lT, pb[5][:, LW:2 * LW], lT, ALU.mult)
                dve.drain()
                v.tensor_tensor(lbT, lT, msk[:, 0:LW], ALU.mult)
                if not first:
                    dve.wait_ge(g_vnm, n)
                    alone(dve)
                dve.drain()
                v.tensor_tensor(cut(Mm, CH), ident(GH), cut(lbT, CH), ALU.subtract).then_inc(g_mats, 1)

            def half(t, g, c0=0):
                return t[:, c0 + g * LW // 2:c0 + (g + 1) * LW // 2]

            def first_level(n):
                for g in range(2):
                    dve.wait_ge(g_up, n * LEVELS * 2 + g + 1)
                    alone(dve)
                    v.tensor_tensor(cut(half(Tm, g), CH), ident(GH // 2), cut(half(pb[4 + g], g), CH), ALU.subtract)
                    v.tensor_tensor(half(lbT, g), half(lT, g), half(msk, g, LW), ALU.mult).then_inc(g_tm, 1)

            def chunk(n, par, left):
                with dve.Fori(0, LEVELS - 2) as q:
                    dve.drain()
                    for g in range(2):
                        dve.wait_ge(g_up, (n * LEVELS + q + 1) * 2 + g + 1)
                        alone(dve)
                        v.tensor_tensor(half(Tm, g), half(Tm, g), half(pb[4 + g], g), ALU.subtract)
                        v.tensor_tensor(half(lbT, g), half(lT, g), msk[:, bass.ds((q + 2) * LW + g * (LW // 2), LW // 2)], ALU.mult)
                        v.tensor_tensor(half(Mm, g), half(Mm, g), half(pb[4 + g], g, LW), ALU.subtract).then_inc(g_tm, 1)
                dve.drain()
                for g in range(2):
                    dve.wait_ge(g_up, (n * LEVELS + LEVELS - 1) * 2 + g + 1)
                    alone(dve)
                    v.tensor_tensor(half(Mm, g), half(Mm, g), half(pb[4 + g], g, LW), ALU.subtract).then_inc(g_tm, 1)
                dve.wait_ge(g_r, n + 1)
                alone(dve)
                v.tensor_tensor(resid, vB, pb[6][:], ALU.subtract).then_inc(g_rsub, 1)
                if not left:
                    return
                prepare_chunk(n + 1, 1 - par, False)
                v.tensor_tensor(cut(st[1 - par], P), cut(st[par], P), over(egl[par][:, :], P, UN), ALU.mult)
                if left > 1:
                    diagonals(n + 2)
                first_level(n + 1)
                dve.wait_ge(g_out, n + 1)
                alone(dve)
                dve.drain()
                for r in range(2):
                    x = st[1 - par][:, r * S:(r + 1) * S]
                    last = v.tensor_tensor(x, x, pb[2 + r][:], ALU.add)
                last.then_inc(g_state, 1)

            diagonals(0)
            prepare_chunk(0, 0, True)
            diagonals(1)
            first_level(0)
            with dve.Fori(0, NCH // 2 - 1) as i:
                for par in range(2):
                    chunk(i * 2 + par, par, 2)
            chunk(NCH - 2, 0, 1)
            chunk(NCH - 1, 1, 0)
            dve.wait_ge(g_o, NCH + 1)
            v.tensor_tensor(of, of, ob, ALU.add).then_inc(o_sum, 1)
            for h in range(GH):
                dve.wait_ge(o_ss, h + 1)
                last = v.tensor_scalar(grp(ob, h), pb[2 + h][:], 1.0 / P, EPS, ALU.mult, ALU.add)
            last.then_inc(o_var, 1)
            dve.wait_ge(o_std, 1)
            v.reciprocal(ob, ob)
            dve.drain()
            v.scalar_tensor_tensor(out=ob, in0=ob, scalar=gn_w[:, 0:1], in1=grp(big, H_Z, 4), op0=ALU.mult, op1=ALU.mult)
            dve.drain()
            v.tensor_tensor(of, of, ob, ALU.mult).then_inc(o_done, 1)
            for d in range(KC):
                dve.wait_ge(lin_ready, DEPTH * LIN_LAYER + N_H + d + 1)
                x = grp(xT, d)
                v.tensor_tensor(x, x, pb[OUT_BANKS[d]][:], ALU.add).then_inc(lin_free, 1)
                if d:
                    add_square(2, d - 1)
            add_square(2, KC - 1)
            rms(2)
            feed_forward(1)
            rms(3)


def _bucket(rel):
    import math
    import numpy as np
    nb, far = 16, 1024
    exact = nb // 2
    n = np.abs(rel)
    large = exact + (np.log(np.maximum(n, 1) / exact) / math.log(far / exact) * (nb - exact)).astype(np.int32)
    return (rel > 0).astype(np.int32) * nb + np.where(n < exact, n, np.minimum(large, nb - 1))


def _constants():
    import numpy as np
    f = np.float32
    i = np.arange(P)
    rot = np.zeros((P, P), f)
    half = i % HEAD_DIM < HEAD_DIM // 2
    rot[i[half] + HEAD_DIM // 2, i[half]] = -1.0
    rot[i[~half] - HEAD_DIM // 2, i[~half]] = 1.0
    cst = np.stack([np.eye(P), np.ones((P, P)), i[:, None] // 64 == i // 64, rot, np.eye(P)[::-1], i[:, None] < i], 1)
    t = np.arange(S)
    adm = np.where(t // 64 <= t[:, None] // 64, 0.0, BIG_NEG)
    far = np.abs(t - t[:, None])
    count = (far <= 64).astype(int) + ((far % 4 == 0) & (far // 4 <= 64)) + ((far % 16 == 0) & (far // 16 <= 64))
    lnw = np.where(count > 0, np.log(np.maximum(count, 1)), BIG_NEG)
    by_tile = lambda m: m.reshape(NT, P, S).transpose(1, 0, 2).reshape(P, NT * S).astype(f)
    rec = 1.0 / np.minimum(np.arange(16) + 1, np.array([[2], [4], [8], [16]]))
    c = np.arange(CH)
    both = lambda m: np.concatenate([np.tile(m, GH), np.tile(m.T, GH)], 0)
    upper = c[:, None] < c
    levels = [both(upper & (c[:, None] // (2 << q) == c // (2 << q)) & (c[:, None] >> q != c >> q)) for q in range(LEVELS)]
    incl = c[:, None] <= c
    oh = (_bucket(np.arange(1024) - (S - 1)) == np.arange(32)[:, None])
    freq = (10000.0 ** (-(i % 32).astype(f) / f(32))).astype(f)
    return {
        "cst": cst.reshape(P, 6 * P).astype(f), "adm": by_tile(adm), "lnw": by_tile(lnw),
        "pool_rec": np.broadcast_to(rec.reshape(1, 64), (P, 64)).astype(f),
        "msk": np.concatenate(levels + [both(incl)], 1).astype(f),
        "gtri": np.concatenate([incl, incl.T], 0).astype(f), "rel_oh": oh.astype(f),
        "inv_freq": freq[:, None], "before": np.broadcast_to(np.arange(4) < np.arange(4)[:, None], (P, 4, 4)).reshape(P, 16).astype(f), "blk_iota": np.broadcast_to(np.arange(N_BLK), (P, N_BLK)).astype(f),
    }


def _layout(a):
    import numpy as np
    cat = np.concatenate

    def by_feature(m):
        return m.T.reshape(-1, P, m.shape[0]).transpose(1, 0, 2).reshape(P, -1)

    def unit(w):
        return w.reshape(-1, P, w.shape[1]).transpose(1, 0, 2).reshape(P, -1)

    def units(w):
        return [unit(w[:, g * P:(g + 1) * P]) for g in range(w.shape[1] // P)]

    def pairs(us):
        return [cat(us[j:j + 2], 1) for j in range(0, len(us), 2)]

    def wide(w, n, j):
        return unit(w[j * 512:(j + 1) * 512, n * 512:(n + 1) * 512])

    cuts = np.cumsum([512, 512, 512, 512, 512, 64, 8, 512])

    def in_columns(w):
        pool, q, k, v, iq, ik, iw, mq, gates = np.split(w, cuts, axis=-1)
        return cat([pool, q, mq, k, iq, ik, ik, v] + [iw] * 16, -1), gates

    out = {}
    x = a["x"][0]
    out["xT"], out["xtok"] = by_feature(x), x.reshape(NT, P, D).transpose(1, 0, 2).reshape(P, NT * D)
    out["memT"], out["positions"] = by_feature(a["mem"][0]), a["positions"][0]
    layers, bp, bg = [], [], []
    for l in range(DEPTH):
        main, gates = in_columns(a["w_in"][l])
        main = cat([main[:, g * P:(g + 1) * P] for g in ORDER], 1)
        gate = units(gates)
        stream = pairs(units(a["w_mem_kv"][l]) + units(main))
        mixed = []
        for n in range(3):
            br = [unit(a["w_br"][l, n][:, d * P:(d + 1) * P]) for d in range(KC)]
            for d in range(0, KC, 2):
                mixed += [gate[n * KC + d], gate[n * KC + d + 1], cat(br[d:d + 2], 1)]
        stream += pairs(mixed) + [wide(a["w_out"][l], n, j) for n in range(2) for j in range(2)]
        layers += stream
        b_main, b_gates = in_columns(a["b_in"][l])
        bp.append(b_main.reshape(N_G, P).T)
        bg.append(b_gates.reshape(24, P).T)
    out["w_layer"], out["bias_p"], out["bias_g"] = np.stack(layers), cat(bp, 1), cat(bg, 1)
    out["w_moe"] = np.stack([
        m for l in range(DEPTH) for e in range(N_EXP)
        for m in [wide(a["w1"][l, e], 0, 0), wide(a["w1"][l, e], 0, 1), wide(a["w3"][l, e], 0, 0), wide(a["w3"][l, e], 0, 1),
                  wide(a["w2"][l, e], 0, 0), wide(a["w2"][l, e], 1, 0)]])
    gap = np.zeros((P, 2 * P), np.float32)

    def ffn(g, u, d):
        up = [m for pair in zip(units(g), units(u)) for m in pair]
        down = [m for w in units(d) for m in np.split(cat([w, gap], 1), 3, axis=1)]
        return pairs(up) + pairs(down)

    qkv, z, ab, swa = np.split(a["w_in_2"][0], [1536, 2048, 2064], axis=1)
    tail = ffn(a["ffn1_w_gate_2"][0], a["ffn1_w_up_2"][0], a["ffn1_w_down_2"][0])
    tail += pairs(units(cat([qkv[:, :1024], swa[:, :1024], qkv[:, 1024:], z, swa[:, 1024:]] + [ab] * 16, 1)))
    tail += [unit4 for half in (1, 0) for g in (0, 4) for unit4 in [
        cat([unit(a["w_out_2"][0][half * 512:(half + 1) * 512, d * P:(d + 1) * P]) for d in range(g, g + 4)], 1)]]
    tail += ffn(a["ffn2_w_gate_2"][0], a["ffn2_w_up_2"][0], a["ffn2_w_down_2"][0])
    out["w_tail"] = np.stack(tail)
    out["pool_w"] = a["pool_w"].reshape(DEPTH * 4, P, P)
    out["pool_scale"] = a["pool_scale"].reshape(DEPTH * 4, P).T
    out["w_router"], out["router_bias"] = unit(a["w_router"]), a["router_bias"]
    out["ln_par"] = np.stack([cat([a[f"ln{n}_g"][l], a[f"ln{n}_b"][l]]) for l in range(DEPTH) for n in (1, 2)])
    out["ln_T"] = cat([a[f"ln{n}_{x}"][l].reshape(KC, P).T for l in range(DEPTH) for n in (1, 2) for x in "gb"], 1)
    out["normw"] = cat([a[n][0].reshape(KC, P).T for n in ("ffn1_norm_2", "mix_norm_2", "ffn2_norm_2", "final_norm_2")], 1)
    out["conv_w"] = a["conv_w_2"][0].reshape(12, P, CONV).transpose(1, 0, 2).reshape(P, 12 * CONV)
    out["gn_w"] = a["gdn_norm_w_2"].reshape(P, 1)
    out["qk_w"] = np.stack([cat([a[n][0]] * 2) for n in ("q_norm_w_2", "k_norm_w_2")], 1)
    out["rel_b"] = a["rel_bias_2"]
    out["a_log"], out["dt_bias"] = a["a_log_2"].reshape(UN), a["dt_bias_2"].reshape(UN)
    return out


def kernel(**inputs):
    import numpy as np
    import concourse.bacc as bacc
    from concourse.bass_utils import run_bass_kernel_spmd

    arrays = {**_constants(), **_layout({k: np.asarray(v) for k, v in inputs.items()})}
    arrays = {k: np.ascontiguousarray(v) for k, v in arrays.items()}
    nc = bacc.Bacc("TRN2", target_bir_lowering=False, num_devices=1)
    aps = {k: nc.dram_tensor(f"in_{k}", v.shape, mybir.dt.from_np(v.dtype), kind="ExternalInput").ap() for k, v in arrays.items()}
    out = nc.dram_tensor("out", (P, KC * S), F32, kind="ExternalOutput").ap()
    two_blocks(nc, aps, out)
    r = run_bass_kernel_spmd(nc, [{f"in_{k}": v for k, v in arrays.items()}], core_ids=[0])
    got = r.results[0]["out"]
    return got.reshape(P, KC, S).transpose(2, 1, 0).reshape(1, S, D)
```
